# Optimizing a Trainium2 kernel written in Bass

```python
import math
import jax, jax.numpy as jnp
from jax import lax
import numpy as np

D_MODEL = 1024
BATCH = 1
SEQ = 512
DEPTH = 1
DEC_BATCH = 8
DEC_SEQ = 1
PAST_LEN = 4096
PAGE_SIZE = 128

DH = 64
HA = 8
KVA = 2
GA = HA // KVA
IDX_H = 4
IDX_D = 64
IDX_TOPK = 256
HB = 8
KVB = 2
GB = HB // KVB
CMP_LEN = 32
CMP_STRIDE = 16
CMP_HID = 64
SLC_LEN = 64
SLC_N = 16
WINDOW = 512
MEM_TOK = 256
HM = 4
DHM = 128
N_BUCKETS = 32
MAX_DIST = 128
N_KEYS = 128
N_EXPERTS = N_KEYS * N_KEYS
PEER_HEADS = 8
PEER_DK = 128
PEER_TOPK = 16
MIX_W = 512
N_BRANCH = 3
Q_BLOCK = 128
SLC_Q_BLOCK = 32
PEER_BLOCK = 128
EPS = 1e-6
IN_SPLITS = (('q_a', HA * DH), ('kv_a', KVA * 2 * DH), ('q_idx', IDX_H * IDX_D), ('w_idx', IDX_H), ('k_idx', IDX_D), ('q_b', HB * DH), ('kv_cmp', KVB * 2 * DH), ('kv_slc', KVB * 2 * DH), ('kv_win', KVB * 2 * DH), ('g_nsa', HB * 3), ('q_m', HM * DHM))
IN_W = sum(n for _, n in IN_SPLITS)

kernel_name = 'hybrid_dsa_nsa_mem_peer_step'

def rmsnorm(x, g):
    x32 = x.astype(jnp.float32)
    y = x32 * lax.rsqrt(jnp.mean(x32 * x32, axis=-1, keepdims=True) + EPS)
    return (y * g.astype(jnp.float32)).astype(x.dtype)

def norm_k(kv, g):
    return jnp.stack([rmsnorm(kv[..., 0, :], g), kv[..., 1, :]], axis=-2)

def t5_bucket(dist):
    n = jnp.maximum(dist, 0)
    exact = N_BUCKETS // 2
    nf = jnp.maximum(n, 1).astype(jnp.float32)
    big = exact + (jnp.log(nf / exact) / math.log(MAX_DIST / exact) * (N_BUCKETS - exact)).astype(jnp.int32)
    return jnp.where(n < exact, n, jnp.minimum(big, N_BUCKETS - 1))

def bias_shared(table, qpos, kpos, n_kv):
    b = table[t5_bucket(qpos[:, None] - kpos[None, :])].astype(jnp.float32)
    q, s, h = b.shape
    return b.reshape(q, s, n_kv, h // n_kv).transpose(0, 2, 3, 1)

def bias_per_query(table, dist, n_kv):
    b = table[t5_bucket(dist)].astype(jnp.float32)
    bb, q, s, h = b.shape
    return b.reshape(bb, q, s, n_kv, h // n_kv).transpose(0, 1, 3, 4, 2)

def bias_per_group(table, dist):
    n_kv = dist.shape[2]
    tbl = table.reshape(N_BUCKETS, n_kv, -1)
    b = tbl[t5_bucket(dist), jnp.arange(n_kv)[:, None]].astype(jnp.float32)
    return jnp.swapaxes(b, -1, -2)

def masked_softmax(logits, mask):
    l = jnp.where(mask, logits.astype(jnp.float32), -jnp.inf)
    m = jnp.max(l, axis=-1, keepdims=True)
    m = jnp.where(jnp.isfinite(m), m, 0.0)
    e = jnp.where(mask, jnp.exp(l - m), 0.0)
    return e / jnp.maximum(jnp.sum(e, axis=-1, keepdims=True), 1e-30)

def gather_rows(kv, idx, head=None):
    b = jnp.arange(idx.shape[0]).reshape((-1,) + (1,) * (idx.ndim - 1))
    return kv[b, idx] if head is None else kv[b, idx, head]

def gather_paged(pool, page_table, new_kv, idx, head=None):
    ps = pool.shape[1]
    past = page_table.shape[1] * ps
    b = jnp.arange(idx.shape[0]).reshape((-1,) + (1,) * (idx.ndim - 1))
    ip = jnp.minimum(idx, past - 1)
    phys = page_table[b, ip // ps]
    off = ip % ps
    rows_p = pool[phys, off] if head is None else pool[phys, off, head]
    rows_n = gather_rows(new_kv, jnp.clip(idx - past, 0, new_kv.shape[1] - 1), head)
    in_past = (idx < past).reshape(idx.shape + (1,) * (rows_p.ndim - idx.ndim))
    return jnp.where(in_past, rows_p, rows_n)

def map_query_blocks(fn, n_q, qb):
    out = lax.map(fn, jnp.arange(n_q // qb) * qb)
    out = jnp.moveaxis(out, 0, 1)
    return out.reshape((out.shape[0], n_q) + out.shape[3:])

def dsa_attend(q_a, q_idx, w_idx, qpos, k_idx_all, gather_kv, table_a, k_top):
    L = k_idx_all.shape[1]
    s = jnp.einsum('bqhd,bsd->bqsh', q_idx, k_idx_all)
    score = jnp.einsum('bqsh,bqh->bqs', jax.nn.relu(s), w_idx).astype(jnp.float32) * (IDX_D ** -0.5 * IDX_H ** -0.5)
    kpos = jnp.arange(L)
    score = jnp.where(kpos[None, None, :] <= qpos[None, :, None], score, -jnp.inf)
    top_v, top_i = lax.top_k(score, k_top)
    valid = top_v > -jnp.inf
    kv = gather_kv(top_i)
    k, v = kv[..., 0, :], kv[..., 1, :]
    logits = jnp.einsum('bqkgd,bqskd->bqkgs', q_a, k).astype(jnp.float32) * DH ** -0.5
    logits = logits + bias_per_query(table_a, qpos[None, :, None] - top_i, KVA)
    p = masked_softmax(logits, valid[:, :, None, None, :])
    o = jnp.einsum('bqkgs,bqskd->bqkgd', p.astype(v.dtype), v)
    return o.reshape(o.shape[0], o.shape[1], HA * DH)

def compress(rows, W):
    bsz, L = rows.shape[:2]
    n_ch = L // CMP_STRIDE
    r = CMP_LEN // CMP_STRIDE
    n_cmp = n_ch - r + 1
    ch = rows[:, :n_ch * CMP_STRIDE].reshape(bsz, n_ch, CMP_STRIDE, KVB, 2, DH)
    w1 = W['w_cmp1'].reshape(2, r, CMP_STRIDE, DH, CMP_HID)
    h = sum(jnp.einsum('bnrgcd,crdh->bngch', ch, w1[:, j])[:, j:j + n_cmp] for j in range(r))
    pe_h = jnp.einsum('crd,crdh->ch', W['cmp_pe'], W['w_cmp1'])
    h = jax.nn.gelu(h + pe_h)
    return jnp.einsum('bngch,chd->bngcd', h, W['w_cmp2'])

def cmp_to_slc(n_cmp, n_slc):
    r = CMP_LEN // CMP_STRIDE
    m = SLC_LEN // CMP_STRIDE
    o = jnp.arange(n_cmp)[:, None] + (r - 1) - m * jnp.arange(n_slc)[None, :] - (r - 1)
    return sum(((o + n >= 0) & (o + n < m)).astype(jnp.float32) for n in range(r))

def nsa_compressed(q, qpos, kv_c, table_b, n_slc):
    n_cmp = kv_c.shape[1]
    end = jnp.arange(n_cmp) * CMP_STRIDE + CMP_LEN - 1
    logits = jnp.einsum('bqkgd,bnkd->bqkgn', q, kv_c[..., 0, :]).astype(jnp.float32) * DH ** -0.5
    logits = logits + bias_shared(table_b, qpos, end, KVB)[None]
    p = masked_softmax(logits, (end[None, :] <= qpos[:, None])[None, :, None, None, :])
    o = jnp.einsum('bqkgn,bnkd->bqkgd', p.astype(kv_c.dtype), kv_c[..., 1, :])
    imp = jnp.einsum('bqkgn,nj->bqkj', p, cmp_to_slc(n_cmp, n_slc))
    j = jnp.arange(n_slc)[None, :]
    cur = (qpos // SLC_LEN)[:, None]
    forced = ((j == 0) | (j == cur) | (j == cur - 1))[None, :, None, :]
    future = (j > cur)[None, :, None, :]
    imp = jnp.where(future, -jnp.inf, jnp.where(forced, jnp.inf, imp))
    top_v, top_i = lax.top_k(imp, min(SLC_N, n_slc))
    return o, top_i, top_v > -jnp.inf

def nsa_selected(q, qpos, sel, sel_ok, gather_kv, table_b):
    bsz, nq = sel.shape[:2]
    pos = (sel[..., None] * SLC_LEN + jnp.arange(SLC_LEN)).reshape(bsz, nq, KVB, -1)
    ok = jnp.repeat(sel_ok, SLC_LEN, axis=-1) & (pos <= qpos[None, :, None, None])
    kv = gather_kv(pos)
    logits = jnp.einsum('bqkgd,bqksd->bqkgs', q, kv[..., 0, :]).astype(jnp.float32) * DH ** -0.5
    logits = logits + bias_per_group(table_b, qpos[None, :, None, None] - pos)
    p = masked_softmax(logits, ok[:, :, :, None, :])
    return jnp.einsum('bqkgs,bqksd->bqkgd', p.astype(kv.dtype), kv[..., 1, :])

def nsa_window(q, qpos, kv_w, kpos, table_b):
    logits = jnp.einsum('bqkgd,bskd->bqkgs', q, kv_w[..., 0, :]).astype(jnp.float32) * DH ** -0.5
    logits = logits + bias_shared(table_b, qpos, kpos, KVB)[None]
    d = qpos[:, None] - kpos[None, :]
    mask = ((d >= 0) & (d <= WINDOW) & (kpos[None, :] >= 0))[None, :, None, None, :]
    p = masked_softmax(logits, mask)
    return jnp.einsum('bqkgs,bskd->bqkgd', p.astype(kv_w.dtype), kv_w[..., 1, :])

def nsa_merge(g, o_cmp, o_slc, o_win):
    g = g.astype(o_cmp.dtype)
    o = g[..., 0:1] * o_cmp + g[..., 1:2] * o_slc + g[..., 2:3] * o_win
    return o.reshape(o.shape[0], o.shape[1], HB * DH)

def memory_kv(mem, W):
    bsz, m, _ = mem.shape
    kv = (rmsnorm(mem, W['ln_mem']) @ W['w_mem_kv']).reshape(bsz, m, HM, 2, DHM)
    return norm_k(kv, W['g_km'])

def memory_attend(q_m, mem_kv):
    logits = jnp.einsum('bqhd,bmhd->bqhm', q_m, mem_kv[..., 0, :]).astype(jnp.float32) * DHM ** -0.5
    p = jax.nn.softmax(logits, axis=-1)
    o = jnp.einsum('bqhm,bmhd->bqhd', p.astype(mem_kv.dtype), mem_kv[..., 1, :])
    return o.reshape(o.shape[0], o.shape[1], HM * DHM)

def peer(x2d, W):
    n = x2d.shape[0]
    n_pad = -(-n // PEER_BLOCK) * PEER_BLOCK
    xp = jnp.pad(x2d, ((0, n_pad - n), (0, 0)))

    def blk(xb):
        nb = xb.shape[0]
        q = (xb @ W['w_pq']).reshape(nb, PEER_HEADS, 2, PEER_DK // 2)
        s = jnp.einsum('nhpd,pkd->nhpk', q, W['sub_keys']).astype(jnp.float32)
        v_top, i_top = lax.top_k(s, PEER_TOPK)
        cand = (v_top[:, :, 0, :, None] + v_top[:, :, 1, None, :]).reshape(nb, PEER_HEADS, -1)
        cidx = (i_top[:, :, 0, :, None] * N_KEYS + i_top[:, :, 1, None, :]).reshape(nb, PEER_HEADS, -1)
        f_v, f_p = lax.top_k(cand, PEER_TOPK)
        e = jnp.take_along_axis(cidx, f_p, axis=-1)
        g = jax.nn.softmax(f_v, axis=-1)
        a = jax.nn.gelu(jnp.einsum('nhkd,nd->nhk', W['u_tab'][e], xb).astype(jnp.float32))
        return jnp.einsum('nhk,nhkd->nd', (g * a).astype(xb.dtype), W['v_tab'][e])

    out = lax.map(blk, xp.reshape(-1, PEER_BLOCK, x2d.shape[1]))
    return out.reshape(n_pad, x2d.shape[1])[:n]

def project(x, W):
    bsz, t, _ = x.shape
    xn = rmsnorm(x, W['ln_mix'])
    p = xn @ W['w_in']
    parts = {}
    off = 0
    for name, n in IN_SPLITS:
        parts[name] = p[..., off:off + n]
        off += n
    q_a = rmsnorm(parts['q_a'].reshape(bsz, t, KVA, GA, DH), W['g_qa'])
    kv_a = norm_k(parts['kv_a'].reshape(bsz, t, KVA, 2, DH), W['g_ka'])
    q_idx = parts['q_idx'].reshape(bsz, t, IDX_H, IDX_D)
    w_idx = parts['w_idx']
    k_idx = parts['k_idx']
    q_b = rmsnorm(parts['q_b'].reshape(bsz, t, KVB, GB, DH), W['g_qb'])
    kv_cmp = parts['kv_cmp'].reshape(bsz, t, KVB, 2, DH)
    kv_slc = norm_k(parts['kv_slc'].reshape(bsz, t, KVB, 2, DH), W['g_kslc'])
    kv_win = norm_k(parts['kv_win'].reshape(bsz, t, KVB, 2, DH), W['g_kwin'])
    g_nsa = jax.nn.sigmoid(parts['g_nsa'].astype(jnp.float32)).reshape(bsz, t, KVB, GB, 3)
    q_m = rmsnorm(parts['q_m'].reshape(bsz, t, HM, DHM), W['g_qm'])
    return xn, (q_a, kv_a, q_idx, w_idx, k_idx, q_b, kv_cmp, kv_slc, kv_win, g_nsa, q_m)

def finish(x, xn, o_a, o_b, o_m, W):
    bsz, t, d = x.shape
    u = jnp.einsum('btcw,cwd->btcd', jnp.stack([o_a, o_b, o_m], axis=2), W['w_branch'])
    gate = jax.nn.sigmoid((xn @ W['w_gate']).astype(jnp.float32)).reshape(bsz, t, N_BRANCH, d)
    h = x + jnp.sum(gate.astype(u.dtype) * u, axis=2) @ W['w_out']
    f = peer(rmsnorm(h, W['ln_ffn']).reshape(bsz * t, d), W).reshape(bsz, t, d)
    return h + f

def prompt_layer(x, mem, nbuf, W):
    bsz, t, _ = x.shape
    qpos = jnp.arange(t)
    xn, (q_a, kv_a, q_idx, w_idx, k_idx, q_b, kv_cmp, kv_slc, kv_win, g_nsa, q_m) = project(x, W)
    table_a = W['rel_table'][:, :HA]
    table_b = W['rel_table'][:, HA:]
    k_top = min(IDX_TOPK, t // 4)

    def a_block(q0):
        sl = lambda a: lax.dynamic_slice_in_dim(a, q0, Q_BLOCK, axis=1)
        return dsa_attend(sl(q_a), sl(q_idx), sl(w_idx), q0 + jnp.arange(Q_BLOCK), k_idx,
                          lambda idx: gather_rows(kv_a, idx), table_a, k_top)
    o_a = map_query_blocks(a_block, t, Q_BLOCK)

    kv_c = norm_k(compress(kv_cmp, W), W['g_kcmp'])
    o_cmp, sel, sel_ok = nsa_compressed(q_b, qpos, kv_c, table_b, -(-t // SLC_LEN))
    head_b = jnp.arange(KVB)[None, None, :, None]

    def s_block(q0):
        sl = lambda a: lax.dynamic_slice_in_dim(a, q0, SLC_Q_BLOCK, axis=1)
        return nsa_selected(sl(q_b), q0 + jnp.arange(SLC_Q_BLOCK), sl(sel), sl(sel_ok),
                            lambda pos: gather_rows(kv_slc, pos, head_b), table_b)
    o_slc = map_query_blocks(s_block, t, SLC_Q_BLOCK)

    kv_win_pad = jnp.pad(kv_win, ((0, 0), (WINDOW, 0), (0, 0), (0, 0), (0, 0)))

    def w_block(q0):
        q_blk = lax.dynamic_slice_in_dim(q_b, q0, Q_BLOCK, axis=1)
        kv_blk = lax.dynamic_slice_in_dim(kv_win_pad, q0, WINDOW + Q_BLOCK, axis=1)
        return nsa_window(q_blk, q0 + jnp.arange(Q_BLOCK), kv_blk, q0 - WINDOW + jnp.arange(WINDOW + Q_BLOCK), table_b)
    o_win = map_query_blocks(w_block, t, Q_BLOCK)
    o_b = nsa_merge(g_nsa, o_cmp, o_slc, o_win)

    mem_kv = memory_kv(mem, W)
    o_m = memory_attend(q_m, mem_kv)
    y = finish(x, xn, o_a, o_b, o_m, W)
    if t >= nbuf:
        win_state = kv_win[:, t - nbuf:]
    else:
        win_state = jnp.pad(kv_win, ((0, 0), (nbuf - t, 0), (0, 0), (0, 0), (0, 0)))
    return y, (kv_a, k_idx, kv_cmp, kv_slc, win_state, mem_kv)

def sample_layer(x, caches, page_table, W):
    cache_a_kv, cache_a_kidx, cache_cmp_kv, cache_slc_kv, cache_win_kv, cache_mem_kv = caches
    db, s, _ = x.shape
    past = page_table.shape[1] * cache_a_kv.shape[1]
    L = past + s
    qpos = past + jnp.arange(s)
    xn, (q_a, kv_a, q_idx, w_idx, k_idx, q_b, kv_cmp, kv_slc, kv_win, g_nsa, q_m) = project(x, W)
    table_a = W['rel_table'][:, :HA]
    table_b = W['rel_table'][:, HA:]

    k_idx_all = jnp.concatenate([cache_a_kidx[page_table].reshape(db, past, IDX_D), k_idx], axis=1)
    o_a = dsa_attend(q_a, q_idx, w_idx, qpos, k_idx_all,
                     lambda idx: gather_paged(cache_a_kv, page_table, kv_a, idx), table_a, min(IDX_TOPK, L // 4))

    cmp_all = jnp.concatenate([cache_cmp_kv[page_table].reshape(db, past, KVB, 2, DH), kv_cmp], axis=1)
    kv_c = norm_k(compress(cmp_all, W), W['g_kcmp'])
    o_cmp, sel, sel_ok = nsa_compressed(q_b, qpos, kv_c, table_b, -(-L // SLC_LEN))
    head_b = jnp.arange(KVB)[None, None, :, None]
    o_slc = nsa_selected(q_b, qpos, sel, sel_ok,
                         lambda pos: gather_paged(cache_slc_kv, page_table, kv_slc, pos, head_b), table_b)
    nbuf = cache_win_kv.shape[1]
    win_all = jnp.concatenate([cache_win_kv, kv_win], axis=1)
    o_win = nsa_window(q_b, qpos, win_all, past - nbuf + jnp.arange(nbuf + s), table_b)
    o_b = nsa_merge(g_nsa, o_cmp, o_slc, o_win)

    o_m = memory_attend(q_m, cache_mem_kv)
    y = finish(x, xn, o_a, o_b, o_m, W)
    return y, (kv_a, k_idx, kv_cmp, kv_slc, win_all[:, s:])

def setup_inputs(seed: int = 0) -> dict:
    key = jax.random.key(seed)
    ks = iter(jax.random.split(key, 48))
    f32 = jnp.float32
    n_pages = PAST_LEN // PAGE_SIZE
    n_used = DEC_BATCH * n_pages
    n_pool = n_used + max(1, n_used // 4)
    nbuf = min(WINDOW, PAST_LEN)

    def nrm(shape, scale):
        return jax.random.normal(next(ks), shape, f32) * scale

    def gain(shape):
        return 1.0 + 0.05 * jax.random.normal(next(ks), shape, f32)

    page_table = jax.random.permutation(next(ks), n_pool)[:n_used].reshape(DEC_BATCH, n_pages).astype(jnp.int32)
    return {
        'x_prompt': nrm((BATCH, SEQ, D_MODEL), 1.0),
        'x_sample': nrm((DEC_BATCH, DEC_SEQ, D_MODEL), 1.0),
        'mem_prompt': nrm((BATCH, MEM_TOK, D_MODEL), 1.0),
        'cache_a_kv': nrm((n_pool, PAGE_SIZE, KVA, 2, DH), 1.0),
        'cache_a_kidx': nrm((n_pool, PAGE_SIZE, IDX_D), 1.0),
        'cache_cmp_kv': nrm((n_pool, PAGE_SIZE, KVB, 2, DH), 1.0),
        'cache_slc_kv': nrm((n_pool, PAGE_SIZE, KVB, 2, DH), 1.0),
        'cache_win_kv': nrm((DEC_BATCH, nbuf, KVB, 2, DH), 1.0),
        'cache_mem_kv': nrm((DEC_BATCH, MEM_TOK, HM, 2, DHM), 1.0),
        'page_table': page_table,
        'ln_mix': gain((D_MODEL,)),
        'w_in': nrm((D_MODEL, IN_W), D_MODEL ** -0.5),
        'g_qa': gain((DH,)),
        'g_ka': gain((DH,)),
        'g_qb': gain((DH,)),
        'g_kcmp': gain((DH,)),
        'g_kslc': gain((DH,)),
        'g_kwin': gain((DH,)),
        'g_qm': gain((DHM,)),
        'g_km': gain((DHM,)),
        'rel_table': nrm((N_BUCKETS, HA + HB), 0.5),
        'w_cmp1': nrm((2, CMP_LEN, DH, CMP_HID), (CMP_LEN * DH) ** -0.5),
        'w_cmp2': nrm((2, CMP_HID, DH), CMP_HID ** -0.5),
        'cmp_pe': nrm((2, CMP_LEN, DH), 0.1),
        'ln_mem': gain((D_MODEL,)),
        'w_mem_kv': nrm((D_MODEL, HM * 2 * DHM), D_MODEL ** -0.5),
        'w_gate': nrm((D_MODEL, N_BRANCH * D_MODEL), D_MODEL ** -0.5),
        'w_branch': nrm((N_BRANCH, MIX_W, D_MODEL), MIX_W ** -0.5),
        'w_out': nrm((D_MODEL, D_MODEL), D_MODEL ** -0.5),
        'ln_ffn': gain((D_MODEL,)),
        'w_pq': nrm((D_MODEL, PEER_HEADS * PEER_DK), D_MODEL ** -0.5),
        'sub_keys': nrm((2, N_KEYS, PEER_DK // 2), (PEER_DK // 2) ** -0.5),
        'u_tab': nrm((N_EXPERTS, D_MODEL), D_MODEL ** -0.5),
        'v_tab': nrm((N_EXPERTS, D_MODEL), PEER_HEADS ** -0.5),
    }

def reference(x_prompt, x_sample, mem_prompt, cache_a_kv, cache_a_kidx, cache_cmp_kv, cache_slc_kv, cache_win_kv, cache_mem_kv, page_table, ln_mix, w_in, g_qa, g_ka, g_qb, g_kcmp, g_kslc, g_kwin, g_qm, g_km, rel_table, w_cmp1, w_cmp2, cmp_pe, ln_mem, w_mem_kv, w_gate, w_branch, w_out, ln_ffn, w_pq, sub_keys, u_tab, v_tab):
    W = {'ln_mix': ln_mix, 'w_in': w_in, 'g_qa': g_qa, 'g_ka': g_ka, 'g_qb': g_qb, 'g_kcmp': g_kcmp,
         'g_kslc': g_kslc, 'g_kwin': g_kwin, 'g_qm': g_qm, 'g_km': g_km, 'rel_table': rel_table,
         'w_cmp1': w_cmp1, 'w_cmp2': w_cmp2, 'cmp_pe': cmp_pe, 'ln_mem': ln_mem, 'w_mem_kv': w_mem_kv,
         'w_gate': w_gate, 'w_branch': w_branch, 'w_out': w_out, 'ln_ffn': ln_ffn, 'w_pq': w_pq,
         'sub_keys': sub_keys, 'u_tab': u_tab, 'v_tab': v_tab}
    caches = (cache_a_kv, cache_a_kidx, cache_cmp_kv, cache_slc_kv, cache_win_kv, cache_mem_kv)
    nbuf = cache_win_kv.shape[1]
    y_p, y_s = x_prompt, x_sample
    for _ in range(DEPTH):
        y_p, st_p = prompt_layer(y_p, mem_prompt, nbuf, W)
        y_s, st_s = sample_layer(y_s, caches, page_table, W)
    a_kv_p, a_kidx_p, cmp_kv_p, slc_kv_p, win_kv_p, mem_kv_p = st_p
    a_kv_s, a_kidx_s, cmp_kv_s, slc_kv_s, win_kv_s = st_s
    return (y_p, y_s, a_kv_p, a_kidx_p, cmp_kv_p, slc_kv_p, win_kv_p, mem_kv_p, a_kv_s, a_kidx_s, cmp_kv_s, slc_kv_s, win_kv_s)


_drawn_inputs = setup_inputs


def setup_inputs(seed=0):
    import zlib

    import numpy as np

    out = dict(_drawn_inputs(seed))
    spreads = {}
    factors = {'g_qa': 4.609, 'g_qb': 3.634, 'g_kcmp': 3.821, 'g_qm': 5.605}
    for name, (base, spread) in spreads.items():
        noise = np.random.default_rng([zlib.crc32(name.encode()), seed]).standard_normal(out[name].shape)
        drawn = base * np.exp(spread * noise) if base else spread * noise
        out[name] = __import__('jax').numpy.asarray(drawn.astype(out[name].dtype))
    for name, factor in factors.items():
        out[name] = (out[name] * factor).astype(out[name].dtype)
    return out
```

```python
import math
from contextlib import ExitStack

import numpy as np

import concourse.bass as bass
from concourse import mybir

F32 = mybir.dt.float32
U32 = mybir.dt.uint32
I32 = mybir.dt.int32
ALU = mybir.AluOpType
ACT = mybir.ActivationFunctionType
AX = mybir.AxisListType.X

P = 128
D = 1024
KD = D // P
SEQ, DB, PAST, PAGE = 512, 8, 4096, 128
NPAGE = PAST // PAGE
TP = SEQ // P
NT = TP + 1
ROWS = [P] * TP + [DB]
NCOL = SEQ + DB
DH, HQ, KV, GRP = 64, 8, 2, 4
IH, TOPA_P, TOPA_S = 4, 128, 256
STRIDE, HID = 16, 64
NCH_S, NCH_P = PAST // STRIDE, SEQ // STRIDE
NCMP_S, NCMP_P = NCH_S - 1, NCH_P - 1
BLK, NBLK, NSEL = 64, PAST // 64, 16
WIN, MEM, HM, DHM = 512, 256, 4, 128
NB = 32
HP, NKEY, PTOP = 8, 128, 16
EPS = 1e-6
NEG = -1e30
TAKEN = -2e30

Q_A, KV_A, Q_I, W_I, K_I = 0, 512, 768, 1024, 1028
Q_B, KV_C, KV_S, KV_W, G_N, Q_M, IN_W = 1092, 1604, 1860, 2116, 2372, 2396, 2908
S_QA, S_QB, S_QM, S_KA, S_KS, S_KW, S_KI, S_QI, N_SLOT = 0, 4, 8, 12, 14, 16, 18, 19, 21


def bucket_bounds():
    n = np.arange(PAST + 1)
    nf = np.maximum(n, 1).astype(np.float32)
    half = NB // 2
    big = half + (np.log(nf / np.float32(half)) / np.float32(math.log(128 / half)) * np.float32(NB - half)).astype(np.int32)
    b = np.where(n < half, n, np.minimum(big, NB - 1))
    lo = np.array([n[b == i].min() for i in range(NB)], np.float32)
    hi = np.array([n[b == i].max() + 1 for i in range(NB)], np.float32)
    return np.ascontiguousarray(np.stack([lo, hi], 1))


class Chain:

    def __init__(self, eng, sem):
        self.eng, self.sem, self.n = eng, sem, 0

    def put(self, ins):
        self.n += 1
        ins.then_inc(self.sem, 1)
        return self.n

    def need(self, count):
        self.eng.wait_ge(self.sem, count)

    def link(self, ins):
        self.need(self.put(ins))


class Kernel:
    def __init__(self, nc, ins, outs, scratch):
        self.nc, self.i, self.o, self.s = nc, ins, outs, scratch
        self.ctx = ExitStack()
        self.live = []

    def sem(self, name):
        self.live.append(self.nc.alloc_semaphore(name=name))
        return self.live[-1]

    def stores(self, name):
        return self.store_sems[name]

    def recycle(self):
        self.nc.clear_and_free_semaphores(self.live)
        self.live = []
        self.nc.all_engine_barrier()

    def sb(self, name, shape, dt=F32, ctx=None):
        return (ctx or self.ctx).enter_context(self.nc.sbuf_tensor(name, shape, dt))

    def ps(self, name, shape, ctx, dt=F32):
        return ctx.enter_context(self.nc.psum_tensor(name, shape, dt))

    def constants(self):
        nc, i = self.nc, self.i
        self.ident = self.sb("ident", [P, P])
        self.eps = self.sb("eps", [P, 1])
        self.g64 = self.sb("g64", [P, 6, DH])
        self.g128 = self.sb("g128", [P, 2, DHM])
        ident, g64, g128 = self.ident, self.g64, self.g128
        zero_done, ident_done, gains_in, scaled = (self.sem(f"const_{n}") for n in ("zero", "ident", "gains", "scaled"))
        with nc.Block() as block:
            @block.gpsimd
            def _(pool):
                pool.memset(ident[:], 0.0).then_inc(zero_done, 1)
                pool.memset(self.eps[:], EPS)
                pool.wait_ge(zero_done, 1)
                pool.affine_select(out=ident[:], in_=ident[:], compare_op=ALU.not_equal, fill=1.0, base=0,
                                   pattern=[[-1, P]], channel_multiplier=1).then_inc(ident_done, 1)

            @block.sync
            def _(sp):
                for n, name in enumerate(("g_qa", "g_ka", "g_qb", "g_kcmp", "g_kslc", "g_kwin")):
                    sp.dma_start(g64[:, n, :], i[name].partition_broadcast(P)).then_inc(gains_in, 16)
                for n, name in enumerate(("g_qm", "g_km")):
                    sp.dma_start(g128[:, n, :], i[name].partition_broadcast(P)).then_inc(gains_in, 16)

            @block.vector
            def _(dve):
                dve.wait_ge(gains_in, 8 * 16)
                dve.tensor_scalar_mul(g64[:, 0, :], g64[:, 0, :], DH ** -0.5).then_inc(scaled, 1)
                dve.tensor_scalar_mul(g64[:, 2, :], g64[:, 2, :], DH ** -0.5).then_inc(scaled, 1)

    def norm_rows(self, tag, load, gain, rows, out_t, keep=None):
        nc, ident = self.nc, self.ident
        nt = len(rows)
        ctx = ExitStack()
        with ctx:
            from_dram = isinstance(load, list)
            x = self.sb(f"{tag}_x", [P, nt, D], F32, ctx) if from_dram else load
            xn = keep if keep is not None else self.sb(f"{tag}_xn", [P, nt, D], F32, ctx)
            junk = self.sb(f"{tag}_sq", [P, D], F32, ctx)
            gb = self.sb(f"{tag}_gain", [P, D], F32, ctx)
            ss = self.sb(f"{tag}_ss", [P, nt], F32, ctx)
            tr = self.ps(f"{tag}_tr", [P, 2, 4, P], ctx)
            x_in, g_in, sq_done, chain, xn_done, tr_done, out_done, junk_done = (
                self.sem(f"{tag}_{n}") for n in ("x_in", "g_in", "sq_done", "chain", "xn_done", "tr_done", "out_done", "junk_done"))
            with nc.Block() as block:
                @block.sync
                def _(sp):
                    if from_dram:
                        for t, r in enumerate(rows):
                            sp.dma_start(x[:r, t, :], load[t]).then_inc(x_in, 16)
                            sp.wait_ge(x_in, 16 * (t + 1))
                    sp.dma_start(gb[:], gain.partition_broadcast(P)).then_inc(g_in, 16)

                @block.scalar
                def _(act):
                    def evac(u):
                        t, r = u // 2, rows[u // 2]
                        act.wait_ge(tr_done, u + 1)
                        act.copy(out_t[:, 4 * (u % 2):4 * (u % 2) + 4, P * t:P * t + r],
                                 tr[:, u % 2, :, :r]).then_inc(out_done, 1)

                    for t, r in enumerate(rows):
                        if from_dram:
                            act.wait_ge(x_in, 16 * (t + 1))
                        if t:
                            act.wait_ge(sq_done, t)
                        act.activation(junk[:r, :], x[:r, t, :], ACT.Square, accum_out=ss[:r, t:t + 1]).then_inc(junk_done, 1)
                        act.wait_ge(junk_done, t + 1)
                        act.activation(ss[:r, t:t + 1], ss[:r, t:t + 1], ACT.Sqrt, bias=self.eps[:r], scale=1.0 / D).then_inc(sq_done, 1)
                        if t:
                            evac(2 * t - 2)
                            evac(2 * t - 1)
                    evac(2 * nt - 2)
                    evac(2 * nt - 1)

                @block.vector
                def _(dve):
                    c = Chain(dve, chain)
                    dve.wait_ge(g_in, 16)
                    for t, r in enumerate(rows):
                        dve.wait_ge(sq_done, t + 1)
                        c.link(dve.reciprocal(ss[:r, t:t + 1], ss[:r, t:t + 1]))
                        dve.scalar_tensor_tensor(out=xn[:r, t, :], in0=x[:r, t, :], scalar=ss[:r, t:t + 1],
                                                 in1=gb[:r, :], op0=ALU.mult, op1=ALU.mult).then_inc(xn_done, 1)

                @block.tensor
                def _(pe):
                    for t, r in enumerate(rows):
                        pe.wait_ge(xn_done, t + 1)
                        for half in range(2):
                            u = 2 * t + half
                            if u >= 2:
                                pe.wait_ge(out_done, u - 1)
                            for k in range(4):
                                c0 = (4 * half + k) * P
                                last = pe.transpose(tr[:, half, k, :r], xn[:r, t, c0:c0 + P], ident[:r, :r])
                            last.then_inc(tr_done, 1)

    def linear(self, tag, xt, rows, weights, width, out, add=None):
        nc = self.nc
        nt = len(rows)
        chunks = [(c, min(512, width - c)) for c in range(0, width, 512)]
        ctx = ExitStack()
        with ctx:
            w = self.sb(f"{tag}_w", [P, 2, KD, 512], F32, ctx)
            acc = self.ps(f"{tag}_acc", [P, 4, 512], ctx)
            w_in = [self.sem(f"{tag}_w_in{b}") for b in range(2)]
            mm_done, even_out, odd_out = (self.sem(f"{tag}_{n}") for n in ("mm", "even_out", "odd_out"))
            units = [(j, t) for j in range(len(chunks)) for t in range(nt)]
            with nc.Block() as block:
                @block.sync
                def _(sp):
                    for j, (c0, n) in enumerate(chunks):
                        if j >= 2:
                            sp.wait_ge(mm_done, (j - 1) * nt)
                        sp.dma_start(w[:, j % 2, :, :n], weights[:, c0:c0 + n].rearrange("(k p) n -> p k n", p=P)).then_inc(w_in[j % 2], 16)

                @block.tensor
                def _(pe):
                    for u, (j, t) in enumerate(units):
                        c0, n = chunks[j]
                        r = rows[t]
                        if t == 0:
                            pe.wait_ge(w_in[j % 2], 16 * (j // 2 + 1))
                        if u >= 4:
                            pe.wait_ge((even_out, odd_out)[u % 2], (u - 4) // 2 + 1)
                        for k in range(KD):
                            last = pe.matmul(acc[:r, u % 4, :n], xt[:, k, P * t:P * t + r], w[:, j % 2, k, :n],
                                             start=(k == 0), stop=(k == KD - 1))
                        last.then_inc(mm_done, 1)

                def evacuate(eng, parity, copy, done):
                    for u, (j, t) in enumerate(units):
                        if u % 2 == parity:
                            c0, n = chunks[j]
                            eng.wait_ge(mm_done, u + 1)
                            copy(eng, out[:rows[t], t, c0:c0 + n], acc[:rows[t], u % 4, :n], t, c0, n).then_inc(done, 1)

                @block.scalar
                def _(act):
                    if add is None:
                        evacuate(act, 0, lambda e, o, p, t, c0, n: e.copy(o, p), even_out)

                @block.vector
                def _(dve):
                    if add is None:
                        evacuate(dve, 1, lambda e, o, p, t, c0, n: e.tensor_copy(o, p), odd_out)
                    else:
                        for u, (j, t) in enumerate(units):
                            c0, n = chunks[j]
                            dve.wait_ge(mm_done, u + 1)
                            dve.tensor_tensor(out[:rows[t], t, c0:c0 + n], acc[:rows[t], u % 4, :n],
                                              add[:rows[t], t, c0:c0 + n], ALU.add).then_inc((even_out, odd_out)[u % 2], 1)

    def norm_heads(self, tag, x, rows, groups):
        nc = self.nc
        heads = sum(g[1] for g in groups)
        ctx = ExitStack()
        with ctx:
            nt = len(rows)
            sq = self.sb(f"{tag}_sq", [P, 512], F32, ctx)
            ss = self.sb(f"{tag}_ss", [P, nt, heads], F32, ctx)
            chain, sums_done, root_done = (self.sem(f"{tag}_{n}") for n in ("chain", "sums", "root"))

            def view(t, r, c0, nh, stride, size):
                return x[:r, t, c0:c0 + nh * stride].rearrange("p (h s) -> p h s", s=stride)[:, :, :size]

            with nc.Block() as block:
                @block.vector
                def _(dve):
                    c = Chain(dve, chain)
                    c.link(dve.memset(ss[:], 1.0))
                    for t, r in enumerate(rows):
                        h = 0
                        for c0, nh, stride, size, gain in groups:
                            v = view(t, r, c0, nh, stride, size)
                            s = sq[:r, :nh * size].rearrange("p (h s) -> p h s", s=size)
                            c.link(dve.tensor_tensor(s, v, v, ALU.mult))
                            c.link(dve.tensor_reduce(ss[:r, t, h:h + nh], s, AX, ALU.add))
                            c.link(dve.tensor_scalar(ss[:r, t, h:h + nh], ss[:r, t, h:h + nh], 1.0 / size, EPS, ALU.mult, ALU.add))
                            h += nh
                    dve.sem_inc(sums_done, 1)
                    dve.wait_ge(root_done, 1)
                    c.link(dve.reciprocal(ss[:], ss[:]))
                    for t, r in enumerate(rows):
                        h = 0
                        for c0, nh, stride, size, gain in groups:
                            v = view(t, r, c0, nh, stride, size)
                            c.link(dve.tensor_tensor(v, v, ss[:r, t, h:h + nh].unsqueeze(2).to_broadcast([r, nh, size]), ALU.mult))
                            c.link(dve.tensor_tensor(v, v, gain[:r, :].unsqueeze(1).to_broadcast([r, nh, size]), ALU.mult))
                            h += nh

                @block.scalar
                def _(act):
                    act.wait_ge(sums_done, 1)
                    act.activation(ss[:], ss[:], ACT.Sqrt).then_inc(root_done, 1)

    def transposes(self, tag, batches):
        nc, ident = self.nc, self.ident
        ctx = ExitStack()
        with ctx:
            tr = self.ps(f"{tag}_tr", [P, 4, 512], ctx)
            tr_done, act_out, dve_out = (self.sem(f"{tag}_{n}") for n in ("tr_done", "act_out", "dve_out"))

            def bank(u):
                dst, srcs = batches[u]
                m, r = dst.shape[0], dst.shape[-1]
                return tr[:m, u % 4, :len(srcs) * r].rearrange("p (n r) -> p n r", r=r)

            with nc.Block() as block:
                @block.tensor
                def _(pe):
                    for u, (dst, srcs) in enumerate(batches):
                        if u >= 4:
                            pe.wait_ge((act_out, dve_out)[u % 2], (u - 4) // 2 + 1)
                        for n, src in enumerate(srcs):
                            r = src.shape[0]
                            last = pe.transpose(bank(u)[:, n, :], src, ident[:r, :r])
                        last.then_inc(tr_done, 1)

                @block.scalar
                def _(act):
                    for u in range(0, len(batches), 2):
                        act.wait_ge(tr_done, u + 1)
                        act.copy(batches[u][0], bank(u)).then_inc(act_out, 1)

                @block.vector
                def _(dve):
                    for u in range(1, len(batches), 2):
                        dve.wait_ge(tr_done, u + 1)
                        dve.tensor_copy(batches[u][0], bank(u)).then_inc(dve_out, 1)

    def copies(self, tag, pairs, done=None):
        done = done or self.sem(f"{tag}_copied")
        with self.nc.Block() as block:
            @block.sync
            def _(sp):
                with self.nc.allow_non_contiguous_dma(reason="small rows"):
                    for dst, src in pairs:
                        sp.dma_start(dst, src).then_inc(done, 16)
                sp.wait_ge(done, 16 * len(pairs))

    def build(self):
        nc, i, o = self.nc, self.i, self.o
        with self.ctx:
            self.store_sems = {n: nc.alloc_semaphore(name=f"stored_{n}") for n in ("new_rows", "mem_rows", "y_even", "y_odd")}
            self.constants()
            xT = self.sb("xn_t", [P, KD, NCOL])
            self.xT = xT
            xs = [i["x_prompt"][0, P * t:P * t + P, :] for t in range(TP)] + [i["x_sample"][:, 0, :]]
            self.norm_rows("mix", xs, i["ln_mix"], ROWS, xT)
            self.oT = self.sb("o_t", [P, 12, NCOL])
            attn = ExitStack()
            with attn:
                self.attention(attn)
            self.finish(xs)

    def attention(self, ctx):
        self.bias_tables(ctx)
        self.ht = self.sb("heads_t", [P, N_SLOT, NCOL], F32, ctx)
        self.qs_t = self.sb("sample_q_t", [P, 2 * HQ, DB], F32, ctx)
        self.qi_t = self.sb("sample_qi_t", [P, IH, DB], F32, ctx)
        self.ks_t = self.sb("sample_k_t", [DH, 3 * KV, DB], F32, ctx)
        self.vals = self.sb("values", [P, NT, 3, KV, DH], F32, ctx)
        self.w_idx = self.sb("index_weights", [P, NT, IH], F32, ctx)
        self.g_nsa = self.sb("branch_gates", [P, NT, 3 * HQ], F32, ctx)
        self.new_score = self.sb("new_key_score", [DB, 1], F32, ctx)
        tmp = ExitStack()
        with tmp:
            self.project(tmp)
        self.recycle()
        self.kc_t = self.sb("cmp_k_t", [P, DB, NCH_S], F32, ctx)
        self.kcp_t = self.sb("cmp_kp_t", [P, KV, NCH_P], F32, ctx)
        self.vc = self.sb("cmp_v", [P, DB, 2, KV, DH], F32, ctx)
        self.vcp = self.sb("cmp_vp", [NCH_P, KV, DH], F32, ctx)
        self.sample_constants(ctx)
        self.best_ix = self.sb("pi_ix", [DB, TOPA_S], U32, ctx)
        space = self.oT[:DB].rearrange("p a b -> p (a b)")
        self.pick_work, self.best = space[:, :PAST + 1], space[:, PAST + 1:PAST + 1 + TOPA_S]
        self.pick_next = 0
        self.index_scores()
        self.copies("da_back", [(self.pick_work[:, 0:PAST], self.s["score"]), (self.pick_work[:, PAST:PAST + 1], self.new_score[:])])
        self.recycle()
        self.compress_all()
        prompt = ExitStack()
        with prompt:
            self.memory_rows(prompt)
            self.recycle()
            self.prompt_attention()
        self.recycle()
        self.sample_attention()

    def pick_round_step(self, c):
        n, part = 8 * (self.pick_next // 3), self.pick_next % 3
        if n >= TOPA_S:
            return
        dve, best, ix, work = c.eng, self.best[:, n:n + 8], self.best_ix[:, n:n + 8], self.pick_work
        if c.n:
            c.need(c.n)
        if part == 0:
            c.put(dve.max(best, work))
        elif part == 1:
            c.put(dve.max_index(ix, best, work))
        else:
            c.put(dve.match_replace(work, best, work, TAKEN))
        self.pick_next += 1

    def finish_rounds(self):
        rounds = self.sem("pi_last_rounds")
        with self.nc.Block() as block:
            @block.vector
            def _(dve):
                c = Chain(dve, rounds)
                while self.pick_next < 3 * TOPA_S // 8:
                    self.pick_round_step(c)
                if c.n:
                    c.need(c.n)

    def project(self, ctx):
        nc, i, o = self.nc, self.i, self.o
        pr = self.pr = self.sb("proj", [P, NT, IN_W], F32, ctx)
        self.linear("in", self.xT, ROWS, i["w_in"], IN_W, pr)
        g64, g128 = self.g64, self.g128
        self.norm_heads("heads", pr, ROWS, [
            (Q_A, HQ, DH, DH, g64[:, 0, :]), (KV_A, KV, 128, DH, g64[:, 1, :]), (Q_B, HQ, DH, DH, g64[:, 2, :]),
            (KV_S, KV, 128, DH, g64[:, 4, :]), (KV_W, KV, 128, DH, g64[:, 5, :]), (Q_M, HM, DHM, DHM, g128[:, 0, :])])
        pairs = []
        for name, c0, w in (("a_kv", KV_A, 256), ("a_kidx", K_I, 64), ("cmp_kv", KV_C, 256), ("slc_kv", KV_S, 256), ("win_kv", KV_W, 256)):
            for t in range(TP):
                pairs.append((o[name + "_p"][0, P * t:P * t + P], pr[:, t, c0:c0 + w]))
            if name != "win_kv":
                pairs.append((o[name + "_s"][:, 0], pr[:DB, TP, c0:c0 + w]))
        pairs.append((o["win_kv_s"][:, WIN - 1], pr[:DB, TP, KV_W:KV_W + 256]))
        pairs.append((o["win_kv_s"][:, 0:WIN - 1], i["cache_win_kv"][:, 1:WIN]))
        self.copies("new_rows", pairs, self.stores("new_rows"))
        self.keep_values()
        self.self_score()
        self.turn_heads()

    def self_score(self):
        pr = self.pr
        ctx = ExitStack()
        with ctx:
            prod = self.sb("own_prod", [DB, IH, DH], F32, ctx)
            dots = self.sb("own_dots", [DB, IH], F32, ctx)
            chain = self.sem("own_chain")
            with self.nc.Block() as block:
                @block.vector
                def _(dve):
                    c = Chain(dve, chain)
                    q = pr[:DB, TP, Q_I:Q_I + 256].rearrange("p (h s) -> p h s", h=IH)
                    k = pr[:DB, TP, K_I:K_I + DH].unsqueeze(1).to_broadcast([DB, IH, DH])
                    c.link(dve.tensor_tensor(prod[:], q, k, ALU.mult))
                    c.link(dve.tensor_reduce(dots[:], prod[:], AX, ALU.add))
                    c.link(dve.scalar_tensor_tensor(out=dots[:], in0=dots[:], scalar=0.0, in1=pr[:DB, TP, W_I:W_I + IH], op0=ALU.max, op1=ALU.mult))
                    c.link(dve.tensor_reduce(self.new_score[:], dots[:], AX, ALU.add))

    def keep_values(self):
        pr, vals, w_idx, g_nsa = self.pr, self.vals, self.w_idx, self.g_nsa
        kept, gated = self.sem("values_kept"), self.sem("gates_done")
        with self.nc.Block() as block:
            @block.gpsimd
            def _(pool):
                for t, r in enumerate(ROWS):
                    for n, c0 in enumerate((KV_A, KV_S, KV_W)):
                        src = pr[:r, t, c0:c0 + 256].rearrange("p (g s) -> p g s", g=KV)[:, :, DH:]
                        pool.tensor_copy(vals[:r, t, n], src).then_inc(kept, 1)
                    pool.tensor_copy(w_idx[:r, t, :], pr[:r, t, W_I:W_I + IH]).then_inc(kept, 1)

            @block.scalar
            def _(act):
                for t, r in enumerate(ROWS):
                    act.activation(g_nsa[:r, t, :], pr[:r, t, G_N:G_N + 3 * HQ], ACT.Sigmoid).then_inc(gated, 1)

    def memory_rows(self, ctx):
        i, o = self.i, self.o
        mt = MEM // P
        mkv = self.mkv = self.sb("mem_kv", [P, mt, HM * 2 * DHM], F32, ctx)
        self.km_t = self.sb("mem_k_t", [P, HM, MEM], F32, ctx)
        tmp = ExitStack()
        with tmp:
            mem_t = self.sb("mem_t", [P, KD, MEM], F32, tmp)
            self.norm_rows("mem", [i["mem_prompt"][0, P * t:P * t + P, :] for t in range(mt)], i["ln_mem"], [P] * mt, mem_t)
            self.linear("mem_kv", mem_t, [P] * mt, i["w_mem_kv"], HM * 2 * DHM, mkv)
        self.norm_heads("mem_heads", mkv, [P] * mt, [(0, HM, 2 * DHM, DHM, self.g128[:, 1, :])])
        self.copies("mem_rows", [(o["mem_kv_p"][0, P * t:P * t + P, :], mkv[:, t, :]) for t in range(mt)],
                    self.stores("mem_rows"))
        self.transposes("mem_k", [(self.km_t[:, 0:4, P * t:P * t + P],
                                   [mkv[:, t, 2 * DHM * h:2 * DHM * h + DHM] for h in range(HM)]) for t in range(mt)])

    def bias_tables(self, ctx):
        nc, i, s = self.nc, self.i, self.s
        nt = PAST // P + 1
        width = nt * P
        tmp = ExitStack()
        self.bias_cmp = self.sb("bias_cmp", [DB * HQ, NCH_S], F32, ctx)
        self.bias_win = self.sb("bias_win", [DB * HQ, WIN], F32, ctx)
        self.bias_self = self.sb("bias_self", [DB * HQ, 2], F32, ctx)
        with tmp:
            bounds = self.sb("bounds", [NB, 2], F32, tmp)
            dist_i = self.sb("dist_i", [NB, width], I32, tmp)
            dist = self.sb("dist", [NB, width], F32, tmp)
            hot = self.sb("hot", [NB, width], F32, tmp)
            table = self.sb("table", [NB, 16], F32, tmp)
            rep = self.sb("table_rep", [NB, 2, DB, HQ], F32, tmp)
            pos = self.sb("pos", [P, nt, 16], F32, tmp)
            rev = self.sb("rev", [16, 640], F32, tmp)
            by_head = self.sb("by_head", [16, PAST], F32, tmp)
            pos_ps = self.ps("pos_ps", [P, 2, 512], tmp)
            rev_ps = self.ps("rev_ps", [P, 512], tmp)
            win_ps = self.ps("win_ps", [P, 512], tmp)
            cmp_ps = self.ps("cmp_ps", [P, 512], tmp)
            self_ps = self.ps("self_ps", [P, 512], tmp)
            row_ps = self.ps("row_ps", [P, 2, 512], tmp)
            row_mm, row_out = self.sem("bias_row_mm"), self.sem("bias_row_out")
            loaded, iota_done, hot_done, mm_done, out_done, chain, stored = (
                self.sem(f"bias_{n}") for n in ("loaded", "iota", "hot", "mm", "out", "chain", "stored"))
            with nc.Block() as block:
                @block.sync
                def _(sp):
                    sp.dma_start(bounds[:], i["bounds"]).then_inc(loaded, 16)
                    sp.dma_start(table[:], i["rel_table"]).then_inc(loaded, 16)
                    sp.wait_ge(out_done, 1)
                    sp.dma_start(s["bias_rev"], rev[:]).then_inc(stored, 16)
                    sp.dma_start(s["bias_pos"][:nt * P].rearrange("(t p) h -> p t h", p=P), pos[:]).then_inc(stored, 16)
                    sp.dma_start(s["bias_head"], by_head[:]).then_inc(stored, 16)
                    sp.wait_ge(stored, 48)

                @block.gpsimd
                def _(pool):
                    pool.iota(dist_i[:], pattern=[[-1, width]], base=PAST, channel_multiplier=0).then_inc(iota_done, 1)

                @block.vector
                def _(dve):
                    c = Chain(dve, chain)
                    dve.wait_ge(iota_done, 1)
                    dve.wait_ge(loaded, 32)
                    c.link(dve.tensor_copy(dist[:], dist_i[:]))
                    c.link(dve.tensor_scalar(hot[:], dist[:], bounds[:, 0:1], None, ALU.is_ge))
                    c.link(dve.tensor_scalar(dist[:], dist[:], bounds[:, 1:2], None, ALU.is_lt))
                    dve.tensor_tensor(hot[:], hot[:], dist[:], ALU.mult).then_inc(hot_done, 1)
                    for b in range(DB):
                        dve.tensor_copy(rep[:, 0, b, :], table[:, 0:HQ])
                        last = dve.tensor_copy(rep[:, 1, b, :], table[:, HQ:16])
                    last.then_inc(hot_done, 1)
                    c.link(dve.memset(rev[:], NEG))
                    dve.wait_ge(mm_done, 1)
                    flat = pos[:].rearrange("p t h -> p (t h)")
                    c.link(dve.tensor_copy(flat[:, 0:512], pos_ps[:, 0, :]))
                    c.link(dve.tensor_copy(flat[:, 512:nt * 16], pos_ps[:, 1, :nt * 16 - 512]))
                    c.link(dve.tensor_copy(rev[:, 0:512], rev_ps[:16, :]))
                    for n in range(PAST // 512):
                        dve.wait_ge(row_mm, n + 1)
                        c.link(dve.tensor_copy(by_head[:, 512 * n:512 * n + 512], row_ps[:16, n % 2, :]))
                        dve.sem_inc(row_out, 1)
                    c.link(dve.tensor_copy(self.bias_win[:], win_ps[:DB * HQ, :]))
                    c.link(dve.tensor_copy(self.bias_cmp[:], cmp_ps[:DB * HQ, :NCH_S]))
                    dve.tensor_copy(self.bias_self[:], self_ps[:DB * HQ, :2]).then_inc(out_done, 1)

                @block.tensor
                def _(pe):
                    pe.wait_ge(hot_done, 2)
                    for t in range(nt):
                        pe.matmul(pos_ps[:, t // 32, 16 * (t % 32):16 * (t % 32) + 16], hot[:, P * t:P * t + P], table[:],
                                  start=True, stop=True)
                    pe.matmul(rev_ps[:16, :], table[:], hot[:, PAST - 511:PAST + 1], start=True, stop=True)
                    rep_b = rep[:, 1].rearrange("k b h -> k (b h)")
                    pe.matmul(win_ps[:DB * HQ, :], rep_b, hot[:, PAST - WIN:PAST], start=True, stop=True)
                    pe.matmul(cmp_ps[:DB * HQ, :NCMP_S], rep_b, hot[:, 31:31 + 16 * NCMP_S - 15:16], start=True, stop=True)
                    pe.matmul(cmp_ps[:DB * HQ, NCMP_S:NCH_S], rep_b, hot[:, 0:1], start=True, stop=True)
                    for n in range(2):
                        last = pe.matmul(self_ps[:DB * HQ, n:n + 1], rep[:, n].rearrange("k b h -> k (b h)"), hot[:, PAST:PAST + 1],
                                         start=True, stop=True)
                    last.then_inc(mm_done, 1)
                    for n in range(PAST // 512):
                        if n >= 2:
                            pe.wait_ge(row_out, n - 1)
                        pe.matmul(row_ps[:16, n % 2, :], table[:], hot[:, 512 * n:512 * n + 512], start=True, stop=True).then_inc(row_mm, 1)

    def turn_heads(self):
        pr = self.pr
        ht = self.ht
        tmp = ExitStack()
        with tmp:
            dup = self.sb("key_pairs", [P, TP, 7, 2, DH], F32, tmp)
            dup_s = self.sb("sample_pairs", [DB, 2 * HQ + IH, 2, DH], F32, tmp)
            dup_done = self.sem("pairs_done")
            with self.nc.Block() as block:
                @block.vector
                def _(dve):
                    for t in range(TP):
                        for n, c0 in enumerate((KV_A, KV_S, KV_W)):
                            src = pr[:, t, c0:c0 + 256].rearrange("p (g s) -> p g s", g=KV)[:, :, :DH]
                            for half in range(2):
                                dve.tensor_copy(dup[:, t, 2 * n:2 * n + 2, half, :], src).then_inc(dup_done, 1)
                        dve.tensor_copy(dup[:, t, 6], pr[:, t, K_I:K_I + DH].unsqueeze(1).to_broadcast([P, 2, DH])).then_inc(dup_done, 1)
                    for half in range(2):
                        for h0, nh, c0 in ((0, HQ, Q_A), (HQ, HQ, Q_B), (2 * HQ, IH, Q_I)):
                            dve.tensor_copy(dup_s[:, h0:h0 + nh, half, :], pr[:DB, TP, c0:c0 + DH * nh].rearrange("p (h s) -> p h s", h=nh)).then_inc(dup_done, 1)

            batches = []
            for t, r in enumerate(ROWS):
                row = pr[:r, t, :]
                if t < TP:
                    srcs = [row[:, c:c + P] for c0 in (Q_A, Q_B, Q_M) for c in range(c0, c0 + 512, P)]
                    srcs += [dup[:, t, n].rearrange("p t d -> p (t d)") for n in range(7)]
                    srcs += [row[:, Q_I:Q_I + P], row[:, Q_I + P:Q_I + 2 * P]]
                else:
                    srcs = [row[:, Q_M + P * h:Q_M + P * h + P] for h in range(HM)]
                first = 0 if t < TP else S_QM
                for n in range(0, len(srcs), 4):
                    m = min(4, len(srcs) - n)
                    batches.append((ht[:, first + n:first + n + m, P * t:P * t + r], srcs[n:n + m]))
            row = pr[:DB, TP, :]
            both = [dup_s[:, h].rearrange("p t d -> p (t d)") for h in range(2 * HQ + IH)]
            batches.append((self.qs_t[:], both[:2 * HQ]))
            batches.append((self.qi_t[:], both[2 * HQ:]))
            batches.append((self.ks_t[:], [row[:, c0 + 128 * g:c0 + 128 * g + DH] for c0 in (KV_A, KV_S, KV_W) for g in range(KV)]))
            self.transposes("turn", batches)

    def compress_all(self):
        nc, i, o, ident = self.nc, self.i, self.o, self.ident
        ROUND_AT = (1, 7, 15)
        kc_t, kcp_t, vc, vcp = self.kc_t, self.kcp_t, self.vc, self.vcp
        tmp = ExitStack()
        with tmp:
            w1 = self.sb("cmp_w1", [P, 2 * STRIDE, P], F32, tmp)
            w2 = self.sb("cmp_w2", [P, P], F32, tmp)
            pe_t = self.sb("cmp_pe_t", [P, 2 * STRIDE], F32, tmp)
            peh = self.sb("cmp_peh", [P, 1], F32, tmp)
            ch = self.sb("cmp_ch", [P, 2, 16, KV, 2, DH], F32, tmp)
            ct = self.sb("cmp_ct", [P, STRIDE, KV, NCH_S], F32, tmp)
            hid = self.sb("cmp_hid", [P, KV, NCH_S], F32, tmp)
            kn = self.sb("cmp_kn", [P, 2, KV, DH], F32, tmp)
            sq = self.sb("cmp_sq", [P, 2, KV, DH], F32, tmp)
            ss = self.sb("cmp_ss", [P, 2 * KV], F32, tmp)
            kdup = self.sb("cmp_kdup", [NCH_P, KV, 2, DH], F32, tmp)
            tr = self.ps("cmp_tr", [P, 2, 512], tmp)
            hp = self.ps("cmp_hp", [P, 2, 512], tmp)
            op = self.ps("cmp_op", [P, 2, KV, 2, DH], tmp)
            kt = self.ps("cmp_kt", [P, 512], tmp)
            pp = self.ps("cmp_pp", [P, 512], tmp)
            (weights_in, chain, ch_in, tr_done, ct_act, ct_dve, hid_mm, hid_done, out_mm, out_v, kn_done,
             root_done, sq_sum, kt_mm, kt_out, peh_mm, peh_done, zeroed) = (self.sem(f"cmp_{n}") for n in (
                 "weights_in", "chain", "ch_in", "tr_done", "ct_act", "ct_dve", "hid_mm", "hid_done",
                 "out_mm", "out_v", "kn_done", "root_done", "sq_sum", "kt_mm", "kt_out", "peh_mm", "peh_done", "zeroed"))
            round_chain = self.sem("cmp_rounds")
            slot_in = [self.sem(f"cmp_slot_in{n}") for n in range(2)]
            units = [("prompt", 0)] + [("sample", b) for b in range(DB)]
            NU = len(units)

            def tiles(u):
                return [(NCH_P, 0)] if u == 0 else [(P, 0), (P, P)]

            def n_cmp(u):
                return NCMP_P if u == 0 else NCMP_S

            def bank(u, k):
                return 16 * u + k

            with nc.Block() as block:
                @block.sync
                def _(sp):
                    with nc.allow_non_contiguous_dma(reason="positional rows"):
                        sp.wait_ge(zeroed, 2)
                        for c in range(2):
                            half = slice(DH * c, DH * c + DH)
                            sp.dma_start(w1[half, :, half], i["w_cmp1"][c].rearrange("r d h -> d r h")).then_inc(weights_in, 16)
                            sp.dma_start(pe_t[half, :], i["cmp_pe"][c].rearrange("r d -> d r")).then_inc(weights_in, 16)
                            sp.dma_start(w2[half, half], i["w_cmp2"][c]).then_inc(weights_in, 16)
                    sp.dma_start(ch[:NCH_P, 0].rearrange("p a b c d -> p (a b c d)"),
                                 o["cmp_kv_p"][0].rearrange("(n r) w -> n (r w)", r=STRIDE)).then_inc(ch_in, 16)

                @block.gpsimd
                def _(pool):
                    pool.memset(w1[:], 0.0).then_inc(zeroed, 1)
                    pool.memset(w2[:], 0.0).then_inc(zeroed, 1)
                    view = i["cache_cmp_kv"].rearrange("n (c r) w -> (n c) (r w)", r=STRIDE)
                    for n in range(2 * DB):
                        slot = (1 + n) % 2
                        if n == 1:
                            pool.wait_ge(tr_done, bank(0, 15) + 1)
                        if n >= 2:
                            pool.wait_ge(tr_done, bank(1 + (n - 2) // 2, 15) + 1)
                        pool.indirect_dma_start(
                            out=ch[:, slot].rearrange("p a b c d -> p (a b c d)"), out_offset=None, in_=view,
                            in_offset=bass.IndirectOffsetOnAxis(ap=self.row_of[:, n:n + 1], axis=0)).then_inc(slot_in[slot], 16)

                def evacuate(eng, copy, done, parity, between=None):
                    def run(u):
                        w = NCH_P if u == 0 else NCH_S
                        if u:
                            eng.wait_ge(hid_mm, u)
                        for k in range(parity, 16, 2):
                            eng.wait_ge(tr_done, bank(u, k) + 1)
                            copy(ct[:, k, :, :w], tr[:, k % 2, :KV * w].rearrange("p (g n) -> p g n", g=KV)).then_inc(done, 1)
                            if u and between and k in ROUND_AT:
                                between()
                    return run

                @block.tensor
                def _(pe):
                    pe.wait_ge(weights_in, 16 * 6)
                    for k in range(2 * STRIDE):
                        last = pe.matmul(pp[:, 0:1], w1[:, k, :], pe_t[:, k:k + 1], start=(k == 0), stop=(k == 2 * STRIDE - 1))
                    last.then_inc(peh_mm, 1)

                    def second(u):
                        n = n_cmp(u)
                        pe.wait_ge(hid_done, u + 1)
                        if u:
                            pe.wait_ge(out_v, 2 * u - 1)
                            pe.wait_ge(kn_done, u)
                        for s0, (r, c0) in enumerate(tiles(u)):
                            m = min(r, n - c0)
                            for g in range(KV):
                                last = pe.matmul(op[:m, s0, g].rearrange("p c d -> p (c d)"), hid[:, g, c0:c0 + m], w2[:], start=True, stop=True)
                        last.then_inc(out_mm, 1)

                    def third(u):
                        n = n_cmp(u)
                        pe.wait_ge(kn_done, u + 1)
                        if u:
                            pe.wait_ge(kt_out, u)
                        if u == 0:
                            for g in range(KV):
                                last = pe.transpose(kt[:, NCH_P * g:NCH_P * g + n], kdup[:n, g].rearrange("p t d -> p (t d)"), ident[:n, :n])
                        else:
                            for s0, (r, c0) in enumerate(tiles(u)):
                                m = min(r, n - c0)
                                last = pe.transpose(kt[:, c0:c0 + m], kn[:m, s0].rearrange("p g d -> p (g d)"), ident[:m, :m])
                        last.then_inc(kt_mm, 1)

                    for u in range(NU):
                        n = n_cmp(u)
                        if u == 0:
                            pe.wait_ge(ch_in, 16)
                        else:
                            pe.wait_ge(slot_in[0], 16 * u)
                            pe.wait_ge(slot_in[1], 16 * u)
                        w = NCH_P if u == 0 else NCH_S
                        for k in range(16):
                            e = bank(u, k)
                            if e >= 2:
                                pe.wait_ge((ct_act, ct_dve)[k % 2], (e - 2) // 2 + 1)
                            for g in range(KV):
                                for s0, (r, c0) in enumerate(tiles(u)):
                                    slot = 0 if u == 0 else (1 + s0) % 2
                                    last = pe.transpose(tr[:, k % 2, g * w + c0:g * w + c0 + r],
                                                        ch[:r, slot, k, g].rearrange("p c d -> p (c d)"), ident[:r, :r])
                            last.then_inc(tr_done, 1)
                        pe.wait_ge(ct_act, 8 * (u + 1))
                        pe.wait_ge(ct_dve, 8 * (u + 1))
                        if u >= 2:
                            pe.wait_ge(hid_done, u - 1)
                        for k in range(2 * STRIDE):
                            j, r = k // STRIDE, k % STRIDE
                            last = pe.matmul(hp[:, u % 2, :KV * n].rearrange("p (g n) -> p g n", g=KV), w1[:, k, :],
                                             ct[:, r, :, j:j + n], start=(k == 0), stop=(k == 2 * STRIDE - 1))
                        last.then_inc(hid_mm, 1)
                        if u:
                            second(u - 1)
                        if u:
                            third(u - 1)
                    second(NU - 1)
                    third(NU - 1)

                @block.scalar
                def _(act):
                    act.wait_ge(peh_done, 1)
                    evac = evacuate(act, act.copy, ct_act, 0)

                    def gelu(u):
                        n = n_cmp(u)
                        act.wait_ge(hid_mm, u + 1)
                        if u:
                            act.wait_ge(out_mm, u)
                        act.activation(hid[:, :, :n], hp[:, u % 2, :KV * n].rearrange("p (g n) -> p g n", g=KV),
                                       ACT.Gelu_apprx_tanh, bias=peh[:, 0:1]).then_inc(hid_done, 1)

                    def root(u):
                        act.wait_ge(sq_sum, u + 1)
                        act.activation(ss[:], ss[:], ACT.Sqrt).then_inc(root_done, 1)

                    for u in range(NU):
                        evac(u)
                        if u:
                            root(u - 1)
                        gelu(u)
                    root(NU - 1)

                @block.vector
                def _(dve):
                    c_ = Chain(dve, chain)
                    rounds = Chain(dve, round_chain)
                    dve.wait_ge(peh_mm, 1)
                    dve.tensor_copy(peh[:], pp[:, 0:1]).then_inc(peh_done, 1)
                    evac = evacuate(dve, dve.tensor_copy, ct_dve, 1, lambda: self.pick_round_step(rounds))
                    c_.link(dve.memset(ss[:], 1.0))

                    def keys(u):
                        n = n_cmp(u)
                        dve.wait_ge(out_mm, u + 1)
                        if u >= 1:
                            dve.wait_ge(kt_mm, u)
                        for s0, (r, c0) in enumerate(tiles(u)):
                            m = min(r, n - c0)
                            dve.tensor_copy(vcp[:m] if u == 0 else vc[:m, u - 1, s0], op[:m, s0, :, 1, :]).then_inc(out_v, 1)
                            c_.link(dve.tensor_copy(kn[:m, s0], op[:m, s0, :, 0, :]))
                            c_.link(dve.tensor_tensor(sq[:m, s0], kn[:m, s0], kn[:m, s0], ALU.mult))
                            c_.link(dve.tensor_reduce(ss[:m, KV * s0:KV * s0 + KV], sq[:m, s0], AX, ALU.add))
                            c_.link(dve.tensor_scalar(ss[:m, KV * s0:KV * s0 + KV], ss[:m, KV * s0:KV * s0 + KV], 1.0 / DH, EPS, ALU.mult, ALU.add))
                        dve.sem_inc(sq_sum, 1)
                        dve.wait_ge(root_done, u + 1)
                        c_.link(dve.reciprocal(ss[:], ss[:]))
                        for s0, (r, c0) in enumerate(tiles(u)):
                            m = min(r, n - c0)
                            for g in range(KV):
                                col = KV * s0 + g
                                last = dve.scalar_tensor_tensor(out=kn[:m, s0, g, :], in0=kn[:m, s0, g, :], scalar=ss[:m, col:col + 1],
                                                                in1=self.g64[:m, 3, :], op0=ALU.mult, op1=ALU.mult)
                                if u == 0:
                                    c_.link(last)
                        if u == 0:
                            for half in range(2):
                                last = dve.tensor_copy(kdup[:n, :, half, :], kn[:n, 0])
                        last.then_inc(kn_done, 1)

                    def turned(u):
                        n = n_cmp(u)
                        dve.wait_ge(kt_mm, u + 1)
                        if u == 0:
                            last = dve.tensor_copy(kcp_t[:, :, :n], kt[:, :KV * NCH_P].rearrange("p (g n) -> p g n", g=KV)[:, :, :n])
                        else:
                            last = dve.tensor_copy(kc_t[:, u - 1, :n], kt[:, :n])
                        last.then_inc(kt_out, 1)

                    for u in range(NU):
                        evac(u)
                        if u:
                            keys(u - 1)
                            turned(u - 1)
                    keys(NU - 1)
                    turned(NU - 1)
                    rounds.need(rounds.n)

    def prompt_attention(self):
        ctx = ExitStack()
        with ctx:
            bias_t = self.bias_t = self.sb("bias_t", [P, 16, SEQ], F32, ctx)
            self.load_bias()
            self.mask_a = self.sb("mask_a", [P, TP - 1, SEQ], F32, ctx)
            self.o_rows = self.sb("o_rows", [P, TP, 3, 512], F32, ctx)
            self.select_prompt()
            self.attend_prompt()
            self.finish_rounds()
            self.transposes("o_turn", [(self.oT[:, 4 * b:4 * b + 4, P * t:P * t + P],
                                        [self.o_rows[:, t, b, P * k:P * k + P] for k in range(4)])
                                       for t in range(TP) for b in range(3)])

    def load_bias(self):
        nc, bias_t = self.nc, self.bias_t
        ctx = ExitStack()
        with ctx:
            up = self.sb("lb_up", [P, 16, SEQ], F32, ctx)
            flip = self.sb("lb_flip", [P, P], F32, ctx)
            ps = self.ps("lb_ps", [P, 4, 512], ctx)
            loaded = [self.sem(f"lb_in{n}") for n in range(4)]
            made, mm, act_out, dve_out = (self.sem(f"lb_{n}") for n in ("made", "mm", "act_out", "dve_out"))
            with nc.Block() as block:
                @block.sync
                def _(sp):
                    for n in range(4):
                        sp.dma_start(up[:, 4 * n:4 * n + 4, :], bass.AP(self.s["bias_rev"].tensor, 640 * 4 * n, [[1, P], [640, 4], [1, SEQ]])).then_inc(loaded[n], 16)

                @block.gpsimd
                def _(pool):
                    pool.memset(flip[:], 0.0).then_inc(made, 1)
                    pool.wait_ge(made, 1)
                    pool.affine_select(out=flip[:], in_=flip[:], compare_op=ALU.not_equal, fill=1.0, base=1 - P, pattern=[[1, P]],
                                       channel_multiplier=1).then_inc(made, 1)

                @block.tensor
                def _(pe):
                    pe.wait_ge(made, 2)
                    for h in range(16):
                        pe.wait_ge(loaded[h // 4], 16)
                        if h >= 4:
                            pe.wait_ge((act_out, dve_out)[h % 2], (h - 4) // 2 + 1)
                        pe.matmul(ps[:, h % 4, :], flip[:], up[:, h, :], start=True, stop=True).then_inc(mm, 1)

                @block.scalar
                def _(act):
                    for h in range(0, 16, 2):
                        act.wait_ge(mm, h + 1)
                        act.copy(bias_t[:, h, :], ps[:, h % 4, :]).then_inc(act_out, 1)

                @block.vector
                def _(dve):
                    for h in range(1, 16, 2):
                        dve.wait_ge(mm, h + 1)
                        dve.tensor_copy(bias_t[:, h, :], ps[:, h % 4, :]).then_inc(dve_out, 1)

    def select_prompt(self):
        nc, ht, w_idx, mask = self.nc, self.ht, self.w_idx, self.mask_a
        ctx = ExitStack()
        with ctx:
            pos = self.sb("ix_relu", [P, 2, SEQ], F32, ctx)
            work = self.sb("ix_score", [P, TP - 1, SEQ], F32, ctx)
            best = self.sb("ix_best", [P, TP - 1, 8], F32, ctx)
            sp_ = self.ps("ix_ps", [P, 2, 512], ctx)
            mm, relu_done, add_done, causal_done, chain = (self.sem(f"ix_{n}") for n in ("mm", "relu", "add", "causal", "chain"))
            units = [(t, h) for t in range(1, TP) for h in range(IH)]
            with nc.Block() as block:
                @block.tensor
                def _(pe):
                    for u, (t, h) in enumerate(units):
                        half = slice(DH * (h % 2), DH * (h % 2) + DH)
                        nk = P * (t + 1)
                        if u >= 2:
                            pe.wait_ge(relu_done, u - 1)
                        pe.matmul(sp_[:, u % 2, :nk], ht[half, S_QI + h // 2, P * t:P * t + P], ht[half, S_KI, :nk],
                                  start=True, stop=True).then_inc(mm, 1)

                @block.scalar
                def _(act):
                    for u, (t, h) in enumerate(units):
                        nk = P * (t + 1)
                        act.wait_ge(mm, u + 1)
                        if u >= 2:
                            act.wait_ge(add_done, u - 1)
                        act.activation(pos[:, u % 2, :nk], sp_[:, u % 2, :nk], ACT.Relu).then_inc(relu_done, 1)

                @block.gpsimd
                def _(pool):
                    for t in range(1, TP):
                        pool.wait_ge(add_done, IH * t)
                        diag = work[:, t - 1, P * t:P * t + P]
                        pool.affine_select(out=diag, in_=diag, compare_op=ALU.is_ge, fill=NEG, base=0,
                                           pattern=[[-1, P]], channel_multiplier=1).then_inc(causal_done, 1)

                @block.vector
                def _(dve):
                    c = Chain(dve, chain)
                    for u, (t, h) in enumerate(units):
                        nk = P * (t + 1)
                        w = work[:, t - 1, :nk]
                        dve.wait_ge(relu_done, u + 1)
                        if h == 0:
                            dve.tensor_scalar(w, pos[:, u % 2, :nk], w_idx[:, t, h:h + 1], None, ALU.mult).then_inc(add_done, 1)
                        else:
                            dve.wait_ge(add_done, u)
                            dve.scalar_tensor_tensor(out=w, in0=pos[:, u % 2, :nk], scalar=w_idx[:, t, h:h + 1], in1=w,
                                                     op0=ALU.mult, op1=ALU.add).then_inc(add_done, 1)
                    dve.wait_ge(causal_done, TP - 1)
                    taken = [None] * TP
                    for _round in range(TOPA_P // 8):
                        found = [None] * TP
                        for t in range(1, TP):
                            if taken[t]:
                                c.need(taken[t])
                            found[t] = c.put(dve.max(best[:, t - 1, :], work[:, t - 1, :P * (t + 1)]))
                        for t in range(1, TP):
                            w = work[:, t - 1, :P * (t + 1)]
                            c.need(found[t])
                            taken[t] = c.put(dve.match_replace(w, best[:, t - 1, :], w, TAKEN))
                    for t in range(1, TP):
                        m, w = mask[:, t - 1, :P * (t + 1)], work[:, t - 1, :P * (t + 1)]
                        c.need(taken[t])
                        c.link(dve.tensor_scalar(m, w, TAKEN, None, ALU.is_equal))
                        c.link(dve.tensor_scalar(m, m, -1.0, -NEG, ALU.add, ALU.mult))

    def attend_prompt(self):
        nc, ht, ident = self.nc, self.ht, self.ident
        ctx = ExitStack()
        units = []
        for t in range(TP):
            units += [("a", h, t) for h in range(HQ)] + [("m", h, t) for h in range(HM)]
            units += [(kind, h, t) for h in range(HQ) for kind in "csw"]
        n = len(units)

        def keys(u):
            kind, h, t = units[u]
            return {"c": min(NCMP_P, (P // STRIDE) * t + 7), "m": MEM}.get(kind, P * (t + 1))

        def parts(u):
            return [(k, min(P, keys(u) - P * k)) for k in range(-(-keys(u) // P))]

        with ctx:
            lg = self.sb("at_logits", [P, 2, SEQ], F32, ctx)
            ex = self.sb("at_exp", [P, 2, SEQ], F32, ctx)
            et = self.sb("at_exp_t", [P, 2, 4, P], F32, ctx)
            mx = self.sb("at_max", [P, n], F32, ctx)
            sm = self.sb("at_sum", [P, n], F32, ctx)
            s_ps = self.ps("at_s_ps", [P, 2, 512], ctx)
            t_ps = self.ps("at_t_ps", [P, 2, 4, P], ctx)
            o_ps = self.ps("at_o_ps", [P, 2, 512], ctx)
            scored, logits_done, exp_done, turned, turn_out, mixed, fin_done, chain, round_chain = (self.sem(f"at_{x}") for x in (
                "scored", "logits", "exp", "turned", "turn_out", "mixed", "fin", "chain", "rounds"))

            with nc.Block() as block:
                @block.tensor
                def _(pe):
                    def score(u):
                        kind, h, t = units[u]
                        nk, g, cols = keys(u), h // GRP, slice(P * t, P * t + P)
                        half = slice(DH * (h % 2), DH * (h % 2) + DH)
                        q0 = S_QA if kind == "a" else S_QB
                        if u >= 2:
                            pe.wait_ge(logits_done, u - 1)
                            if units[u - 2][0] == "m":
                                pe.wait_ge(exp_done, u - 1)
                        if kind == "m":
                            lhs, rhs = ht[:, S_QM + h, cols], self.km_t[:, h, :]
                        else:
                            lhs = ht[half, q0 + h // 2, cols]
                            rhs = self.kcp_t[half, g, :nk] if kind == "c" else ht[half, {"a": S_KA, "s": S_KS, "w": S_KW}[kind] + g, :nk]
                        pe.matmul(s_ps[:, u % 2, :nk], lhs, rhs, start=True, stop=True).then_inc(scored, 1)

                    def turn(u):
                        pe.wait_ge(exp_done, u + 1)
                        if u >= 2:
                            pe.wait_ge(turn_out, u - 1)
                        for k, w in parts(u):
                            last = pe.transpose(t_ps[:w, u % 2, k, :], ex[:, u % 2, P * k:P * k + w], ident[:])
                        last.then_inc(turned, 1)

                    def mix(u):
                        kind, h, t = units[u]
                        g = h // GRP
                        pe.wait_ge(turn_out, u + 1)
                        if u >= 2:
                            pe.wait_ge(fin_done, u - 1)
                        dv = DHM if kind == "m" else DH
                        ps = parts(u)
                        for k, w in ps:
                            if kind == "m":
                                v = self.mkv[:, k, 2 * DHM * h + DHM:2 * DHM * (h + 1)]
                            elif kind == "c":
                                v = self.vcp[:w, g, :]
                            else:
                                v = self.vals[:w, k, {"a": 0, "s": 1, "w": 2}[kind], g, :]
                            last = pe.matmul(o_ps[:, u % 2, :dv], et[:w, u % 2, k, :], v, start=(k == 0), stop=(k == len(ps) - 1))
                        last.then_inc(mixed, 1)

                    for u in range(n + 2):
                        if u < n:
                            score(u)
                        if 1 <= u <= n:
                            turn(u - 1)
                        if u >= 2:
                            mix(u - 2)

                @block.scalar
                def _(act):
                    def exp(u):
                        kind, h, t = units[u]
                        act.wait_ge(logits_done, u + 1)
                        if u >= 2:
                            act.wait_ge(turned, u - 1)
                        src, scale = (s_ps, DHM ** -0.5) if kind == "m" else (lg, 1.0)
                        act.activation(ex[:, u % 2, :keys(u)], src[:, u % 2, :keys(u)], ACT.Exp, bias=mx[:, u:u + 1], scale=scale,
                                       accum_out=sm[:, u:u + 1]).then_inc(exp_done, 1)

                    def out(u):
                        act.wait_ge(turned, u + 1)
                        if u >= 2:
                            act.wait_ge(mixed, u - 1)
                        w = min(P, keys(u))
                        nk = len(parts(u))
                        act.copy(et[:w, u % 2, :nk, :], t_ps[:w, u % 2, :nk, :]).then_inc(turn_out, 1)

                    for u in range(n + 1):
                        if u < n:
                            exp(u)
                        if u >= 1:
                            out(u - 1)

                @block.vector
                def _(dve):
                    c = Chain(dve, chain)

                    def logits(u):
                        kind, h, t = units[u]
                        nk = keys(u)
                        l, m, sc = lg[:, u % 2, :nk], mx[:, u:u + 1], s_ps[:, u % 2, :nk]
                        dve.wait_ge(scored, u + 1)
                        if u >= 2:
                            dve.wait_ge(exp_done, u - 1)
                        x0 = SEQ - P - P * t
                        if kind == "m":
                            c.link(dve.tensor_reduce(m, sc, AX, ALU.max))
                            dve.tensor_scalar_mul(m, m, -DHM ** -0.5).then_inc(logits_done, 1)
                            return
                        if kind == "c":
                            bias = self.bias_t[:, HQ + h, x0 + 31:x0 + 31 + STRIDE * (nk - 1) + 1:STRIDE]
                        else:
                            bias = self.bias_t[:, h + (0 if kind == "a" else HQ), x0:x0 + nk]
                        if kind == "a" and t:
                            c.link(dve.tensor_tensor(l, sc, bias, ALU.add))
                            sc, bias = l, self.mask_a[:, t - 1, :nk]
                        c.link(dve.tensor_tensor_reduce(out=l, in0=sc, in1=bias, scale=1.0, scalar=NEG, op0=ALU.add, op1=ALU.max, accum_out=m))
                        dve.tensor_scalar(m, m, NEG / 10, -1.0, ALU.max, ALU.mult).then_inc(logits_done, 1)

                    def fin(u):
                        kind, h, t = units[u]
                        r = sm[:, u:u + 1]
                        dve.wait_ge(mixed, u + 1)
                        c.link(dve.tensor_scalar(r, r, 1e-30, None, ALU.max))
                        c.link(dve.reciprocal(r, r))
                        if kind == "a" or kind == "m":
                            w, b = (DH, 0) if kind == "a" else (DHM, 2)
                            dve.tensor_scalar(self.o_rows[:, t, b, w * h:w * h + w], o_ps[:, u % 2, :w], r, None, ALU.mult).then_inc(fin_done, 1)
                            return
                        o = self.o_rows[:, t, 1, DH * h:DH * h + DH]
                        gate = self.g_nsa[:, t, 3 * h + "csw".index(kind):3 * h + "csw".index(kind) + 1]
                        if kind == "c":
                            dve.tensor_scalar(o, o_ps[:, u % 2, :DH], r, gate, ALU.mult, ALU.mult).then_inc(fin_done, 1)
                        else:
                            c.link(dve.tensor_tensor(r, r, gate, ALU.mult))
                            dve.wait_ge(fin_done, u)
                            dve.scalar_tensor_tensor(out=o, in0=o_ps[:, u % 2, :DH], scalar=r, in1=o, op0=ALU.mult, op1=ALU.add).then_inc(fin_done, 1)

                    rounds = Chain(dve, round_chain)
                    for u in range(n + 3):
                        if u < n:
                            logits(u)
                        if u >= 3:
                            fin(u - 3)
                        if u % 3 == 2:
                            self.pick_round_step(rounds)
                    if rounds.n:
                        rounds.need(rounds.n)

    def sample_attention(self):
        ctx = ExitStack()
        with ctx:
            self.sample_dsa()
            self.recycle()
            self.sample_cmp_slc()
            self.recycle()
            self.sample_window()
            self.sample_memory()
            self.recycle()

    def sample_constants(self, ctx):
        nc, i, s = self.nc, self.i, self.s
        self.own_mask = self.sb("own_mask", [DB * HQ, DB], F32, ctx)
        self.gate_bh = self.sb("gate_bh", [DB * HQ, 3], F32, ctx)
        self.pages_all = self.sb("pages_all", [P, DB, NPAGE], F32, ctx)
        self.group_of = self.sb("group_of", [DB * HQ, DB * KV], F32, ctx)
        self.heads_of = self.sb("heads_of", [DB * KV, DB * HQ], F32, ctx)
        self.iota32 = self.sb("iota32", [P, NPAGE], F32, ctx)
        self.part = self.sb("partition_no", [P, 1], I32, ctx)
        self.row_of = self.sb("chunk_rows", [P, 2 * DB], U32, ctx)
        own, group, heads = self.own_mask, self.group_of, self.heads_of
        tmp = ExitStack()
        self.copies("gates_out", [(s["gates"], self.g_nsa[:DB, TP, :]), (s["w8"], self.w_idx[:DB, TP, :])])
        with tmp:
            pages_i = self.sb("pages_i", [P, DB * NPAGE], I32, tmp)
            iota_i = self.sb("iota32_i", [P, NPAGE], I32, tmp)
            page_of = self.sb("chunk_pages", [P, 2 * DB], I32, tmp)
            page_f = self.sb("chunk_page_f", [P, 2 * DB], F32, tmp)
            sub_i = self.sb("chunk_sub_i", [P, 1], I32, tmp)
            sub_f = self.sb("chunk_sub_f", [P, 1], F32, tmp)
            loaded, made, chain = self.sem("sc_loaded"), self.sem("sc_made"), self.sem("sc_chain")
            with nc.Block() as block:
                @block.sync
                def _(sp):
                    sp.dma_start(self.gate_bh[:], s["gates"].rearrange("b (h c) -> (b h) c", c=3)).then_inc(loaded, 16)
                    sp.dma_start(pages_i[:], bass.AP(i["page_table"].tensor, 0, [[0, P], [1, DB * NPAGE]])).then_inc(loaded, 16)
                    with nc.allow_non_contiguous_dma(reason="the table of pages"):
                        for q in range(16):
                            src = bass.AP(i["page_table"].tensor, q, [[0, 8], [16, 2 * DB]])
                            sp.dma_start(page_of[8 * q:8 * q + 8, :], src).then_inc(loaded, 16)

                @block.gpsimd
                def _(pool):
                    n = 0

                    def link(ins):
                        nonlocal n
                        n += 1
                        ins.then_inc(made, 1)
                        pool.wait_ge(made, n)

                    link(pool.iota(iota_i[:], pattern=[[1, NPAGE]], base=0, channel_multiplier=0))
                    link(pool.iota(self.part[:], pattern=[[0, 1]], base=0, channel_multiplier=1))
                    link(pool.memset(own[:], 0.0))
                    link(pool.affine_select(out=own[:], in_=own[:], compare_op=ALU.is_ge, fill=NEG, base=0, pattern=[[-HQ, DB]], channel_multiplier=1))
                    link(pool.affine_select(out=own[:], in_=own[:], compare_op=ALU.is_ge, fill=NEG, base=HQ - 1, pattern=[[HQ, DB]], channel_multiplier=-1))
                    link(pool.memset(group[:], 1.0))
                    link(pool.affine_select(out=group[:], in_=group[:], compare_op=ALU.is_ge, fill=0.0, base=0, pattern=[[-GRP, DB * KV]], channel_multiplier=1))
                    link(pool.affine_select(out=group[:], in_=group[:], compare_op=ALU.is_ge, fill=0.0, base=GRP - 1, pattern=[[GRP, DB * KV]], channel_multiplier=-1))
                    link(pool.memset(heads[:], 1.0))
                    link(pool.affine_select(out=heads[:], in_=heads[:], compare_op=ALU.is_ge, fill=0.0, base=0, pattern=[[1, DB * HQ]], channel_multiplier=-GRP))
                    link(pool.affine_select(out=heads[:], in_=heads[:], compare_op=ALU.is_ge, fill=0.0, base=GRP - 1, pattern=[[-1, DB * HQ]], channel_multiplier=GRP))

                @block.vector
                def _(dve):
                    c = Chain(dve, chain)
                    dve.wait_ge(loaded, 16 * 18)
                    dve.wait_ge(made, 2)
                    c.link(dve.tensor_copy(page_f[:], page_of[:]))
                    c.link(dve.tensor_scalar(sub_i[:], self.part[:], 7, None, ALU.bitwise_and))
                    c.link(dve.tensor_copy(sub_f[:], sub_i[:]))
                    c.link(dve.tensor_scalar(page_f[:], page_f[:], float(PAGE // STRIDE), sub_f[:, 0:1], ALU.mult, ALU.add))
                    c.link(dve.tensor_copy(self.row_of[:], page_f[:]))
                    c.link(dve.tensor_copy(self.pages_all[:].rearrange("p b n -> p (b n)"), pages_i[:]))
                    c.link(dve.tensor_copy(self.iota32[:], iota_i[:]))

    def attend_samples(self, tag, nk, q0, keys, values, waits=(), keys_t=None, bias_t=None, bias=None, own=None, own_bias=0, gate=None,
                       prob=None, add=False, out0=0):
        nc, ident, qs = self.nc, self.ident, self.qs_t
        BH = DB * HQ
        tiles = [(j, min(P, nk - P * j)) for j in range(-(-nk // P))]
        nt = len(tiles)
        nown = DB if own is not None else 0
        units = [(b, j, m) for b in range(DB) for j, m in tiles]
        ctx = ExitStack()
        with ctx:
            kt = self.sb(f"{tag}_kt", [DH, 2, KV, P], F32, ctx)
            lt = self.sb(f"{tag}_lt", [P, nt, DB, KV, GRP], F32, ctx)
            lown = self.sb(f"{tag}_lown", [DB, DB, HQ], F32, ctx)
            pr = self.sb(f"{tag}_p", [BH, nk + DB], F32, ctx)
            plain = prob
            pt = self.sb(f"{tag}_pt", [P, nt, DB, HQ], F32, ctx)
            pown = self.sb(f"{tag}_pown", [DB, DB, HQ], F32, ctx)
            mx = self.sb(f"{tag}_mx", [BH, 1], F32, ctx)
            sm = self.sb(f"{tag}_sm", [BH, 1], F32, ctx)
            kt_ps = self.ps(f"{tag}_kt_ps", [P, 2, 512], ctx)
            lt_ps = self.ps(f"{tag}_lt_ps", [P, KV, 512], ctx)
            l_ps = self.ps(f"{tag}_l_ps", [P, 2, 512], ctx)
            pt_ps = self.ps(f"{tag}_pt_ps", [P, 512], ctx)
            o_ps = self.ps(f"{tag}_o_ps", [P, 512], ctx)
            k_turned, k_out, scored, lt_out, l_turned, chain, soft_in, exp_done, prob_done, p_turned, p_out, mixed = (
                self.sem(f"{tag}_{n}") for n in ("k_turned", "k_out", "scored", "lt_out", "l_turned", "chain", "soft_in", "exp_done",
                                                 "prob_done", "p_turned", "p_out", "mixed"))
            ltv = lt_ps[:, :, :nt * DB * GRP].rearrange("p g (j b i) -> p g j b i", j=nt, b=DB)
            ptv = pt_ps[:, :nt * BH].rearrange("p (j c) -> p j c", j=nt)
            ov = o_ps[:, 0:4 * DB].rearrange("p (i b) -> p i b", b=DB)
            own_l, own_lt, own_p = o_ps[:DB, 64:64 + BH], o_ps[:BH, 128:128 + DB], o_ps[:DB, 192:192 + BH]

            with nc.Block() as block:
                @block.tensor
                def _(pe):
                    def turn(u):
                        b, j, m = units[u]
                        for sem, value in (waits(b) if waits else ()):
                            pe.wait_ge(sem, value)
                        if u >= 2:
                            pe.wait_ge(k_out, u - 1)
                        for g in range(KV):
                            last = pe.transpose(kt_ps[:DH, u % 2, P * g:P * g + m], keys(b, j, g), ident[:m, :m])
                        last.then_inc(k_turned, 1)

                    def score(u):
                        b, j, m = units[u]
                        if keys_t is None:
                            pe.wait_ge(k_out, u + 1)
                        for g in range(KV):
                            if keys_t is None:
                                lhs, q = kt[:, u % 2, g, :m], qs[:DH, q0 + GRP * g:q0 + GRP * g + GRP, b]
                            else:
                                lhs, q = keys_t(b, j, g), qs[DH * g:DH * g + DH, q0 + GRP * g:q0 + GRP * g + GRP, b]
                            last = pe.matmul(ltv[:m, g, j, b, :], lhs, q, start=True, stop=True)
                        last.then_inc(scored, 1)

                    if keys_t is None:
                        for u in range(len(units) + 1):
                            if u < len(units):
                                turn(u)
                            if u:
                                score(u - 1)
                    else:
                        for u in range(len(units)):
                            score(u)
                    if nown:
                        for g in range(KV):
                            q = qs[:DH, q0 + GRP * g:q0 + GRP * g + GRP, :].rearrange("p h b -> p b h")
                            dst = own_l.rearrange("p (b h) -> p b h", h=HQ)[:, :, GRP * g:GRP * g + GRP]
                            last = pe.matmul(dst, self.ks_t[:, KV * own + g, :], q, start=True, stop=True)
                        last.then_inc(scored, 1)
                    pe.wait_ge(lt_out, 1)
                    for j, m in tiles:
                        last = pe.transpose(l_ps[:BH, j // 4, P * (j % 4):P * (j % 4) + m], lt[:m, j].rearrange("p b g i -> p (b g i)"), ident[:m, :m])
                    if nown:
                        last = pe.transpose(own_lt, lown[:].rearrange("p b h -> p (b h)"), ident[:DB, :DB])
                    last.then_inc(l_turned, 1)
                    pe.wait_ge(prob_done, 1)
                    for j, m in tiles:
                        last = pe.transpose(ptv[:m, j, :], pr[:, P * j:P * j + m], ident[:BH, :BH])
                    if nown:
                        last = pe.transpose(own_p, pr[:, nk:nk + DB], ident[:BH, :BH])
                    last.then_inc(p_turned, 1)
                    pe.wait_ge(p_out, 1)
                    started = [False, False]
                    for par in range(2):
                        half = slice(DH * par, DH * par + DH)
                        for g in range(KV):
                            if nown:
                                rhs = pown[:, :, GRP * g + par:GRP * g + GRP:2].rearrange("p b i -> p i b")
                                last = pe.matmul(ov[half, 2 * g:2 * g + 2, :], self.vals[:DB, TP, own, g, :], rhs,
                                                 start=not started[par], stop=False, skip_group_check=True)
                                started[par] = True
                    for b, j, m in units:
                        for g in range(KV):
                            for par in range(2):
                                half = slice(DH * par, DH * par + DH)
                                last = pe.matmul(ov[half, 2 * g:2 * g + 2, b], values(b, j, g), pt[:m, j, b, GRP * g + par:GRP * g + GRP:2],
                                                 start=not started[par], stop=True, skip_group_check=True)
                                started[par] = True
                    last.then_inc(mixed, 1)

                @block.scalar
                def _(act):
                    if keys_t is None:
                        for u, (b, j, m) in enumerate(units):
                            act.wait_ge(k_turned, u + 1)
                            if u >= 2:
                                act.wait_ge(scored, u - 1)
                            act.copy(kt[:, u % 2, :, :m], kt_ps[:DH, u % 2, :KV * P].rearrange("p (g m) -> p g m", g=KV)[:, :, :m]).then_inc(k_out, 1)
                    act.wait_ge(soft_in, 1)
                    act.activation(pr[:, :nk + nown], pr[:, :nk + nown], ACT.Exp, bias=mx[:], accum_out=sm[:]).then_inc(exp_done, 1)

                @block.vector
                def _(dve):
                    c = Chain(dve, chain)
                    dve.wait_ge(scored, len(units) + (1 if nown else 0))
                    for j, m in tiles:
                        for g in range(KV):
                            if bias_t is None:
                                c.put(dve.tensor_copy(lt[:m, j, :, g, :], ltv[:m, g, j]))
                            else:
                                c.put(dve.tensor_tensor(lt[:m, j, :, g, :], ltv[:m, g, j], bias_t(j)[:, :, GRP * g:GRP * g + GRP], ALU.add))
                    if nown:
                        c.put(dve.tensor_copy(lown[:].rearrange("p b h -> p (b h)"), own_l))
                    c.need(c.n)
                    dve.sem_inc(lt_out, 1)
                    dve.wait_ge(l_turned, 1)
                    for a in range(-(-nk // 512)):
                        w = min(512, nk - 512 * a)
                        dst = pr[:, 512 * a:512 * a + w]
                        if bias is None:
                            c.put(dve.tensor_copy(dst, l_ps[:BH, a, :w]))
                        else:
                            c.put(dve.tensor_tensor(dst, l_ps[:BH, a, :w], bias[:, 512 * a:512 * a + w], ALU.add))
                    if nown:
                        c.put(dve.scalar_tensor_tensor(out=pr[:, nk:nk + DB], in0=own_lt, scalar=self.bias_self[:, own_bias:own_bias + 1],
                                                       in1=self.own_mask[:], op0=ALU.add, op1=ALU.add))
                    c.need(c.n)
                    c.link(dve.tensor_reduce(mx[:], pr[:, :nk + nown], AX, ALU.max))
                    dve.tensor_scalar(mx[:], mx[:], -1.0, None, ALU.mult).then_inc(soft_in, 1)
                    dve.wait_ge(exp_done, 1)
                    c.link(dve.reciprocal(sm[:], sm[:]))
                    if prob is not None:
                        c.link(dve.tensor_scalar(plain[:, :nk], pr[:, :nk], sm[:, 0:1], None, ALU.mult))
                    if gate is not None:
                        c.link(dve.tensor_tensor(sm[:], sm[:], gate, ALU.mult))
                    dve.tensor_scalar(pr[:, :nk + nown], pr[:, :nk + nown], sm[:, 0:1], None, ALU.mult).then_inc(prob_done, 1)
                    dve.wait_ge(p_turned, 1)
                    for j, m in tiles:
                        c.put(dve.tensor_copy(pt[:m, j].rearrange("p b h -> p (b h)"), ptv[:m, j, :]))
                    if nown:
                        c.put(dve.tensor_copy(pown[:].rearrange("p b h -> p (b h)"), own_p))
                    c.need(c.n)
                    dve.sem_inc(p_out, 1)
                    dve.wait_ge(mixed, 1)
                    o = self.oT[:, out0:out0 + 4, SEQ:]
                    if add:
                        c.link(dve.tensor_tensor(o, o, ov, ALU.add))
                    else:
                        c.link(dve.tensor_copy(o, ov))

    def sample_dsa(self):
        nc, i, s = self.nc, self.i, self.s
        ctx = ExitStack()
        with ctx:
            phys = self.sb("da_phys", [P, 2 * DB], U32, ctx)
            past_ix = self.sb("da_past_ix", [P, 2 * DB], U32, ctx)
            is_new = self.sb("da_is_new", [P, 2 * DB], F32, ctx)
            kv = self.sb("da_kv", [P, 2, DB, KV * 2 * DH], F32, ctx)
            bias = self.sb("da_bias", [P, 2, DB, 16], F32, ctx)
            own_bias = self.sb("da_own", [DB, 1], F32, ctx)
            self.pick_keys(phys, past_ix, is_new)
            self.gather("da_rows", [(kv[:, n // DB, n % DB, :], i["cache_a_kv"].rearrange("n p w -> (n p) w"), phys[:, n:n + 1]) for n in range(2 * DB)]
                        + [(bias[:, n // DB, n % DB, :], s["bias_pos"], past_ix[:, n:n + 1]) for n in range(2 * DB)])
            chain, was_new, old_self, new_self = (self.sem(f"da_{n}") for n in ("chain", "was_new", "old_self", "new_self"))
            ones = self.sb("da_ones", [P, DB * HQ], F32, ctx)
            hits = self.sb("da_hits", [DB * HQ, 2 * DB], F32, ctx)
            hit = self.sb("da_hit", [DB * HQ, DB], F32, ctx)
            own_saved = self.sb("da_own_saved", [DB * HQ, DB], F32, ctx)
            with nc.psum_tensor("da_h_ps", [P, 512], F32) as h_ps, nc.Block() as block:
                @block.vector
                def _(dve):
                    c = Chain(dve, chain)
                    c.link(dve.memset(ones[:], 1.0))
                    dve.sem_inc(was_new, 1)
                    c.link(dve.tensor_copy(own_saved[:], self.own_mask[:]))
                    flat = bias[:].rearrange("p j b h -> p (j b) h")
                    m = is_new[:].unsqueeze(2).to_broadcast([P, 2 * DB, 16])
                    c.link(dve.scalar_tensor_tensor(out=flat, in0=m, scalar=NEG, in1=flat, op0=ALU.mult, op1=ALU.add))
                    dve.wait_ge(new_self, 1)
                    c.link(dve.tensor_copy(hits[:], h_ps[:DB * HQ, :2 * DB]))
                    c.link(dve.tensor_tensor(hit[:], hits[:, 0:DB], hits[:, DB:2 * DB], ALU.add))
                    c.link(dve.tensor_scalar(hit[:], hit[:], -1.0, -NEG, ALU.add, ALU.mult))
                    c.link(dve.tensor_tensor(self.own_mask[:], self.own_mask[:], hit[:], ALU.add))

                @block.tensor
                def _(pe):
                    pe.wait_ge(was_new, 1)
                    pe.matmul(h_ps[:DB * HQ, :2 * DB], ones[:], is_new[:], start=True, stop=True).then_inc(new_self, 1)

            self.attend_samples("da_at", TOPA_S, 0, keys=lambda b, j, g: kv[:, j, b, 128 * g:128 * g + DH],
                                values=lambda b, j, g: kv[:, j, b, 128 * g + DH:128 * g + 128],
                                bias_t=lambda j: bias[:, j, :, 0:HQ], own=0, own_bias=0, out0=0)
            restored = self.sem("da_restored")
            with nc.Block() as block:
                @block.vector
                def _(dve):
                    dve.tensor_copy(self.own_mask[:], own_saved[:]).then_inc(restored, 1)

    def gather(self, tag, jobs, depth=8):
        sems = [self.sem(f"{tag}_in{n}") for n in range(min(depth, len(jobs)))]
        with self.nc.Block() as block:
            @block.gpsimd
            def _(pool):
                for n, (dst, table, rows) in enumerate(jobs):
                    pool.indirect_dma_start(out=dst, out_offset=None, in_=table,
                                            in_offset=bass.IndirectOffsetOnAxis(ap=rows, axis=0)).then_inc(sems[n % depth], 16)
                for n, sem in enumerate(sems):
                    pool.wait_ge(sem, 16 * len(range(n, len(jobs), depth)))

    def index_scores(self):
        nc, i, s, ident = self.nc, self.i, self.s, self.ident
        ctx = ExitStack()
        NU, NBUF = 2 * DB, 4
        with ctx:
            ch = self.sb("is_ch", [P, NBUF, STRIDE * DH], F32, ctx)
            kt = self.sb("is_kt", [P, 2, 8, P], F32, ctx)
            qb = self.sb("is_q", [P, DB, 2, IH], F32, ctx)
            w = self.sb("is_w", [P, DB, IH], F32, ctx)
            rl = self.sb("is_relu", [P, STRIDE, IH], F32, ctx)
            sc = self.sb("is_score", [P, NU, STRIDE], F32, ctx)
            tr = self.ps("is_tr", [P, 4, 512], ctx)
            sp_ = self.ps("is_sp", [P, 2, 512], ctx)
            ch_in = [self.sem(f"is_ch_in{n}") for n in range(NBUF)]
            w_in, q_done, turned, act_out, dve_out, scored, sum_done, chain, stored = (self.sem(f"is_{n}") for n in (
                "w_in", "q", "turned", "act_out", "dve_out", "scored", "sum", "chain", "stored"))
            with nc.Block() as block:
                @block.sync
                def _(sp):
                    sp.dma_start(w[:].rearrange("p b h -> p (b h)"), bass.AP(s["w8"].tensor, 0, [[0, P], [1, DB * IH]])).then_inc(w_in, 16)
                    sp.wait_ge(sum_done, NU)
                    sp.dma_start(s["score"].rearrange("b (h c t) -> c (b h) t", h=2, t=STRIDE), sc[:]).then_inc(stored, 16)
                    sp.wait_ge(stored, 16)

                @block.gpsimd
                def _(pool):
                    view = i["cache_a_kidx"].rearrange("n (c r) w -> (n c) (r w)", r=STRIDE)
                    for u in range(NU):
                        if u >= NBUF:
                            pool.wait_ge(turned, 2 * (u - NBUF + 1))
                        pool.indirect_dma_start(out=ch[:, u % NBUF, :], out_offset=None, in_=view,
                                                in_offset=bass.IndirectOffsetOnAxis(ap=self.row_of[:, u:u + 1], axis=0)).then_inc(ch_in[u % NBUF], 16)

                @block.tensor
                def _(pe):
                    def turn(u):
                        pe.wait_ge(ch_in[u % NBUF], 16 * (u // NBUF + 1))
                        for a in range(2):
                            bank = 2 * (u % 2) + a
                            if u >= 2:
                                pe.wait_ge((act_out, dve_out)[a], u - 1)
                            for k in range(4):
                                c0 = (4 * a + k) * P
                                last = pe.transpose(tr[:, bank, P * k:P * k + P], ch[:, u % NBUF, c0:c0 + P], ident[:])
                            last.then_inc(turned, 1)

                    def score(u):
                        pe.wait_ge(act_out, u + 1)
                        pe.wait_ge(dve_out, u + 1)
                        if u >= 2:
                            pe.wait_ge(sum_done, u - 1)
                        for k in range(8):
                            last = pe.matmul(sp_[:, u % 2, 8 * k:8 * k + 8], kt[:, u % 2, k, :], qb[:, u // 2].rearrange("p t h -> p (t h)"),
                                             start=True, stop=True)
                        last.then_inc(scored, 1)

                    pe.wait_ge(q_done, 3)
                    for u in range(NU + 1):
                        if u < NU:
                            turn(u)
                        if u:
                            score(u - 1)

                @block.scalar
                def _(act):
                    for u in range(NU):
                        act.wait_ge(turned, 2 * u + 1)
                        if u >= 2:
                            act.wait_ge(scored, u - 1)
                        act.copy(kt[:, u % 2, 0:4, :], tr[:, 2 * (u % 2), :].rearrange("p (k n) -> p k n", k=4)).then_inc(act_out, 1)

                @block.vector
                def _(dve):
                    c = Chain(dve, chain)
                    dve.memset(qb[:], 0.0).then_inc(q_done, 1)
                    dve.wait_ge(q_done, 1)
                    for t in range(2):
                        half = slice(DH * t, DH * t + DH)
                        dve.tensor_copy(qb[half, :, t, :], self.qi_t[half].rearrange("p h b -> p b h")).then_inc(q_done, 1)
                    dve.wait_ge(w_in, 16)

                    def total(u):
                        dve.wait_ge(scored, u + 1)
                        c.link(dve.scalar_tensor_tensor(out=rl[:], in0=sp_[:, u % 2, :STRIDE * IH].rearrange("p (t h) -> p t h", h=IH), scalar=0.0,
                                                        in1=w[:, u // 2, :].unsqueeze(1).to_broadcast([P, STRIDE, IH]), op0=ALU.max, op1=ALU.mult))
                        c.link(dve.tensor_reduce(sc[:, u, :], rl[:], AX, ALU.add))
                        dve.sem_inc(sum_done, 1)

                    for u in range(NU):
                        dve.wait_ge(turned, 2 * u + 2)
                        if u >= 2:
                            dve.wait_ge(scored, u - 1)
                        dve.tensor_copy(kt[:, u % 2, 4:8, :], tr[:, 2 * (u % 2) + 1, :].rearrange("p (k n) -> p k n", k=4)).then_inc(dve_out, 1)
                        if u:
                            total(u - 1)
                    total(NU - 1)

    def pick_keys(self, phys, past_ix, is_new):
        nc, ident = self.nc, self.ident
        ctx = ExitStack()
        NC = 2 * DB
        with ctx:
            ixf = self.sb("pi_ixf", [DB, TOPA_S], F32, ctx)
            t_f = self.sb("pi_t", [P, NC], F32, ctx)
            t_i = self.sb("pi_ti", [P, 3, NC], U32, ctx)
            page = self.sb("pi_page", [P, 2, NC], F32, ctx)
            hot = self.sb("pi_hot", [P, DB, NPAGE], F32, ctx)
            tr = self.ps("pi_tr", [P, 512], ctx)
            chain, ready, turned = self.sem("pi_chain"), self.sem("pi_ready"), self.sem("pi_turned")
            with nc.Block() as block:
                @block.vector
                def _(dve):
                    c = Chain(dve, chain)
                    c.link(dve.tensor_copy(ixf[:], self.best_ix[:]))
                    dve.sem_inc(ready, 1)
                    dve.wait_ge(turned, 1)
                    c.link(dve.tensor_copy(t_f[:], tr[:, :NC]))
                    c.link(dve.tensor_scalar(is_new[:], t_f[:], float(PAST), None, ALU.is_equal))
                    c.link(dve.tensor_scalar(t_f[:], t_f[:], float(PAST - 1), None, ALU.min))
                    c.link(dve.tensor_copy(past_ix[:], t_f[:]))
                    c.link(dve.tensor_scalar(t_i[:, 0], past_ix[:], 7, None, ALU.logical_shift_right))
                    c.link(dve.tensor_scalar(t_i[:, 1], past_ix[:], PAGE - 1, None, ALU.bitwise_and))
                    c.link(dve.tensor_copy(page[:], t_i[:, 0:2]))
                    full = [P, DB, NPAGE]
                    for j in range(2):
                        cols = slice(DB * j, DB * j + DB)
                        c.link(dve.tensor_tensor(hot[:], page[:, 0, cols].unsqueeze(2).to_broadcast(full),
                                                 self.iota32[:].unsqueeze(1).to_broadcast(full), ALU.is_equal))
                        c.link(dve.tensor_tensor(hot[:], hot[:], self.pages_all[:], ALU.mult))
                        c.link(dve.tensor_reduce(t_f[:, cols], hot[:], AX, ALU.add))
                    c.link(dve.scalar_tensor_tensor(out=t_f[:], in0=t_f[:], scalar=float(PAGE), in1=page[:, 1], op0=ALU.mult, op1=ALU.add))
                    c.link(dve.tensor_copy(phys[:], t_f[:]))

                @block.tensor
                def _(pe):
                    pe.wait_ge(ready, 1)
                    for j in range(2):
                        last = pe.transpose(tr[:, DB * j:DB * j + DB], ixf[:, P * j:P * j + P], ident[:DB, :DB])
                    last.then_inc(turned, 1)

    def sample_cmp_slc(self):
        nc, i, s = self.nc, self.i, self.s
        ctx = ExitStack()
        NSLOT, NG = NSEL, DB * KV
        with ctx:
            rows = self.sb("sl_rows", [P, NG * 8], U32, ctx)
            bias = self.sb("sl_bias", [DB * HQ, NSLOT * BLK], F32, ctx)
            bias_rows = self.sb("sl_bias_rows", [DB * HQ, NSLOT], U32, ctx)
            tmp = ExitStack()
            with tmp:
                prob = self.sb("cm_prob", [DB * HQ, NCH_S + DB], F32, tmp)
                self.attend_samples("cm_at", NCMP_S, HQ, keys=None, keys_t=lambda b, j, g: self.kc_t[DH * g:DH * g + DH, b, P * j:P * j + min(P, NCMP_S - P * j)],
                                    values=lambda b, j, g: self.vc[:min(P, NCMP_S - P * j), b, j, g, :], bias=self.bias_cmp, prob=prob, out0=4,
                                    gate=self.gate_bh[:, 0:1])
                self.pick_blocks(prob, rows, bias_rows)
            kv = self.sb("sl_kv", [P, NG, 8, 2 * DH], F32, ctx)
            self.gather("sl_gather", [(bias[:, BLK * n:BLK * n + BLK], s["bias_head"].rearrange("h (b t) -> (h b) t", t=BLK), bias_rows[:, n:n + 1])
                                      for n in range(NSLOT)]
                        + [(kv[:, n // 8, n % 8, :], i["cache_slc_kv"].rearrange("n p (g w) -> (n p g) w", g=KV), rows[:, n:n + 1]) for n in range(8 * NG)])
            dropped = self.sem("sl_dropped")
            with nc.Block() as block:
                @block.vector
                def _(dve):
                    dve.memset(bias[:, BLK * (NSLOT - 1):], NEG).then_inc(dropped, 1)
            self.attend_samples("sl_at", NSLOT * BLK, HQ, keys=lambda b, j, g: kv[:, KV * b + g, j, 0:DH], values=lambda b, j, g: kv[:, KV * b + g, j, DH:],
                                bias=bias, own=1, own_bias=1, gate=self.gate_bh[:, 1:2], add=True, out0=4)

    def pick_blocks(self, prob, rows, bias_rows):
        nc, s = self.nc, self.s
        BH, NG = DB * HQ, DB * KV
        ctx = ExitStack()
        with ctx:
            pad = self.sb("pb_pad", [BH, NCH_S + 1], F32, ctx)
            imp = self.sb("pb_imp", [BH, 2, NBLK], F32, ctx)
            work = self.sb("pb_work", [NG, NBLK], F32, ctx)
            best = self.sb("pb_best", [NG, 2, 8], F32, ctx)
            blk = self.sb("pb_blk", [NG, NSEL], U32, ctx)
            parts = self.sb("pb_parts", [NG, 2, NSEL], U32, ctx)
            pf = self.sb("pb_pf", [NG, 2, NSEL], F32, ctx)
            blkf = self.sb("pb_blkf", [NG, NSEL], F32, ctx)
            hot = self.sb("pb_hot", [NG, NSEL, NPAGE], F32, ctx)
            base = self.sb("pb_base", [NG, NSEL], F32, ctx)
            pages_i = self.sb("pb_pages_i", [NG, NPAGE], I32, ctx)
            pages = self.sb("pb_pages", [NG, NPAGE], F32, ctx)
            odd_i = self.sb("pb_odd_i", [P, 4], I32, ctx)
            odd = self.sb("pb_odd", [P, 4], F32, ctx)
            two = self.sb("pb_two", [2, P], F32, ctx)
            base2 = self.sb("pb_base2", [2, NG, 8], F32, ctx)
            g_ps = self.ps("pb_g_ps", [P, 512], ctx)
            r_ps = self.ps("pb_r_ps", [P, 512], ctx)
            b_ps = self.ps("pb_b_ps", [P, 512], ctx)
            chain, pages_in, imp_done, g_done, blk_done, b_done, base_done, stored, base_in, r_done, two_done = (self.sem(f"pb_{n}") for n in (
                "chain", "pages_in", "imp", "g", "blk", "b", "base", "stored", "base_in", "r", "two"))
            with nc.Block() as block:
                @block.sync
                def _(sp):
                    sp.dma_start(pages_i[:], bass.AP(self.i["page_table"].tensor, 0, [[NPAGE, DB], [0, KV], [1, NPAGE]])).then_inc(pages_in, 16)
                    sp.wait_ge(base_done, 1)
                    sp.dma_start(s["sel_base"], base[:]).then_inc(stored, 16)
                    sp.wait_ge(stored, 16)
                    with nc.allow_non_contiguous_dma(reason="256 words"):
                        sp.dma_start(base2[:], bass.AP(s["sel_base"].tensor, 0, [[1, 2], [NSEL, NG], [2, 8]])).then_inc(base_in, 16)

                @block.gpsimd
                def _(pool):
                    pool.memset(two[:], 1.0).then_inc(two_done, 1)
                    pool.wait_ge(two_done, 1)
                    pool.affine_select(out=two[:], in_=two[:], compare_op=ALU.is_ge, fill=0.0, base=0, pattern=[[1, P]], channel_multiplier=-BLK).then_inc(two_done, 1)
                    pool.wait_ge(two_done, 2)
                    pool.affine_select(out=two[:], in_=two[:], compare_op=ALU.is_ge, fill=0.0, base=BLK - 1, pattern=[[-1, P]], channel_multiplier=BLK).then_inc(two_done, 1)

                @block.tensor
                def _(pe):
                    pe.wait_ge(imp_done, 1)
                    pe.matmul(g_ps[:NG, :NBLK], self.group_of[:], imp[:, 0, :], start=True, stop=True).then_inc(g_done, 1)
                    pe.wait_ge(blk_done, 1)
                    pe.matmul(b_ps[:BH, :NSEL], self.heads_of[:], blkf[:], start=True, stop=True).then_inc(b_done, 1)
                    pe.wait_ge(base_in, 16)
                    pe.wait_ge(two_done, 3)
                    pe.matmul(r_ps[:, :8 * NG], two[:], base2[:].rearrange("f q k -> f (q k)"), start=True, stop=True).then_inc(r_done, 1)

                @block.vector
                def _(dve):
                    c = Chain(dve, chain)
                    c.link(dve.tensor_scalar(odd_i[:, 0:1], self.part[:], 1, None, ALU.bitwise_and))
                    c.link(dve.tensor_scalar(odd_i[:, 1:2], self.part[:], BLK - 1, None, ALU.bitwise_and))
                    c.link(dve.tensor_scalar(odd_i[:, 2:3], self.part[:], HQ - 1, None, ALU.bitwise_and))
                    c.link(dve.tensor_copy(odd[:, 0:3], odd_i[:, 0:3]))
                    c.link(dve.tensor_scalar(odd[:, 1:2], odd[:, 1:2], float(KV), None, ALU.mult))
                    c.link(dve.tensor_scalar(odd[:, 2:3], odd[:, 2:3], float(HQ), float(NBLK), ALU.add, ALU.mult))
                    c.link(dve.memset(pad[:], 0.0))
                    c.link(dve.tensor_copy(pad[:, 1:1 + NCMP_S], prob[:, :NCMP_S]))
                    for n in range(2):
                        c.link(dve.tensor_reduce(imp[:, n], pad[:, 1 - n:1 - n + NCH_S].rearrange("p (j m) -> p j m", m=BLK // STRIDE), AX, ALU.add))
                    c.link(dve.tensor_tensor(imp[:, 0], imp[:, 0], imp[:, 1], ALU.add))
                    dve.sem_inc(imp_done, 1)
                    dve.wait_ge(g_done, 1)
                    c.link(dve.tensor_copy(work[:], g_ps[:NG, :NBLK]))
                    c.link(dve.memset(work[:, 0:1], -NEG))
                    c.link(dve.memset(work[:, NBLK - 1:NBLK], -NEG))
                    c.link(dve.max(best[:, 0], work[:]))
                    c.link(dve.max_index(blk[:, 0:8], best[:, 0], work[:]))
                    c.link(dve.match_replace(work[:], best[:, 0], work[:], TAKEN))
                    c.link(dve.max(best[:, 1], work[:]))
                    c.link(dve.max_index(blk[:, 8:16], best[:, 1], work[:]))
                    c.link(dve.tensor_copy(blkf[:], blk[:]))
                    dve.sem_inc(blk_done, 1)
                    dve.wait_ge(b_done, 1)
                    c.link(dve.tensor_scalar(bias_rows[:], b_ps[:BH, :NSEL], odd[:BH, 2:3], None, ALU.add))
                    c.link(dve.tensor_scalar(parts[:, 0], blk[:], 1, None, ALU.logical_shift_right))
                    c.link(dve.tensor_scalar(parts[:, 1], blk[:], 1, None, ALU.bitwise_and))
                    c.link(dve.tensor_copy(pf[:], parts[:]))
                    dve.wait_ge(pages_in, 16)
                    c.link(dve.tensor_copy(pages[:], pages_i[:]))
                    full = [NG, NSEL, NPAGE]
                    c.link(dve.tensor_tensor(hot[:], pf[:, 0].unsqueeze(2).to_broadcast(full), self.iota32[:NG].unsqueeze(1).to_broadcast(full), ALU.is_equal))
                    c.link(dve.tensor_tensor(hot[:], hot[:], pages[:].unsqueeze(1).to_broadcast(full), ALU.mult))
                    c.link(dve.tensor_reduce(base[:], hot[:], AX, ALU.add))
                    c.link(dve.tensor_scalar(base[:], base[:], float(PAGE * KV), odd[:NG, 0:1], ALU.mult, ALU.add))
                    c.link(dve.scalar_tensor_tensor(out=base[:], in0=pf[:, 1], scalar=float(BLK * KV), in1=base[:], op0=ALU.mult, op1=ALU.add))
                    dve.sem_inc(base_done, 1)
                    dve.wait_ge(r_done, 1)
                    c.link(dve.tensor_scalar(rows[:], r_ps[:, :8 * NG], odd[:, 1:2], None, ALU.add))

    def sample_window(self):
        i = self.i
        ctx = ExitStack()
        with ctx:
            kv = self.sb("wi_kv", [P, DB, WIN // P, KV * 2 * DH], F32, ctx)
            self.copies("wi_rows", [(kv[:], i["cache_win_kv"].rearrange("b (j p) w -> p b j w", p=P))])
            self.attend_samples("wi_at", WIN, HQ, keys=lambda b, j, g: kv[:, b, j, 128 * g:128 * g + DH],
                                values=lambda b, j, g: kv[:, b, j, 128 * g + DH:128 * g + 128], bias=self.bias_win, own=2, own_bias=1,
                                gate=self.gate_bh[:, 2:3], add=True, out0=4)

    def sample_memory(self):
        nc, i, ident, ht = self.nc, self.i, self.ident, self.ht
        ctx = ExitStack()
        mt, BH = MEM // P, DB * HM
        units = [(b, j, h) for b in range(DB) for j in range(mt) for h in range(HM)]
        with ctx:
            kv = self.sb("me_kv", [P, DB, mt, HM * 2 * DHM], F32, ctx)
            kt = self.sb("me_kt", [P, 2, 4, P], F32, ctx)
            lt = self.sb("me_lt", [P, mt, DB, HM], F32, ctx)
            pr = self.sb("me_p", [BH, MEM], F32, ctx)
            pt = self.sb("me_pt", [P, mt, BH], F32, ctx)
            mx = self.sb("me_mx", [BH, 1], F32, ctx)
            sm = self.sb("me_sm", [BH, 1], F32, ctx)
            kt_ps = self.ps("me_kt_ps", [P, 2, 512], ctx)
            lt_ps = self.ps("me_lt_ps", [P, mt, DB, HM], ctx)
            l_ps = self.ps("me_l_ps", [P, 512], ctx)
            pt_ps = self.ps("me_pt_ps", [P, 512], ctx)
            o_ps = self.ps("me_o_ps", [P, 512], ctx)
            kv_in = [self.sem(f"me_kv_in{b}") for b in range(DB)]
            turned, out_done, scored, lt_out, l_turned, chain, soft_in, exp_done, prob_done, p_turned, p_out, mixed = (self.sem(f"me_{n}") for n in (
                "turned", "out", "scored", "lt_out", "l_turned", "chain", "soft_in", "exp", "prob", "p_turned", "p_out", "mixed"))
            ov = o_ps[:, :HM * DB].rearrange("p (h b) -> p h b", b=DB)
            with nc.Block() as block:
                @block.sync
                def _(sp):
                    for b in range(DB):
                        sp.dma_start(kv[:, b], i["cache_mem_kv"][b].rearrange("(j p) w -> p j w", p=P)).then_inc(kv_in[b], 16)

                @block.tensor
                def _(pe):
                    def turn(u):
                        b, j = u // mt, u % mt
                        pe.wait_ge(kv_in[b], 16)
                        if u >= 2:
                            pe.wait_ge(out_done, u - 1)
                        for h in range(HM):
                            last = pe.transpose(kt_ps[:, u % 2, P * h:P * h + P], kv[:, b, j, 2 * DHM * h:2 * DHM * h + DHM], ident[:])
                        last.then_inc(turned, 1)

                    def score(u):
                        b, j = u // mt, u % mt
                        pe.wait_ge(out_done, u + 1)
                        for h in range(HM):
                            last = pe.matmul(lt_ps[:, j, b, h:h + 1], kt[:, u % 2, h, :], ht[:, S_QM + h, SEQ + b:SEQ + b + 1], start=True, stop=True)
                        last.then_inc(scored, 1)

                    for u in range(DB * mt + 1):
                        if u < DB * mt:
                            turn(u)
                        if u:
                            score(u - 1)
                    pe.wait_ge(lt_out, 1)
                    for j in range(mt):
                        last = pe.transpose(l_ps[:BH, P * j:P * j + P], lt[:, j].rearrange("p b h -> p (b h)"), ident[:])
                    last.then_inc(l_turned, 1)
                    pe.wait_ge(prob_done, 1)
                    for j in range(mt):
                        last = pe.transpose(pt_ps[:, BH * j:BH * j + BH], pr[:, P * j:P * j + P], ident[:BH, :BH])
                    last.then_inc(p_turned, 1)
                    pe.wait_ge(p_out, 1)
                    for b in range(DB):
                        for h in range(HM):
                            for j in range(mt):
                                last = pe.matmul(ov[:, h, b:b + 1], kv[:, b, j, 2 * DHM * h + DHM:2 * DHM * (h + 1)], pt[:, j, HM * b + h:HM * b + h + 1],
                                                 start=(j == 0), stop=(j == mt - 1))
                    last.then_inc(mixed, 1)

                @block.scalar
                def _(act):
                    for u in range(DB * mt):
                        act.wait_ge(turned, u + 1)
                        if u >= 2:
                            act.wait_ge(scored, u - 1)
                        act.copy(kt[:, u % 2], kt_ps[:, u % 2, :].rearrange("p (h m) -> p h m", h=HM)).then_inc(out_done, 1)
                    act.wait_ge(soft_in, 1)
                    act.activation(pr[:], pr[:], ACT.Exp, bias=mx[:], scale=DHM ** -0.5, accum_out=sm[:]).then_inc(exp_done, 1)

                @block.vector
                def _(dve):
                    c = Chain(dve, chain)
                    dve.wait_ge(scored, DB * mt)
                    c.link(dve.tensor_copy(lt[:], lt_ps[:]))
                    dve.sem_inc(lt_out, 1)
                    dve.wait_ge(l_turned, 1)
                    c.link(dve.tensor_copy(pr[:], l_ps[:BH, :MEM]))
                    c.link(dve.tensor_reduce(mx[:], pr[:], AX, ALU.max))
                    dve.tensor_scalar(mx[:], mx[:], -DHM ** -0.5, None, ALU.mult).then_inc(soft_in, 1)
                    dve.wait_ge(exp_done, 1)
                    c.link(dve.reciprocal(sm[:], sm[:]))
                    dve.tensor_scalar(pr[:], pr[:], sm[:, 0:1], None, ALU.mult).then_inc(prob_done, 1)
                    dve.wait_ge(p_turned, 1)
                    c.link(dve.tensor_copy(pt[:].rearrange("p j c -> p (j c)"), pt_ps[:, :mt * BH]))
                    dve.sem_inc(p_out, 1)
                    dve.wait_ge(mixed, 1)
                    c.link(dve.tensor_copy(self.oT[:, 8:12, SEQ:], ov))

    def finish(self, xs):
        self.h = self.sb("h", [P, NT, D])
        tmp = ExitStack()
        with tmp:
            mixed = self.sb("mixed", [P, NT, D], F32, tmp)
            self.merge(mixed)
            x = self.sb("fin_x", [P, NT, D], F32, tmp)
            mixed_t = self.sb("mixed_t", [P, KD, NCOL], F32, tmp)
            self.copies("fin_x", [(x[:r, t, :], xs[t]) for t, r in enumerate(ROWS)])
            self.transposes("mixed", [(mixed_t[:, 4 * q:4 * q + 4, P * t:P * t + r], [mixed[:r, t, P * k:P * k + P] for k in range(4 * q, 4 * q + 4)])
                                      for t, r in enumerate(ROWS) for q in range(2)])
            self.linear("out", mixed_t, ROWS, self.i["w_out"], D, self.h, add=x)
        self.experts()

    def merge(self, mixed):
        nc, i, xT, oT = self.nc, self.i, self.xT, self.oT
        ctx = ExitStack()
        jobs = [(q, c) for q in range(2) for c in range(3)]
        units = [(j, t) for j in range(len(jobs)) for t in range(NT)]
        with ctx:
            wg = self.sb("mg_wg", [P, 2, KD, 512], F32, ctx)
            wb = self.sb("mg_wb", [P, 2, 4, 512], F32, ctx)
            sig = self.sb("mg_sig", [P, 2, 512], F32, ctx)
            prod = self.sb("mg_prod", [P, 512], F32, ctx)
            g_ps = self.ps("mg_g_ps", [P, 2, 512], ctx)
            u_ps = self.ps("mg_u_ps", [P, 2, 512], ctx)
            w_in = [self.sem(f"mg_w_in{n}") for n in range(2)]
            gate_mm, branch_mm, sig_done, sum_done, chain = (self.sem(f"mg_{n}") for n in ("gate_mm", "branch_mm", "sig", "sum", "chain"))
            with nc.Block() as block:
                @block.sync
                def _(sp):
                    for j, (q, c) in enumerate(jobs):
                        if j >= 2:
                            sp.wait_ge(branch_mm, (j - 1) * NT)
                        sp.dma_start(wg[:, j % 2], i["w_gate"][:, D * c + 512 * q:D * c + 512 * q + 512].rearrange("(k p) n -> p k n", p=P)).then_inc(w_in[j % 2], 16)
                        sp.dma_start(wb[:, j % 2], i["w_branch"][c, :, 512 * q:512 * q + 512].rearrange("(k p) n -> p k n", p=P)).then_inc(w_in[j % 2], 16)

                @block.tensor
                def _(pe):
                    for u, (j, t) in enumerate(units):
                        q, c = jobs[j]
                        r, cols = ROWS[t], slice(P * t, P * t + ROWS[t])
                        if t == 0:
                            pe.wait_ge(w_in[j % 2], 32 * (j // 2 + 1))
                        if u >= 2:
                            pe.wait_ge(sig_done, u - 1)
                        for k in range(KD):
                            last = pe.matmul(g_ps[:r, u % 2, :], xT[:, k, cols], wg[:, j % 2, k, :], start=(k == 0), stop=(k == KD - 1))
                        last.then_inc(gate_mm, 1)
                        if u >= 2:
                            pe.wait_ge(sum_done, u - 1)
                        for k in range(4):
                            last = pe.matmul(u_ps[:r, u % 2, :], oT[:, 4 * c + k, cols], wb[:, j % 2, k, :], start=(k == 0), stop=(k == 3))
                        last.then_inc(branch_mm, 1)

                @block.scalar
                def _(act):
                    for u, (j, t) in enumerate(units):
                        act.wait_ge(gate_mm, u + 1)
                        if u >= 2:
                            act.wait_ge(sum_done, u - 1)
                        act.activation(sig[:ROWS[t], u % 2, :], g_ps[:ROWS[t], u % 2, :], ACT.Sigmoid).then_inc(sig_done, 1)

                @block.vector
                def _(dve):
                    ch = Chain(dve, chain)
                    for u, (j, t) in enumerate(units):
                        q, c = jobs[j]
                        r = ROWS[t]
                        m = mixed[:r, t, 512 * q:512 * q + 512]
                        dve.wait_ge(sig_done, u + 1)
                        dve.wait_ge(branch_mm, u + 1)
                        if c == 0:
                            dve.tensor_tensor(m, sig[:r, u % 2, :], u_ps[:r, u % 2, :], ALU.mult).then_inc(sum_done, 1)
                        else:
                            if u:
                                dve.wait_ge(sum_done, u)
                            ch.link(dve.tensor_tensor(prod[:r, :], sig[:r, u % 2, :], u_ps[:r, u % 2, :], ALU.mult))
                            dve.tensor_tensor(m, m, prod[:r, :], ALU.add).then_inc(sum_done, 1)

    def experts(self):
        i = self.i
        self.e_idx = self.sb("e_idx", [P, NT, HP * PTOP], U32)
        self.e_gate = self.sb("e_gate", [P, NT, HP * PTOP])
        xf = self.xf = self.sb("xf", [P, NT, D])
        self.e_xf8 = self.sb("e_xf8", [P, D])
        self.e_idx8 = self.sb("e_idx8", [P, HP], U32)
        self.e_gate8 = self.sb("e_gate8", [P, HP])
        ctx = ExitStack()
        with ctx:
            q_t = self.xT
            tmp = ExitStack()
            with tmp:
                xf_t = self.sb("xf_t", [P, KD, NCOL], F32, tmp)
                self.norm_rows("ffn", self.h, i["ln_ffn"], ROWS, xf_t, keep=xf)
                q = self.sb("pq", [P, NT, D], F32, tmp)
                self.linear("pq", xf_t, ROWS, i["w_pq"], D, q)
                self.transposes("pq", [(q_t[:, 4 * a:4 * a + 4, P * t:P * t + r], [q[:r, t, P * k:P * k + P] for k in range(4 * a, 4 * a + 4)])
                                       for t, r in enumerate(ROWS) for a in range(2)])
            self.recycle()
            self.retrieval(q_t, ctx)
            self.spread_samples()
            self.mix_experts()

    def retrieval(self, q_t, ctx):
        nc, i, ident = self.nc, self.i, self.ident
        HK = 2 * HP
        turns = self.turns = [TP] + list(range(TP))
        self.pk_keys_t = keys_t = self.sb("sk_t", [P, NKEY], F32, ctx)
        iota_f = self.sb("pk_iota_f", [P, PTOP], F32, ctx)
        sc = self.sb("pk_score", [P, HK, NKEY], F32, ctx)
        v = self.sb("pk_v", [P, HK, PTOP], F32, ctx)
        ix = self.sb("pk_i", [P, HK, PTOP], U32, ctx)
        ixf = self.sb("pk_if", [P, HK, PTOP], F32, ctx)
        cand = self.sb("pk_cand", [P, HP, PTOP, PTOP], F32, ctx)
        fv = self.sb("pk_fv", [P, HP, PTOP], F32, ctx)
        fp = self.sb("pk_fp", [P, HP, PTOP], U32, ctx)
        fa = self.sb("pk_fa", [P, 2, HP, PTOP], U32, ctx)
        faf = self.sb("pk_faf", [P, 2, HP, PTOP], F32, ctx)
        hot = self.sb("pk_hot", [P, HP, PTOP, PTOP], F32, ctx)
        sel = self.sb("pk_sel", [P, 2, HP, PTOP], F32, ctx)
        ss = self.sb("pk_sum", [P, HP], F32, ctx)
        s_ps = self.ps("pk_s_ps", [P, 4, 4, NKEY], ctx)
        mm, out_done, taken, idx_done, tile_done, chain, diff_done, exp_done = (self.sem(f"pk_{n}") for n in (
            "mm", "out", "taken", "idx", "tile", "chain", "diff", "exp"))
        self.pk_idx_done = idx_done
        c = Chain(None, chain)

        def scores(pe, n):
            t = turns[n]
            r = ROWS[t]
            for a in range(2):
                if n:
                    pe.wait_ge(out_done, 4 * (n - 1) + 2 * a + 2)
                for b in range(4):
                    for p in range(2):
                        half = slice(DH * p, DH * p + DH)
                        last = pe.matmul(s_ps[:r, 2 * a + p, b, :], q_t[half, 4 * a + b, P * t:P * t + r], keys_t[half, :],
                                         start=True, stop=True)
                        if b == 3:
                            last.then_inc(mm, 1)

        def keep(act, n):
            r = ROWS[turns[n]]
            if n:
                act.wait_ge(taken, n)
            for a in range(4):
                act.wait_ge(mm, 4 * n + a + 1)
                h0, p = 4 * (a // 2), a % 2
                act.copy(sc[:r, 2 * h0 + p:2 * h0 + 8:2, :], s_ps[:r, a]).then_inc(out_done, 1)

        def soft(act, n):
            r = ROWS[turns[n]]
            act.wait_ge(diff_done, n + 1)
            act.activation(fv[:r], fv[:r], ACT.Exp).then_inc(exp_done, 1)

        def pick(dve, n):
            t = turns[n]
            r = ROWS[t]
            c.eng = dve

            def top16(m, src, vals, idx):
                at = []
                for k in range(m):
                    at.append(c.put(dve.max(vals[:r, k, 0:8], src(k))))
                    yield
                for k in range(m):
                    c.need(at[k])
                    at[k] = c.put(dve.max_index(idx[:r, k, 0:8], vals[:r, k, 0:8], src(k)))
                    yield
                for k in range(m):
                    c.need(at[k])
                    at[k] = c.put(dve.match_replace(src(k), vals[:r, k, 0:8], src(k), NEG))
                    yield
                for k in range(m):
                    c.need(at[k])
                    at[k] = c.put(dve.max(vals[:r, k, 8:16], src(k)))
                    yield
                for k in range(m):
                    c.need(at[k])
                    at[k] = c.put(dve.max_index(idx[:r, k, 8:16], vals[:r, k, 8:16], src(k)))
                    yield
                c.need(at[m - 1])

            dve.wait_ge(out_done, 4 * n + 4)
            yield from top16(HK, lambda k: sc[:r, k, :], v, ix)
            dve.sem_inc(taken, 1)
            c.link(dve.tensor_copy(ixf[:r], ix[:r]))
            yield
            v2 = v[:r].rearrange("p (h s) k -> p h s k", s=2)
            i2 = ixf[:r].rearrange("p (h s) k -> p h s k", s=2)
            full = [r, HP, PTOP, PTOP]
            c.link(dve.tensor_tensor(cand[:r], v2[:, :, 0, :].unsqueeze(3).to_broadcast(full),
                                     v2[:, :, 1, :].unsqueeze(2).to_broadcast(full), ALU.add))
            yield
            yield from top16(HP, lambda k: cand[:r, k].rearrange("p a b -> p (a b)"), fv, fp)
            c.link(dve.tensor_scalar(fa[:r, 0], fp[:r], 4, None, ALU.logical_shift_right))
            c.link(dve.tensor_scalar(fa[:r, 1], fp[:r], 15, None, ALU.bitwise_and))
            c.link(dve.tensor_copy(faf[:r], fa[:r]))
            yield
            for a in range(2):
                c.link(dve.tensor_tensor(hot[:r], faf[:r, a].unsqueeze(3).to_broadcast(full),
                                         iota_f[:r].unsqueeze(1).unsqueeze(1).to_broadcast(full), ALU.is_equal))
                yield
                c.link(dve.tensor_tensor(hot[:r], hot[:r], i2[:, :, a, :].unsqueeze(2).to_broadcast(full), ALU.mult))
                yield
                c.link(dve.tensor_reduce(sel[:r, a], hot[:r], AX, ALU.add))
                yield
            flat = lambda x: x.rearrange("p h k -> p (h k)")
            c.link(dve.scalar_tensor_tensor(out=flat(sel[:r, 0]), in0=flat(sel[:r, 0]), scalar=float(NKEY), in1=flat(sel[:r, 1]),
                                            op0=ALU.mult, op1=ALU.add))
            dve.tensor_copy(self.e_idx[:r, t, :], flat(sel[:r, 0])).then_inc(idx_done, 1)
            c.link(dve.tensor_copy(ss[:r], fv[:r, :, 0]))
            dve.tensor_tensor(fv[:r], fv[:r], ss[:r].unsqueeze(2).to_broadcast([r, HP, PTOP]), ALU.subtract).then_inc(diff_done, 1)
            yield

        def gate(dve, n):
            t = turns[n]
            r = ROWS[t]
            c.eng = dve
            dve.wait_ge(exp_done, n + 1)
            c.link(dve.tensor_reduce(ss[:r], fv[:r], AX, ALU.add))
            c.link(dve.reciprocal(ss[:r], ss[:r]))
            dve.tensor_tensor(self.e_gate[:r, t, :].rearrange("p (h k) -> p h k", h=HP), fv[:r],
                              ss[:r].unsqueeze(2).to_broadcast([r, HP, PTOP]), ALU.mult).then_inc(tile_done, 1)
            dve.wait_ge(tile_done, n + 1)

        self.pk_scores, self.pk_keep, self.pk_soft, self.pk_pick, self.pk_gate = scores, keep, soft, pick, gate
        tmp = ExitStack()
        with tmp:
            rows = self.sb("sk_rows", [NKEY, 2, DH], F32, tmp)
            iota_i = self.sb("pk_iota_i", [P, PTOP], I32, tmp)
            k_ps = self.ps("pk_k_ps", [P, P], tmp)
            keys_in, keys_mm, keys_done, iota_done = (self.sem(f"pk_{n}") for n in ("keys_in", "keys_mm", "keys_done", "iota"))
            with nc.Block() as block:
                @block.sync
                def _(sp):
                    sp.dma_start(rows[:], i["sub_keys"].rearrange("p k d -> k p d")).then_inc(keys_in, 16)

                @block.gpsimd
                def _(pool):
                    pool.iota(iota_i[:], pattern=[[1, PTOP]], base=0, channel_multiplier=0).then_inc(iota_done, 1)

                @block.tensor
                def _(pe):
                    pe.wait_ge(keys_in, 16)
                    pe.transpose(k_ps[:], rows[:].rearrange("k p d -> k (p d)"), ident[:]).then_inc(keys_mm, 1)
                    pe.wait_ge(keys_done, 1)
                    for n in range(2):
                        scores(pe, n)

                @block.scalar
                def _(act):
                    act.wait_ge(keys_mm, 1)
                    act.copy(keys_t[:], k_ps[:]).then_inc(keys_done, 1)
                    for n in range(2):
                        keep(act, n)
                        soft(act, n)

                @block.vector
                def _(dve):
                    c.eng = dve
                    dve.wait_ge(iota_done, 1)
                    c.link(dve.tensor_copy(iota_f[:], iota_i[:]))
                    for n in range(2):
                        for _ in pick(dve, n):
                            pass
                        gate(dve, n)

    def spread_samples(self):
        s = self.s
        self.copies("spread_out", [(s["x8"], self.xf[:DB, TP, :]), (s["gate8"], self.e_gate[:DB, TP, :]), (s["idx8"], self.e_idx[:DB, TP, :])])
        pairs = []
        for k in range(PTOP):
            at = slice(DB * k, DB * k + DB)
            pairs.append((self.e_xf8[at, :], s["x8"]))
            pairs.append((self.e_gate8[at, :], bass.AP(s["gate8"].tensor, k, [[P, DB], [PTOP, HP]])))
            pairs.append((self.e_idx8[at, :], bass.AP(s["idx8"].tensor, k, [[P, DB], [PTOP, HP]])))
        self.copies("spread_in", pairs)

    def mix_experts(self):
        nc, i, o, ident = self.nc, self.i, self.o, self.ident
        NBUF = 8
        PACE = 3
        ctx = ExitStack()
        slots = [HP * PTOP] * TP + [HP]
        first = [HP * PTOP * t for t in range(NT + 1)]
        total = first[TP] + HP
        with ctx:
            ub = self.sb("ex_u", [P, NBUF, D], F32, ctx)
            vb = self.sb("ex_v", [P, NBUF, D], F32, ctx)
            dots = self.sb("ex_dots", [P, NT, HP * PTOP], F32, ctx)
            coef = self.sb("ex_coef", [P, NT, HP * PTOP], F32, ctx)
            diag = self.sb("ex_diag", [P, 4, P], F32, ctx)
            same = self.sb("ex_same", [P, DB], F32, ctx)
            y = self.sb("ex_y", [P, 2, D], F32, ctx)
            y_ps = self.ps("ex_y_ps", [P, 2, 2, 512], ctx)
            u_in = [self.sem(f"ex_u_in{n}") for n in range(NBUF)]
            v_in = [self.sem(f"ex_v_in{n}") for n in range(NBUF)]
            stored = [self.stores("y_even"), self.stores("y_odd")]
            dot_done, gelu_done, coef_done, diag_done, mix_done, y_done, same_done = (self.sem(f"ex_{n}") for n in (
                "dot", "gelu", "coef", "diag", "mix", "y", "same"))

            def steps(k):
                nu = slots[k] if k < NT else 0
                nv = slots[k - 1] if k else 0
                return [(s if s < nu else None, s if s < nv else None) for s in range(max(nu, nv))]

            def index(t, s):
                return self.e_idx8[:, s:s + 1] if t == TP else self.e_idx[:, t, s:s + 1]

            with nc.Block() as block:
                @block.gpsimd
                def _(pool):
                    pool.memset(same[:], 0.0).then_inc(same_done, 1)
                    pool.wait_ge(same_done, 1)
                    for n in range(P // DB):
                        pool.wait_ge(same_done, n + 1)
                        pool.affine_select(out=same[:], in_=same[:], compare_op=ALU.not_equal, fill=1.0, base=-DB * n,
                                           pattern=[[-1, DB]], channel_multiplier=1).then_inc(same_done, 1)
                    for k in range(NT + 1):
                        if 1 <= k < TP:
                            pool.wait_ge(self.pk_idx_done, k + 2)
                        for su, sv in steps(k):
                            if su is not None:
                                n = first[k] + su
                                if n >= NBUF:
                                    pool.wait_ge(dot_done, n - NBUF + 1)
                                pool.indirect_dma_start(out=ub[:, n % NBUF, :], out_offset=None, in_=i["u_tab"],
                                                        in_offset=bass.IndirectOffsetOnAxis(ap=index(k, su), axis=0)).then_inc(u_in[n % NBUF], 16)
                            if sv is not None:
                                n = first[k - 1] + sv
                                if n >= NBUF:
                                    pool.wait_ge(mix_done, n - NBUF + 1)
                                pool.indirect_dma_start(out=vb[:, n % NBUF, :], out_offset=None, in_=i["v_tab"],
                                                        in_offset=bass.IndirectOffsetOnAxis(ap=index(k - 1, sv), axis=0)).then_inc(v_in[n % NBUF], 16)

                @block.vector
                def _(dve):
                    for k in range(NT + 1):
                        if k < NT:
                            x = self.e_xf8[:] if k == TP else self.xf[:, k, :]
                            picks = self.pk_pick(dve, k + 2) if k + 1 < TP else iter(())
                            for s in range(slots[k]):
                                n = first[k] + s
                                b = ub[:, n % NBUF, :]
                                dve.wait_ge(u_in[n % NBUF], 16 * (n // NBUF + 1))
                                dve.tensor_tensor_reduce(out=b, in0=b, in1=x, scale=1.0, scalar=0.0, op0=ALU.mult, op1=ALU.add,
                                                         accum_out=dots[:, k, s:s + 1]).then_inc(dot_done, 1)
                                for _ in range(PACE):
                                    next(picks, None)
                            for _ in picks:
                                pass
                            if k + 1 < TP:
                                self.pk_gate(dve, k + 2)
                            dve.wait_ge(gelu_done, k + 1)
                            g = self.e_gate8[:] if k == TP else self.e_gate[:, k, :]
                            dve.tensor_tensor(coef[:, k, :slots[k]], coef[:, k, :slots[k]], g, ALU.mult).then_inc(coef_done, 1)
                        if k:
                            t, r = k - 1, ROWS[k - 1]
                            dve.wait_ge(mix_done, first[t] + slots[t])
                            if t >= 2:
                                dve.wait_ge(stored[t % 2], 16 * (t // 2))
                            for q in range(2):
                                dve.tensor_tensor(y[:r, t % 2, 512 * q:512 * q + 512], y_ps[:r, t % 2, q, :],
                                                  self.h[:r, t, 512 * q:512 * q + 512], ALU.add).then_inc(y_done, 1)

                @block.scalar
                def _(act):
                    for k in range(NT + 1):
                        if k + 1 < TP:
                            self.pk_keep(act, k + 2)
                        if k:
                            t = k - 1
                            act.wait_ge(coef_done, k)
                            for s in range(slots[t]):
                                n = first[t] + s
                                if n >= 4:
                                    act.wait_ge(mix_done, n - 3)
                                if t == TP:
                                    act.wait_ge(same_done, P // DB + 1)
                                src, w = (same, DB) if t == TP else (ident, P)
                                act.activation(diag[:, n % 4, :w], src[:], ACT.Copy, scale=coef[:, t, s:s + 1]).then_inc(diag_done, 1)
                        if k + 1 < TP:
                            self.pk_soft(act, k + 2)
                        if k < NT:
                            act.wait_ge(dot_done, first[k] + slots[k])
                            act.activation(coef[:, k, :slots[k]], dots[:, k, :slots[k]], ACT.Gelu_apprx_tanh).then_inc(gelu_done, 1)

                @block.tensor
                def _(pe):
                    self.pk_scores(pe, 2)
                    for t, r in enumerate(ROWS):
                        if t + 2 < TP:
                            self.pk_scores(pe, t + 3)
                        if t >= 2:
                            pe.wait_ge(y_done, 2 * (t - 1))
                        for s in range(slots[t]):
                            n = first[t] + s
                            pe.wait_ge(diag_done, n + 1)
                            pe.wait_ge(v_in[n % NBUF], 16 * (n // NBUF + 1))
                            for q in range(2):
                                last = pe.matmul(y_ps[:r, t % 2, q, :], diag[:, n % 4, :r], vb[:, n % NBUF, 512 * q:512 * q + 512],
                                                 start=(s == 0), stop=(s == slots[t] - 1))
                            last.then_inc(mix_done, 1)

                @block.sync
                def _(sp):
                    for t, r in enumerate(ROWS):
                        sp.wait_ge(y_done, 2 * (t + 1))
                        dst = o["y_sample"][:, 0, :] if t == TP else o["y_prompt"][0, P * t:P * t + P, :]
                        sp.dma_start(dst, y[:r, t % 2, :]).then_inc(stored[t % 2], 16)
                    sp.wait_ge(stored[0], 16 * (TP // 2 + 1))
                    sp.wait_ge(stored[1], 16 * (TP // 2))


_INS = ["x_prompt", "x_sample", "mem_prompt", "cache_a_kv", "cache_a_kidx", "cache_cmp_kv", "cache_slc_kv", "cache_win_kv",
        "cache_mem_kv", "page_table", "ln_mix", "w_in", "g_qa", "g_ka", "g_qb", "g_kcmp", "g_kslc", "g_kwin", "g_qm", "g_km",
        "rel_table", "w_cmp1", "w_cmp2", "cmp_pe", "ln_mem", "w_mem_kv", "w_gate", "w_branch", "w_out", "ln_ffn", "w_pq",
        "sub_keys", "u_tab", "v_tab"]
_OUTS = [("y_prompt", (1, SEQ, D)), ("y_sample", (DB, 1, D)),
         ("a_kv_p", (1, SEQ, KV * 2 * DH)), ("a_kidx_p", (1, SEQ, DH)), ("cmp_kv_p", (1, SEQ, KV * 2 * DH)),
         ("slc_kv_p", (1, SEQ, KV * 2 * DH)), ("win_kv_p", (1, WIN, KV * 2 * DH)), ("mem_kv_p", (1, MEM, HM * 2 * DHM)),
         ("a_kv_s", (DB, 1, KV * 2 * DH)), ("a_kidx_s", (DB, 1, DH)), ("cmp_kv_s", (DB, 1, KV * 2 * DH)),
         ("slc_kv_s", (DB, 1, KV * 2 * DH)), ("win_kv_s", (DB, WIN, KV * 2 * DH))]
_FULL = {"a_kv": (KV, 2, DH), "a_kidx": (DH,), "cmp_kv": (KV, 2, DH), "slc_kv": (KV, 2, DH), "win_kv": (KV, 2, DH), "mem_kv": (HM, 2, DHM)}
_FLAT = {"cache_a_kv": 3, "cache_cmp_kv": 3, "cache_slc_kv": 3, "cache_win_kv": 3, "cache_mem_kv": 3}
_SCRATCH = [("bias_rev", (16, 640)), ("bias_pos", (PAST + P, 16)), ("gates", (DB, 24)), ("score", (DB, PAST)),
            ("sel_base", (16, 16)), ("self_logit", (3, DB, HQ)), ("bias_head", (16, PAST)), ("w8", (DB, IH)), ("x8", (DB, D)), ("gate8", (DB, P)), ("idx8", (DB, P))]


def kernel(**inputs):
    import numpy as _np
    import concourse.bacc as _bacc
    from concourse import mybir as _mybir
    from concourse.bass_utils import run_bass_kernel_spmd as _run

    nc = _bacc.Bacc("TRN2", target_bir_lowering=False, num_devices=1)
    arrays, ins, outs, scratch = {}, {}, {}, {}
    for name in _INS:
        a = _np.ascontiguousarray(inputs[name])
        if name in _FLAT:
            a = a.reshape(a.shape[:2] + (-1,))
        arrays[f"in_{name}"] = a
        ins[name] = nc.dram_tensor(f"in_{name}", a.shape, _mybir.dt.from_np(a.dtype), kind="ExternalInput").ap()
    ins["bounds"] = nc.inline_tensor(bucket_bounds(), "bucket_bounds").ap()
    for name, shape in _OUTS:
        outs[name] = nc.dram_tensor(f"out_{name}", shape, _mybir.dt.float32, kind="ExternalOutput").ap()
    for name, shape in _SCRATCH:
        scratch[name] = nc.dram_tensor(f"tmp_{name}", shape, _mybir.dt.uint32 if name.startswith("idx") else _mybir.dt.float32).ap()
    Kernel(nc, ins, outs, scratch).build()
    r = _run(nc, [arrays], core_ids=[0])
    got = []
    for name, shape in _OUTS:
        a = r.results[0][f"out_{name}"]
        tail = _FULL.get(name[:-2])
        got.append(a.reshape(shape[:2] + tail) if tail else a)
    return tuple(got)
```

```python
import math
from contextlib import ExitStack, contextmanager

import numpy as np

import concourse.bass as bass
from concourse import mybir

F32 = mybir.dt.float32
U32 = mybir.dt.uint32
I32 = mybir.dt.int32
ALU = mybir.AluOpType
ACT = mybir.ActivationFunctionType
AX = mybir.AxisListType.X

P = 128
D = 1024
KD = D // P
SEQ, DB, PAST, PAGE = 512, 8, 4096, 128
NPAGE = PAST // PAGE
TP = SEQ // P
NT = TP + 1
ROWS = [P] * TP + [DB]
NCOL = SEQ + DB
DH, HQ, KV, GRP = 64, 8, 2, 4
IH, TOPA_P, TOPA_S = 4, 128, 256
STRIDE, HID = 16, 64
NCH_S, NCH_P = PAST // STRIDE, SEQ // STRIDE
NCMP_S, NCMP_P = NCH_S - 1, NCH_P - 1
BLK, NBLK, NSEL = 64, PAST // 64, 16
WIN, MEM, HM, DHM = 512, 256, 4, 128
NB = 32
HP, NKEY, PTOP = 8, 128, 16
EPS = 1e-6
NEG = -1e30
TAKEN = -2e30

Q_A, KV_A, Q_I, W_I, K_I = 0, 512, 768, 1024, 1028
Q_B, KV_C, KV_S, KV_W, G_N, Q_M, IN_W = 1092, 1604, 1860, 2116, 2372, 2396, 2908
S_QA, S_QB, S_QM, S_KA, S_KS, S_KW, S_KI, S_QI, N_SLOT = 0, 4, 8, 12, 14, 16, 18, 19, 21


def bucket_bounds():
    n = np.arange(PAST + 1)
    nf = np.maximum(n, 1).astype(np.float32)
    half = NB // 2
    big = half + (np.log(nf / np.float32(half)) / np.float32(math.log(128 / half)) * np.float32(NB - half)).astype(np.int32)
    b = np.where(n < half, n, np.minimum(big, NB - 1))
    lo = np.array([n[b == i].min() for i in range(NB)], np.float32)
    hi = np.array([n[b == i].max() + 1 for i in range(NB)], np.float32)
    return np.ascontiguousarray(np.stack([lo, hi], 1))


class Chain:

    def __init__(self, eng, sem):
        self.eng, self.sem, self.n = eng, sem, 0

    def put(self, ins):
        self.n += 1
        ins.then_inc(self.sem, 1)
        return self.n

    def need(self, count):
        self.eng.wait_ge(self.sem, count)

    def link(self, ins):
        self.need(self.put(ins))


RETRIEVE_NEXT, RETRIEVE_LAST, COMPRESS, ATTEND, MEMORY = 125, 40, 140, 30, 80
ENGINES = ("tensor", "vector", "scalar", "gpsimd", "sync")


class Stage:

    def __init__(self, block):
        for name in ENGINES:
            self.add(name, block)

    def add(self, name, block):
        take = {"tensor": block.tensor, "vector": block.vector, "scalar": block.scalar, "gpsimd": block.gpsimd, "sync": block.sync}[name]

        def program(f):
            @take
            def _(eng):
                for _ in f(eng) or ():
                    pass

        if name == "tensor":
            self.tensor = program
        elif name == "vector":
            self.vector = program
        elif name == "scalar":
            self.scalar = program
        elif name == "gpsimd":
            self.gpsimd = program
        else:
            self.sync = program


class Beside:

    def __init__(self, ended):
        self.ended, self.stages, self.before = ended, {name: [] for name in ENGINES}, 0
        self.now = {name: None for name in ENGINES}
        self.next_step = 0

    def stage(self, first, last):
        return SideStage(self, first, last)

    def advance(self, name, eng, step):
        while True:
            if self.now[name] is None:
                if not self.stages[name] or self.stages[name][0][1] > step:
                    return
                before, first, last, program = self.stages[name].pop(0)
                if before:
                    eng.wait_ge(self.ended, before)
                self.now[name] = [program(eng) or iter(()), 0.0, first, last]
            work, at, first, last = self.now[name]
            if first + at * (last - first) > step:
                return
            at = next(work, None)
            if at is None:
                self.now[name] = None
                if name != "gpsimd":
                    eng.drain()
                eng.sem_inc(self.ended, 1)
            else:
                self.now[name][1] = at


class SideStage:
    def __init__(self, beside, first, last):
        self.beside, self.first, self.last, self.taken = beside, first, last, 0

    def put(self, name, program):
        b = self.beside
        b.stages[name].append((b.before, self.first, self.last, program))
        self.taken += 1

    def tensor(self, f):
        self.put("tensor", f)

    def vector(self, f):
        self.put("vector", f)

    def scalar(self, f):
        self.put("scalar", f)

    def gpsimd(self, f):
        self.put("gpsimd", f)

    def sync(self, f):
        self.put("sync", f)

    def __enter__(self):
        return self

    def __exit__(self, *error):
        self.beside.before += self.taken


class Kernel:
    def __init__(self, nc, ins, outs, scratch):
        self.nc, self.i, self.o, self.s = nc, ins, outs, scratch
        self.beside = None
        self.ctx = ExitStack()
        self.live = []

    def sem(self, name):
        self.live.append(self.nc.alloc_semaphore(name=name))
        return self.live[-1]

    def stores(self, name):
        return self.store_sems[name]

    @contextmanager
    def block(self, steps=1):
        if self.beside is None:
            with self.nc.Block() as block:
                yield Stage(block)
        else:
            first = self.beside.next_step
            self.beside.next_step += steps
            with self.beside.stage(first, first + steps) as stage:
                yield stage

    def recycle(self):
        if self.beside is not None:
            return
        self.nc.clear_and_free_semaphores(self.live)
        self.live = []
        self.nc.all_engine_barrier()

    def sb(self, name, shape, dt=F32, ctx=None):
        return (ctx or self.ctx).enter_context(self.nc.sbuf_tensor(name, shape, dt))

    def ps(self, name, shape, ctx, dt=F32):
        return ctx.enter_context(self.nc.psum_tensor(name, shape, dt))

    def constants(self):
        nc, i = self.nc, self.i
        self.ident = self.sb("ident", [P, P])
        self.eps = self.sb("eps", [P, 1])
        self.g64 = self.sb("g64", [P, 6, DH])
        self.g128 = self.sb("g128", [P, 2, DHM])
        ident, g64, g128 = self.ident, self.g64, self.g128
        zero_done, ident_done, gains_in, scaled = (self.sem(f"const_{n}") for n in ("zero", "ident", "gains", "scaled"))
        with nc.Block() as block:
            @block.gpsimd
            def _(pool):
                pool.memset(ident[:], 0.0).then_inc(zero_done, 1)
                pool.memset(self.eps[:], EPS)
                pool.wait_ge(zero_done, 1)
                pool.affine_select(out=ident[:], in_=ident[:], compare_op=ALU.not_equal, fill=1.0, base=0,
                                   pattern=[[-1, P]], channel_multiplier=1).then_inc(ident_done, 1)

            @block.sync
            def _(sp):
                for n, name in enumerate(("g_qa", "g_ka", "g_qb", "g_kcmp", "g_kslc", "g_kwin")):
                    sp.dma_start(g64[:, n, :], i[name].partition_broadcast(P)).then_inc(gains_in, 16)
                for n, name in enumerate(("g_qm", "g_km")):
                    sp.dma_start(g128[:, n, :], i[name].partition_broadcast(P)).then_inc(gains_in, 16)

            @block.vector
            def _(dve):
                dve.wait_ge(gains_in, 8 * 16)
                dve.tensor_scalar_mul(g64[:, 0, :], g64[:, 0, :], DH ** -0.5).then_inc(scaled, 1)
                dve.tensor_scalar_mul(g64[:, 2, :], g64[:, 2, :], DH ** -0.5).then_inc(scaled, 1)

    def norm_rows(self, tag, load, gain, rows, out_t, keep=None):
        nc, ident = self.nc, self.ident
        nt = len(rows)
        ctx = ExitStack()
        with ctx:
            from_dram = isinstance(load, list)
            x = self.sb(f"{tag}_x", [P, nt, D], F32, ctx) if from_dram else load
            xn = keep if keep is not None else self.sb(f"{tag}_xn", [P, nt, D], F32, ctx)
            junk = self.sb(f"{tag}_sq", [P, D], F32, ctx)
            gb = self.sb(f"{tag}_gain", [P, D], F32, ctx)
            ss = self.sb(f"{tag}_ss", [P, nt], F32, ctx)
            tr = self.ps(f"{tag}_tr", [P, 2, 4, P], ctx)
            x_in, g_in, sq_done, chain, xn_done, tr_done, out_done, junk_done = (
                self.sem(f"{tag}_{n}") for n in ("x_in", "g_in", "sq_done", "chain", "xn_done", "tr_done", "out_done", "junk_done"))
            with nc.Block() as block:
                @block.sync
                def _(sp):
                    if from_dram:
                        for t, r in enumerate(rows):
                            sp.dma_start(x[:r, t, :], load[t]).then_inc(x_in, 16)
                            sp.wait_ge(x_in, 16 * (t + 1))
                    sp.dma_start(gb[:], gain.partition_broadcast(P)).then_inc(g_in, 16)

                @block.scalar
                def _(act):
                    def evac(u):
                        t, r = u // 2, rows[u // 2]
                        act.wait_ge(tr_done, u + 1)
                        act.copy(out_t[:, 4 * (u % 2):4 * (u % 2) + 4, P * t:P * t + r],
                                 tr[:, u % 2, :, :r]).then_inc(out_done, 1)

                    for t, r in enumerate(rows):
                        if from_dram:
                            act.wait_ge(x_in, 16 * (t + 1))
                        if t:
                            act.wait_ge(sq_done, t)
                        act.activation(junk[:r, :], x[:r, t, :], ACT.Square, accum_out=ss[:r, t:t + 1]).then_inc(junk_done, 1)
                        act.wait_ge(junk_done, t + 1)
                        act.activation(ss[:r, t:t + 1], ss[:r, t:t + 1], ACT.Sqrt, bias=self.eps[:r], scale=1.0 / D).then_inc(sq_done, 1)
                        if t:
                            evac(2 * t - 2)
                            evac(2 * t - 1)
                    evac(2 * nt - 2)
                    evac(2 * nt - 1)

                @block.vector
                def _(dve):
                    c = Chain(dve, chain)
                    dve.wait_ge(g_in, 16)
                    for t, r in enumerate(rows):
                        dve.wait_ge(sq_done, t + 1)
                        c.link(dve.reciprocal(ss[:r, t:t + 1], ss[:r, t:t + 1]))
                        dve.scalar_tensor_tensor(out=xn[:r, t, :], in0=x[:r, t, :], scalar=ss[:r, t:t + 1],
                                                 in1=gb[:r, :], op0=ALU.mult, op1=ALU.mult).then_inc(xn_done, 1)

                @block.tensor
                def _(pe):
                    for t, r in enumerate(rows):
                        pe.wait_ge(xn_done, t + 1)
                        for half in range(2):
                            u = 2 * t + half
                            if u >= 2:
                                pe.wait_ge(out_done, u - 1)
                            for k in range(4):
                                c0 = (4 * half + k) * P
                                last = pe.transpose(tr[:, half, k, :r], xn[:r, t, c0:c0 + P], ident[:r, :r])
                            last.then_inc(tr_done, 1)

    def linear(self, tag, xt, rows, weights, width, out, add=None, also=(), rounds=0):
        nc = self.nc
        nt = len(rows)
        chunks = [(c, min(512, width - c)) for c in range(0, width, 512)]
        ctx = ExitStack()
        with ctx:
            w = self.sb(f"{tag}_w", [P, 2, KD, 512], F32, ctx)
            acc = self.ps(f"{tag}_acc", [P, 4, 512], ctx)
            w_in = [self.sem(f"{tag}_w_in{b}") for b in range(2)]
            mm_done, even_out, odd_out, also_done, round_done = (self.sem(f"{tag}_{n}") for n in ("mm", "even_out", "odd_out", "also", "rounds"))
            units = [(j, t) for j in range(len(chunks)) for t in range(nt)]
            with nc.Block() as block:
                @block.sync
                def _(sp):
                    for j, (c0, n) in enumerate(chunks):
                        if j >= 2:
                            sp.wait_ge(mm_done, (j - 1) * nt)
                        sp.dma_start(w[:, j % 2, :, :n], weights[:, c0:c0 + n].rearrange("(k p) n -> p k n", p=P)).then_inc(w_in[j % 2], 16)
                    for dst, src in also:
                        sp.dma_start(dst, src).then_inc(also_done, 16)
                    if also:
                        sp.wait_ge(also_done, 16 * len(also))

                @block.tensor
                def _(pe):
                    for u, (j, t) in enumerate(units):
                        c0, n = chunks[j]
                        r = rows[t]
                        if t == 0:
                            pe.wait_ge(w_in[j % 2], 16 * (j // 2 + 1))
                        if u >= 4:
                            pe.wait_ge((even_out, odd_out)[u % 2], (u - 4) // 2 + 1)
                        for k in range(KD):
                            last = pe.matmul(acc[:r, u % 4, :n], xt[:, k, P * t:P * t + r], w[:, j % 2, k, :n],
                                             start=(k == 0), stop=(k == KD - 1))
                        last.then_inc(mm_done, 1)

                def evacuate(eng, parity, copy, done, between=None):
                    for u, (j, t) in enumerate(units):
                        if u % 2 == parity:
                            c0, n = chunks[j]
                            eng.wait_ge(mm_done, u + 1)
                            copy(eng, out[:rows[t], t, c0:c0 + n], acc[:rows[t], u % 4, :n], t, c0, n).then_inc(done, 1)
                            if between:
                                between()

                @block.scalar
                def _(act):
                    if add is None:
                        evacuate(act, 0, lambda e, o, p, t, c0, n: e.copy(o, p), even_out)

                @block.vector
                def _(dve):
                    steps, share = Chain(dve, round_done), [0]

                    def between():
                        share[0] += rounds
                        while share[0] >= 1:
                            share[0] -= 1
                            self.pick_round_step(steps)

                    if add is None:
                        evacuate(dve, 1, lambda e, o, p, t, c0, n: e.tensor_copy(o, p), odd_out, between)
                    else:
                        for u, (j, t) in enumerate(units):
                            c0, n = chunks[j]
                            dve.wait_ge(mm_done, u + 1)
                            dve.tensor_tensor(out[:rows[t], t, c0:c0 + n], acc[:rows[t], u % 4, :n],
                                              add[:rows[t], t, c0:c0 + n], ALU.add).then_inc((even_out, odd_out)[u % 2], 1)
                            between()
                    if steps.n:
                        steps.need(steps.n)

    def norm_heads(self, tag, x, rows, groups):
        nc = self.nc
        heads = sum(g[1] for g in groups)
        ctx = ExitStack()
        with ctx:
            nt = len(rows)
            sq = self.sb(f"{tag}_sq", [P, 512], F32, ctx)
            ss = self.sb(f"{tag}_ss", [P, nt, heads], F32, ctx)
            chain, sums_done, root_done = (self.sem(f"{tag}_{n}") for n in ("chain", "sums", "root"))

            def view(t, r, c0, nh, stride, size):
                return x[:r, t, c0:c0 + nh * stride].rearrange("p (h s) -> p h s", s=stride)[:, :, :size]

            with nc.Block() as block:
                @block.vector
                def _(dve):
                    c = Chain(dve, chain)
                    c.link(dve.memset(ss[:], 1.0))
                    for t, r in enumerate(rows):
                        h = 0
                        for c0, nh, stride, size, gain in groups:
                            v = view(t, r, c0, nh, stride, size)
                            s = sq[:r, :nh * size].rearrange("p (h s) -> p h s", s=size)
                            c.link(dve.tensor_tensor(s, v, v, ALU.mult))
                            c.link(dve.tensor_reduce(ss[:r, t, h:h + nh], s, AX, ALU.add))
                            c.link(dve.tensor_scalar(ss[:r, t, h:h + nh], ss[:r, t, h:h + nh], 1.0 / size, EPS, ALU.mult, ALU.add))
                            h += nh
                    dve.sem_inc(sums_done, 1)
                    dve.wait_ge(root_done, 1)
                    c.link(dve.reciprocal(ss[:], ss[:]))
                    for t, r in enumerate(rows):
                        h = 0
                        for c0, nh, stride, size, gain in groups:
                            v = view(t, r, c0, nh, stride, size)
                            c.link(dve.tensor_tensor(v, v, ss[:r, t, h:h + nh].unsqueeze(2).to_broadcast([r, nh, size]), ALU.mult))
                            c.link(dve.tensor_tensor(v, v, gain[:r, :].unsqueeze(1).to_broadcast([r, nh, size]), ALU.mult))
                            h += nh

                @block.scalar
                def _(act):
                    act.wait_ge(sums_done, 1)
                    act.activation(ss[:], ss[:], ACT.Sqrt).then_inc(root_done, 1)

    def transposes(self, tag, batches):
        nc, ident = self.nc, self.ident
        ctx = ExitStack()
        with ctx:
            tr = self.ps(f"{tag}_tr", [P, 4, 512], ctx)
            tr_done, act_out, dve_out = (self.sem(f"{tag}_{n}") for n in ("tr_done", "act_out", "dve_out"))

            def bank(u):
                dst, srcs = batches[u]
                m, r = dst.shape[0], dst.shape[-1]
                return tr[:m, u % 4, :len(srcs) * r].rearrange("p (n r) -> p n r", r=r)

            with nc.Block() as block:
                @block.tensor
                def _(pe):
                    for u, (dst, srcs) in enumerate(batches):
                        if u >= 4:
                            pe.wait_ge((act_out, dve_out)[u % 2], (u - 4) // 2 + 1)
                        for n, src in enumerate(srcs):
                            r = src.shape[0]
                            last = pe.transpose(bank(u)[:, n, :], src, ident[:r, :r])
                        last.then_inc(tr_done, 1)

                @block.scalar
                def _(act):
                    for u in range(0, len(batches), 2):
                        act.wait_ge(tr_done, u + 1)
                        act.copy(batches[u][0], bank(u)).then_inc(act_out, 1)

                @block.vector
                def _(dve):
                    for u in range(1, len(batches), 2):
                        dve.wait_ge(tr_done, u + 1)
                        dve.tensor_copy(batches[u][0], bank(u)).then_inc(dve_out, 1)

    def copies(self, tag, pairs, done=None):
        done = done or self.sem(f"{tag}_copied")
        with self.block() as block:
            @block.sync
            def _(sp):
                with self.nc.allow_non_contiguous_dma(reason="small rows"):
                    for dst, src in pairs:
                        sp.dma_start(dst, src).then_inc(done, 16)
                sp.wait_ge(done, 16 * len(pairs))

    def build(self):
        nc, i, o = self.nc, self.i, self.o
        with self.ctx:
            self.store_sems = {n: nc.alloc_semaphore(name=f"stored_{n}") for n in ("new_rows", "mem_rows", "y_even", "y_odd", "y_sample")}
            self.constants()
            xT = self.sb("xn_t", [P, KD, NCOL])
            self.xT = xT
            xs = self.xs = [i["x_prompt"][0, P * t:P * t + P, :] for t in range(TP)] + [i["x_sample"][:, 0, :]]
            self.norm_rows("mix", xs, i["ln_mix"], ROWS, xT)
            self.oT = self.sb("o_t", [P, 12, SEQ])
            self.x8_t = self.sb("sample_xn_t", [P, KD, DB])
            self.o8_t = self.sb("sample_o_t", [P, 12, DB])
            self.e_idx8 = self.sb("e_idx8", [P, HP], U32)
            self.e_gate8 = self.sb("e_gate8", [P, HP])
            attn = ExitStack()
            with attn:
                self.attention(attn)
            self.finish()

    def attention(self, ctx):
        self.bias_tables(ctx)
        self.ht = self.sb("heads_t", [P, N_SLOT, SEQ], F32, ctx)
        self.qm_t = self.sb("sample_qm_t", [P, HM, DB], F32, ctx)
        self.qs_t = self.sb("sample_q_t", [P, 2 * HQ, DB], F32, ctx)
        self.qi_t = self.sb("sample_qi_t", [P, IH, DB], F32, ctx)
        self.ks_t = self.sb("sample_k_t", [DH, 3 * KV, DB], F32, ctx)
        self.vals = self.sb("values", [P, NT, 3, KV, DH], F32, ctx)
        self.w_idx = self.sb("index_weights", [P, NT, IH], F32, ctx)
        self.g_nsa = self.sb("branch_gates", [P, NT, 3 * HQ], F32, ctx)
        self.new_score = self.sb("new_key_score", [DB, 1], F32, ctx)
        tmp = ExitStack()
        with tmp:
            self.project(tmp)
        self.recycle()
        self.kc_t = self.sb("cmp_k_t", [P, DB, NCH_S], F32, ctx)
        self.kcp_t = self.sb("cmp_kp_t", [P, KV, NCH_P], F32, ctx)
        self.vc = self.sb("cmp_v", [P, DB, 2, KV, DH], F32, ctx)
        self.vcp = self.sb("cmp_vp", [NCH_P, KV, DH], F32, ctx)
        self.sample_constants(ctx)
        self.compress([("prompt", 0)])
        prompt = ExitStack()
        with prompt:
            self.memory_rows(prompt)
            self.recycle()
            self.prompt_attention()
            self.recycle()
        self.best_ix = self.sb("pi_ix", [DB, TOPA_S], U32, ctx)
        picking = ExitStack()
        with picking:
            self.pick_work = self.sb("pi_work", [DB, PAST + 1], F32, picking)
            self.best = self.sb("pi_best", [DB, TOPA_S], F32, picking)
            self.pick_next = 0
            self.index_scores()
            self.copies("da_back", [(self.pick_work[:, 0:PAST], self.s["score"]), (self.pick_work[:, PAST:PAST + 1], self.new_score[:])])
            self.recycle()
            self.finish_prompt()
            self.finish_rounds()
            self.recycle()
        self.prompt_experts()
        self.recycle()

    def pick_round_step(self, c):
        n, part = 8 * (self.pick_next // 3), self.pick_next % 3
        if n >= TOPA_S:
            return
        dve, best, ix, work = c.eng, self.best[:, n:n + 8], self.best_ix[:, n:n + 8], self.pick_work[:]
        if c.n:
            c.need(c.n)
        if part == 0:
            c.put(dve.max(best, work))
        elif part == 1:
            c.put(dve.max_index(ix, best, work))
        else:
            c.put(dve.match_replace(work, best, work, TAKEN))
        self.pick_next += 1

    def finish_rounds(self):
        rounds = self.sem("pi_last_rounds")
        with self.nc.Block() as block:
            @block.vector
            def _(dve):
                c = Chain(dve, rounds)
                while self.pick_next < 3 * TOPA_S // 8:
                    self.pick_round_step(c)
                if c.n:
                    c.need(c.n)

    def project(self, ctx):
        nc, i, o = self.nc, self.i, self.o
        pr = self.pr = self.sb("proj", [P, NT, IN_W], F32, ctx)
        self.linear("in", self.xT, ROWS, i["w_in"], IN_W, pr)
        g64, g128 = self.g64, self.g128
        self.norm_heads("heads", pr, ROWS, [
            (Q_A, HQ, DH, DH, g64[:, 0, :]), (KV_A, KV, 128, DH, g64[:, 1, :]), (Q_B, HQ, DH, DH, g64[:, 2, :]),
            (KV_S, KV, 128, DH, g64[:, 4, :]), (KV_W, KV, 128, DH, g64[:, 5, :]), (Q_M, HM, DHM, DHM, g128[:, 0, :])])
        pairs = []
        for name, c0, w in (("a_kv", KV_A, 256), ("a_kidx", K_I, 64), ("cmp_kv", KV_C, 256), ("slc_kv", KV_S, 256), ("win_kv", KV_W, 256)):
            for t in range(TP):
                pairs.append((o[name + "_p"][0, P * t:P * t + P], pr[:, t, c0:c0 + w]))
            if name != "win_kv":
                pairs.append((o[name + "_s"][:, 0], pr[:DB, TP, c0:c0 + w]))
        pairs.append((o["win_kv_s"][:, WIN - 1], pr[:DB, TP, KV_W:KV_W + 256]))
        pairs.append((o["win_kv_s"][:, 0:WIN - 1], i["cache_win_kv"][:, 1:WIN]))
        self.copies("new_rows", pairs, self.stores("new_rows"))
        self.keep_values()
        self.self_score()
        self.turn_heads()

    def self_score(self):
        pr = self.pr
        ctx = ExitStack()
        with ctx:
            prod = self.sb("own_prod", [DB, IH, DH], F32, ctx)
            dots = self.sb("own_dots", [DB, IH], F32, ctx)
            chain = self.sem("own_chain")
            with self.nc.Block() as block:
                @block.vector
                def _(dve):
                    c = Chain(dve, chain)
                    q = pr[:DB, TP, Q_I:Q_I + 256].rearrange("p (h s) -> p h s", h=IH)
                    k = pr[:DB, TP, K_I:K_I + DH].unsqueeze(1).to_broadcast([DB, IH, DH])
                    c.link(dve.tensor_tensor(prod[:], q, k, ALU.mult))
                    c.link(dve.tensor_reduce(dots[:], prod[:], AX, ALU.add))
                    c.link(dve.scalar_tensor_tensor(out=dots[:], in0=dots[:], scalar=0.0, in1=pr[:DB, TP, W_I:W_I + IH], op0=ALU.max, op1=ALU.mult))
                    c.link(dve.tensor_reduce(self.new_score[:], dots[:], AX, ALU.add))

    def keep_values(self):
        pr, vals, w_idx, g_nsa = self.pr, self.vals, self.w_idx, self.g_nsa
        kept, gated = self.sem("values_kept"), self.sem("gates_done")
        with self.nc.Block() as block:
            @block.gpsimd
            def _(pool):
                for t, r in enumerate(ROWS):
                    for n, c0 in enumerate((KV_A, KV_S, KV_W)):
                        src = pr[:r, t, c0:c0 + 256].rearrange("p (g s) -> p g s", g=KV)[:, :, DH:]
                        pool.tensor_copy(vals[:r, t, n], src).then_inc(kept, 1)
                    pool.tensor_copy(w_idx[:r, t, :], pr[:r, t, W_I:W_I + IH]).then_inc(kept, 1)

            @block.scalar
            def _(act):
                for t, r in enumerate(ROWS):
                    act.activation(g_nsa[:r, t, :], pr[:r, t, G_N:G_N + 3 * HQ], ACT.Sigmoid).then_inc(gated, 1)

    def memory_rows(self, ctx):
        i, o = self.i, self.o
        mt = MEM // P
        mkv = self.mkv = self.sb("mem_kv", [P, mt, HM * 2 * DHM], F32, ctx)
        self.km_t = self.sb("mem_k_t", [P, HM, MEM], F32, ctx)
        tmp = ExitStack()
        with tmp:
            mem_t = self.sb("mem_t", [P, KD, MEM], F32, tmp)
            self.norm_rows("mem", [i["mem_prompt"][0, P * t:P * t + P, :] for t in range(mt)], i["ln_mem"], [P] * mt, mem_t)
            self.linear("mem_kv", mem_t, [P] * mt, i["w_mem_kv"], HM * 2 * DHM, mkv)
        self.norm_heads("mem_heads", mkv, [P] * mt, [(0, HM, 2 * DHM, DHM, self.g128[:, 1, :])])
        self.copies("mem_rows", [(o["mem_kv_p"][0, P * t:P * t + P, :], mkv[:, t, :]) for t in range(mt)],
                    self.stores("mem_rows"))
        self.transposes("mem_k", [(self.km_t[:, 0:4, P * t:P * t + P],
                                   [mkv[:, t, 2 * DHM * h:2 * DHM * h + DHM] for h in range(HM)]) for t in range(mt)])

    def bias_tables(self, ctx):
        nc, i, s = self.nc, self.i, self.s
        nt = PAST // P + 1
        width = nt * P
        tmp = ExitStack()
        self.bias_cmp = self.sb("bias_cmp", [DB * HQ, NCH_S], F32, ctx)
        self.bias_win = self.sb("bias_win", [DB * HQ, WIN], F32, ctx)
        self.bias_self = self.sb("bias_self", [DB * HQ, 2], F32, ctx)
        with tmp:
            bounds = self.sb("bounds", [NB, 2], F32, tmp)
            dist_i = self.sb("dist_i", [NB, width], I32, tmp)
            dist = self.sb("dist", [NB, width], F32, tmp)
            hot = self.sb("hot", [NB, width], F32, tmp)
            table = self.sb("table", [NB, 16], F32, tmp)
            rep = self.sb("table_rep", [NB, 2, DB, HQ], F32, tmp)
            pos = self.sb("pos", [P, nt, 16], F32, tmp)
            rev = self.sb("rev", [16, 640], F32, tmp)
            by_head = self.sb("by_head", [16, PAST], F32, tmp)
            pos_ps = self.ps("pos_ps", [P, 2, 512], tmp)
            rev_ps = self.ps("rev_ps", [P, 512], tmp)
            win_ps = self.ps("win_ps", [P, 512], tmp)
            cmp_ps = self.ps("cmp_ps", [P, 512], tmp)
            self_ps = self.ps("self_ps", [P, 512], tmp)
            row_ps = self.ps("row_ps", [P, 2, 512], tmp)
            row_mm, row_out = self.sem("bias_row_mm"), self.sem("bias_row_out")
            loaded, iota_done, hot_done, mm_done, out_done, chain, stored = (
                self.sem(f"bias_{n}") for n in ("loaded", "iota", "hot", "mm", "out", "chain", "stored"))
            with nc.Block() as block:
                @block.sync
                def _(sp):
                    sp.dma_start(bounds[:], i["bounds"]).then_inc(loaded, 16)
                    sp.dma_start(table[:], i["rel_table"]).then_inc(loaded, 16)
                    sp.wait_ge(out_done, 1)
                    sp.dma_start(s["bias_rev"], rev[:]).then_inc(stored, 16)
                    sp.dma_start(s["bias_pos"][:nt * P].rearrange("(t p) h -> p t h", p=P), pos[:]).then_inc(stored, 16)
                    sp.dma_start(s["bias_head"], by_head[:]).then_inc(stored, 16)
                    sp.wait_ge(stored, 48)

                @block.gpsimd
                def _(pool):
                    pool.iota(dist_i[:], pattern=[[-1, width]], base=PAST, channel_multiplier=0).then_inc(iota_done, 1)

                @block.vector
                def _(dve):
                    c = Chain(dve, chain)
                    dve.wait_ge(iota_done, 1)
                    dve.wait_ge(loaded, 32)
                    c.link(dve.tensor_copy(dist[:], dist_i[:]))
                    c.link(dve.tensor_scalar(hot[:], dist[:], bounds[:, 0:1], None, ALU.is_ge))
                    c.link(dve.tensor_scalar(dist[:], dist[:], bounds[:, 1:2], None, ALU.is_lt))
                    dve.tensor_tensor(hot[:], hot[:], dist[:], ALU.mult).then_inc(hot_done, 1)
                    for b in range(DB):
                        dve.tensor_copy(rep[:, 0, b, :], table[:, 0:HQ])
                        last = dve.tensor_copy(rep[:, 1, b, :], table[:, HQ:16])
                    last.then_inc(hot_done, 1)
                    c.link(dve.memset(rev[:], NEG))
                    dve.wait_ge(mm_done, 1)
                    flat = pos[:].rearrange("p t h -> p (t h)")
                    c.link(dve.tensor_copy(flat[:, 0:512], pos_ps[:, 0, :]))
                    c.link(dve.tensor_copy(flat[:, 512:nt * 16], pos_ps[:, 1, :nt * 16 - 512]))
                    c.link(dve.tensor_copy(rev[:, 0:512], rev_ps[:16, :]))
                    for n in range(PAST // 512):
                        dve.wait_ge(row_mm, n + 1)
                        c.link(dve.tensor_copy(by_head[:, 512 * n:512 * n + 512], row_ps[:16, n % 2, :]))
                        dve.sem_inc(row_out, 1)
                    c.link(dve.tensor_copy(self.bias_win[:], win_ps[:DB * HQ, :]))
                    c.link(dve.tensor_copy(self.bias_cmp[:], cmp_ps[:DB * HQ, :NCH_S]))
                    dve.tensor_copy(self.bias_self[:], self_ps[:DB * HQ, :2]).then_inc(out_done, 1)

                @block.tensor
                def _(pe):
                    pe.wait_ge(hot_done, 2)
                    for t in range(nt):
                        pe.matmul(pos_ps[:, t // 32, 16 * (t % 32):16 * (t % 32) + 16], hot[:, P * t:P * t + P], table[:],
                                  start=True, stop=True)
                    pe.matmul(rev_ps[:16, :], table[:], hot[:, PAST - 511:PAST + 1], start=True, stop=True)
                    rep_b = rep[:, 1].rearrange("k b h -> k (b h)")
                    pe.matmul(win_ps[:DB * HQ, :], rep_b, hot[:, PAST - WIN:PAST], start=True, stop=True)
                    pe.matmul(cmp_ps[:DB * HQ, :NCMP_S], rep_b, hot[:, 31:31 + 16 * NCMP_S - 15:16], start=True, stop=True)
                    pe.matmul(cmp_ps[:DB * HQ, NCMP_S:NCH_S], rep_b, hot[:, 0:1], start=True, stop=True)
                    for n in range(2):
                        last = pe.matmul(self_ps[:DB * HQ, n:n + 1], rep[:, n].rearrange("k b h -> k (b h)"), hot[:, PAST:PAST + 1],
                                         start=True, stop=True)
                    last.then_inc(mm_done, 1)
                    for n in range(PAST // 512):
                        if n >= 2:
                            pe.wait_ge(row_out, n - 1)
                        pe.matmul(row_ps[:16, n % 2, :], table[:], hot[:, 512 * n:512 * n + 512], start=True, stop=True).then_inc(row_mm, 1)

    def turn_heads(self):
        pr = self.pr
        ht = self.ht
        tmp = ExitStack()
        with tmp:
            dup = self.sb("key_pairs", [P, TP, 7, 2, DH], F32, tmp)
            dup_s = self.sb("sample_pairs", [DB, 2 * HQ + IH, 2, DH], F32, tmp)
            dup_done = self.sem("pairs_done")
            with self.nc.Block() as block:
                @block.vector
                def _(dve):
                    for t in range(TP):
                        for n, c0 in enumerate((KV_A, KV_S, KV_W)):
                            src = pr[:, t, c0:c0 + 256].rearrange("p (g s) -> p g s", g=KV)[:, :, :DH]
                            for half in range(2):
                                dve.tensor_copy(dup[:, t, 2 * n:2 * n + 2, half, :], src).then_inc(dup_done, 1)
                        dve.tensor_copy(dup[:, t, 6], pr[:, t, K_I:K_I + DH].unsqueeze(1).to_broadcast([P, 2, DH])).then_inc(dup_done, 1)
                    for half in range(2):
                        for h0, nh, c0 in ((0, HQ, Q_A), (HQ, HQ, Q_B), (2 * HQ, IH, Q_I)):
                            dve.tensor_copy(dup_s[:, h0:h0 + nh, half, :], pr[:DB, TP, c0:c0 + DH * nh].rearrange("p (h s) -> p h s", h=nh)).then_inc(dup_done, 1)

            batches = []
            for t, r in enumerate(ROWS):
                row = pr[:r, t, :]
                if t < TP:
                    srcs = [row[:, c:c + P] for c0 in (Q_A, Q_B, Q_M) for c in range(c0, c0 + 512, P)]
                    srcs += [dup[:, t, n].rearrange("p t d -> p (t d)") for n in range(7)]
                    srcs += [row[:, Q_I:Q_I + P], row[:, Q_I + P:Q_I + 2 * P]]
                else:
                    srcs = [row[:, Q_M + P * h:Q_M + P * h + P] for h in range(HM)]
                dst = ht[:, :, P * t:P * t + P] if t < TP else self.qm_t
                for n in range(0, len(srcs), 4):
                    m = min(4, len(srcs) - n)
                    batches.append((dst[:, n:n + m, :], srcs[n:n + m]))
            row = pr[:DB, TP, :]
            both = [dup_s[:, h].rearrange("p t d -> p (t d)") for h in range(2 * HQ + IH)]
            batches.append((self.qs_t[:], both[:2 * HQ]))
            batches.append((self.qi_t[:], both[2 * HQ:]))
            batches.append((self.ks_t[:], [row[:, c0 + 128 * g:c0 + 128 * g + DH] for c0 in (KV_A, KV_S, KV_W) for g in range(KV)]))
            self.transposes("turn", batches)

    def compress(self, units, steps=0, w1=None):
        nc, i, o, ident = self.nc, self.i, self.o, self.ident
        tag = "cmp_" + units[0][0]
        kc_t, kcp_t, vc, vcp = self.kc_t, self.kcp_t, self.vc, self.vcp
        tmp = ExitStack()
        with tmp:
            w1 = self.sb(f"{tag}_w1", [P, 2 * STRIDE, P], F32, tmp) if w1 is None else w1
            w2 = self.sb(f"{tag}_w2", [P, P], F32, tmp)
            pe_t = self.sb(f"{tag}_pe_t", [P, 2 * STRIDE], F32, tmp)
            peh = self.sb(f"{tag}_peh", [P, 1], F32, tmp)
            ch = self.sb(f"{tag}_ch", [P, 2, 16, KV, 2, DH], F32, tmp)
            ct = self.sb(f"{tag}_ct", [P, STRIDE, KV, NCH_S], F32, tmp)
            hid = self.sb(f"{tag}_hid", [P, KV, NCH_S], F32, tmp)
            kn = self.sb(f"{tag}_kn", [P, 2, KV, DH], F32, tmp)
            sq = self.sb(f"{tag}_sq", [P, 2, KV, DH], F32, tmp)
            ss = self.sb(f"{tag}_ss", [P, 2 * KV], F32, tmp)
            kdup = self.sb(f"{tag}_kdup", [NCH_P, KV, 2, DH], F32, tmp)
            tr = self.ps(f"{tag}_tr", [P, 2, 512], tmp)
            hp = self.ps(f"{tag}_hp", [P, 2, 512], tmp)
            op = self.ps(f"{tag}_op", [P, 2, KV, 2, DH], tmp)
            kt = self.ps(f"{tag}_kt", [P, 512], tmp)
            pp = kt
            (weights_in, chain, ch_in, tr_done, ct_act, ct_dve, hid_mm, hid_done, out_mm, out_v, kn_done,
             root_done, sq_sum, kt_mm, kt_out, peh_mm, peh_done, zeroed) = (self.sem(f"{tag}_{n}") for n in (
                 "weights_in", "chain", "ch_in", "tr_done", "ct_act", "ct_dve", "hid_mm", "hid_done",
                 "out_mm", "out_v", "kn_done", "root_done", "sq_sum", "kt_mm", "kt_out", "peh_mm", "peh_done", "zeroed"))
            slot_in = [self.sem(f"{tag}_slot_in{n}") for n in range(2)]
            NU = len(units)
            prompt = units[0][0] == "prompt"

            def at(u, part):
                return min(1.0, (u + part) / NU)

            def tiles(u):
                return [(NCH_P, 0)] if prompt else [(P, 0), (P, P)]

            def n_cmp(u):
                return NCMP_P if prompt else NCMP_S

            def bank(u, k):
                return 16 * u + k

            with self.block(steps) as block:
                @block.sync
                def _(sp):
                    with nc.allow_non_contiguous_dma(reason="positional rows"):
                        sp.wait_ge(zeroed, 2)
                        for c in range(2):
                            half = slice(DH * c, DH * c + DH)
                            sp.dma_start(w1[half, :, half], i["w_cmp1"][c].rearrange("r d h -> d r h")).then_inc(weights_in, 16)
                            sp.dma_start(pe_t[half, :], i["cmp_pe"][c].rearrange("r d -> d r")).then_inc(weights_in, 16)
                            sp.dma_start(w2[half, half], i["w_cmp2"][c]).then_inc(weights_in, 16)
                    if prompt:
                        sp.dma_start(ch[:NCH_P, 0].rearrange("p a b c d -> p (a b c d)"),
                                     o["cmp_kv_p"][0].rearrange("(n r) w -> n (r w)", r=STRIDE)).then_inc(ch_in, 16)

                @block.gpsimd
                def _(pool):
                    pool.memset(w1[:], 0.0).then_inc(zeroed, 1)
                    pool.memset(w2[:], 0.0).then_inc(zeroed, 1)
                    view = i["cache_cmp_kv"].rearrange("n (c r) w -> (n c) (r w)", r=STRIDE)
                    for n in range(0 if prompt else 2 * NU):
                        u, slot = n // 2, n % 2
                        if u:
                            yield at(u - 1, 0.3)
                            pool.wait_ge(tr_done, bank(u - 1, 15) + 1)
                        pool.indirect_dma_start(
                            out=ch[:, slot].rearrange("p a b c d -> p (a b c d)"), out_offset=None, in_=view,
                            in_offset=bass.IndirectOffsetOnAxis(ap=self.row_of[:, n:n + 1], axis=0)).then_inc(slot_in[slot], 16)

                def evacuate(eng, copy, done, parity):
                    def run(u):
                        w = NCH_P if prompt else NCH_S
                        if u:
                            eng.wait_ge(hid_mm, u)
                        for k in range(parity, 16, 2):
                            yield at(u, 0.3 * k / 16)
                            eng.wait_ge(tr_done, bank(u, k) + 1)
                            copy(ct[:, k, :, :w], tr[:, k % 2, :KV * w].rearrange("p (g n) -> p g n", g=KV)).then_inc(done, 1)
                    return run

                @block.tensor
                def _(pe):
                    pe.wait_ge(weights_in, 16 * 6)
                    pe.wait_ge(zeroed, 2)
                    for k in range(2 * STRIDE):
                        last = pe.matmul(pp[:, 0:1], w1[:, k, :], pe_t[:, k:k + 1], start=(k == 0), stop=(k == 2 * STRIDE - 1))
                    last.then_inc(peh_mm, 1)

                    def second(u):
                        n = n_cmp(u)
                        pe.wait_ge(hid_done, u + 1)
                        if u:
                            pe.wait_ge(out_v, 2 * u)
                            pe.wait_ge(kn_done, u)
                        for s0, (r, c0) in enumerate(tiles(u)):
                            m = min(r, n - c0)
                            for g in range(KV):
                                last = pe.matmul(op[:m, s0, g].rearrange("p c d -> p (c d)"), hid[:, g, c0:c0 + m], w2[:], start=True, stop=True)
                        last.then_inc(out_mm, 1)

                    def third(u):
                        n = n_cmp(u)
                        pe.wait_ge(kn_done, u + 1)
                        if u:
                            pe.wait_ge(kt_out, u)
                        if u == 0:
                            pe.wait_ge(peh_done, 1)
                        if prompt:
                            for g in range(KV):
                                last = pe.transpose(kt[:, NCH_P * g:NCH_P * g + n], kdup[:n, g].rearrange("p t d -> p (t d)"), ident[:n, :n])
                        else:
                            for s0, (r, c0) in enumerate(tiles(u)):
                                m = min(r, n - c0)
                                last = pe.transpose(kt[:, c0:c0 + m], kn[:m, s0].rearrange("p g d -> p (g d)"), ident[:m, :m])
                        last.then_inc(kt_mm, 1)

                    for u in range(NU):
                        n = n_cmp(u)
                        if prompt:
                            pe.wait_ge(ch_in, 16)
                        else:
                            pe.wait_ge(slot_in[0], 16 * (u + 1))
                            pe.wait_ge(slot_in[1], 16 * (u + 1))
                        w = NCH_P if prompt else NCH_S
                        for k in range(16):
                            yield at(u, 0.3 * k / 16)
                            e = bank(u, k)
                            if e >= 2:
                                pe.wait_ge((ct_act, ct_dve)[k % 2], (e - 2) // 2 + 1)
                            for g in range(KV):
                                for s0, (r, c0) in enumerate(tiles(u)):
                                    slot = s0
                                    last = pe.transpose(tr[:, k % 2, g * w + c0:g * w + c0 + r],
                                                        ch[:r, slot, k, g].rearrange("p c d -> p (c d)"), ident[:r, :r])
                            last.then_inc(tr_done, 1)
                        pe.wait_ge(ct_act, 8 * (u + 1))
                        pe.wait_ge(ct_dve, 8 * (u + 1))
                        if u >= 2:
                            pe.wait_ge(hid_done, u - 1)
                        for k in range(2 * STRIDE):
                            j, r = k // STRIDE, k % STRIDE
                            yield at(u, 0.3 + 0.7 * k / (2 * STRIDE))
                            if u and k == 10:
                                second(u - 1)
                            if u and k == 28:
                                third(u - 1)
                            last = pe.matmul(hp[:, u % 2, :KV * n].rearrange("p (g n) -> p g n", g=KV), w1[:, k, :],
                                             ct[:, r, :, j:j + n], start=(k == 0), stop=(k == 2 * STRIDE - 1))
                        last.then_inc(hid_mm, 1)
                    yield 1.0
                    second(NU - 1)
                    third(NU - 1)

                @block.scalar
                def _(act):
                    act.wait_ge(peh_done, 1)
                    evac = evacuate(act, act.copy, ct_act, 0)

                    def gelu(u):
                        n = n_cmp(u)
                        act.wait_ge(hid_mm, u + 1)
                        if u:
                            act.wait_ge(out_mm, u)
                        act.activation(hid[:, :, :n], hp[:, u % 2, :KV * n].rearrange("p (g n) -> p g n", g=KV),
                                       ACT.Gelu_apprx_tanh, bias=peh[:, 0:1]).then_inc(hid_done, 1)

                    def root(u):
                        act.wait_ge(sq_sum, u + 1)
                        act.activation(ss[:], ss[:], ACT.Sqrt).then_inc(root_done, 1)

                    for u in range(NU):
                        yield from evac(u)
                        if u:
                            yield at(u, 0.7)
                            root(u - 1)
                        yield at(u, 1)
                        gelu(u)
                    yield 1.0
                    root(NU - 1)

                @block.vector
                def _(dve):
                    c_ = Chain(dve, chain)
                    dve.wait_ge(peh_mm, 1)
                    dve.tensor_copy(peh[:], pp[:, 0:1]).then_inc(peh_done, 1)
                    evac = evacuate(dve, dve.tensor_copy, ct_dve, 1)
                    c_.link(dve.memset(ss[:], 1.0))

                    def squares(u):
                        n = n_cmp(u)
                        dve.wait_ge(out_mm, u + 1)
                        if u >= 1:
                            dve.wait_ge(kt_mm, u)
                        for s0, (r, c0) in enumerate(tiles(u)):
                            m = min(r, n - c0)
                            dve.tensor_copy(vcp[:m] if prompt else vc[:m, units[u][1], s0], op[:m, s0, :, 1, :]).then_inc(out_v, 1)
                            c_.link(dve.tensor_copy(kn[:m, s0], op[:m, s0, :, 0, :]))
                            c_.link(dve.tensor_tensor(sq[:m, s0], kn[:m, s0], kn[:m, s0], ALU.mult))
                            c_.link(dve.tensor_reduce(ss[:m, KV * s0:KV * s0 + KV], sq[:m, s0], AX, ALU.add))
                            c_.link(dve.tensor_scalar(ss[:m, KV * s0:KV * s0 + KV], ss[:m, KV * s0:KV * s0 + KV], 1.0 / DH, EPS, ALU.mult, ALU.add))
                        dve.sem_inc(sq_sum, 1)

                    def keys(u):
                        n = n_cmp(u)
                        dve.wait_ge(root_done, u + 1)
                        c_.link(dve.reciprocal(ss[:], ss[:]))
                        for s0, (r, c0) in enumerate(tiles(u)):
                            m = min(r, n - c0)
                            for g in range(KV):
                                col = KV * s0 + g
                                last = dve.scalar_tensor_tensor(out=kn[:m, s0, g, :], in0=kn[:m, s0, g, :], scalar=ss[:m, col:col + 1],
                                                                in1=self.g64[:m, 3, :], op0=ALU.mult, op1=ALU.mult)
                                if prompt:
                                    c_.link(last)
                        if prompt:
                            for half in range(2):
                                last = dve.tensor_copy(kdup[:n, :, half, :], kn[:n, 0])
                        last.then_inc(kn_done, 1)

                    def turned(u):
                        n = n_cmp(u)
                        dve.wait_ge(kt_mm, u + 1)
                        if prompt:
                            last = dve.tensor_copy(kcp_t[:, :, :n], kt[:, :KV * NCH_P].rearrange("p (g n) -> p g n", g=KV)[:, :, :n])
                        else:
                            last = dve.tensor_copy(kc_t[:, units[u][1], :n], kt[:, :n])
                        last.then_inc(kt_out, 1)

                    for u in range(NU):
                        yield from evac(u)
                        if u:
                            yield at(u, 0.53)
                            squares(u - 1)
                            yield at(u, 0.75)
                            keys(u - 1)
                            yield at(u, 0.95)
                            turned(u - 1)
                        yield at(u, 1)
                    squares(NU - 1)
                    keys(NU - 1)
                    turned(NU - 1)

    def prompt_attention(self):
        ctx = ExitStack()
        with ctx:
            bias_t = self.bias_t = self.sb("bias_t", [P, 16, SEQ], F32, ctx)
            self.load_bias()
            self.mask_a = self.sb("mask_a", [P, TP - 1, SEQ], F32, ctx)
            self.o_rows = self.sb("o_rows", [P, TP, 3, 512], F32, ctx)
            self.select_prompt()
            self.attend_prompt()
            self.transposes("o_turn", [(self.oT[:, 4 * b:4 * b + 4, P * t:P * t + P],
                                        [self.o_rows[:, t, b, P * k:P * k + P] for k in range(4)])
                                       for t in range(TP) for b in range(3)])

    def load_bias(self):
        nc, bias_t = self.nc, self.bias_t
        ctx = ExitStack()
        with ctx:
            up = self.sb("lb_up", [P, 16, SEQ], F32, ctx)
            flip = self.sb("lb_flip", [P, P], F32, ctx)
            ps = self.ps("lb_ps", [P, 4, 512], ctx)
            loaded = [self.sem(f"lb_in{n}") for n in range(4)]
            made, mm, act_out, dve_out = (self.sem(f"lb_{n}") for n in ("made", "mm", "act_out", "dve_out"))
            with nc.Block() as block:
                @block.sync
                def _(sp):
                    for n in range(4):
                        sp.dma_start(up[:, 4 * n:4 * n + 4, :], bass.AP(self.s["bias_rev"].tensor, 640 * 4 * n, [[1, P], [640, 4], [1, SEQ]])).then_inc(loaded[n], 16)

                @block.gpsimd
                def _(pool):
                    pool.memset(flip[:], 0.0).then_inc(made, 1)
                    pool.wait_ge(made, 1)
                    pool.affine_select(out=flip[:], in_=flip[:], compare_op=ALU.not_equal, fill=1.0, base=1 - P, pattern=[[1, P]],
                                       channel_multiplier=1).then_inc(made, 1)

                @block.tensor
                def _(pe):
                    pe.wait_ge(made, 2)
                    for h in range(16):
                        pe.wait_ge(loaded[h // 4], 16)
                        if h >= 4:
                            pe.wait_ge((act_out, dve_out)[h % 2], (h - 4) // 2 + 1)
                        pe.matmul(ps[:, h % 4, :], flip[:], up[:, h, :], start=True, stop=True).then_inc(mm, 1)

                @block.scalar
                def _(act):
                    for h in range(0, 16, 2):
                        act.wait_ge(mm, h + 1)
                        act.copy(bias_t[:, h, :], ps[:, h % 4, :]).then_inc(act_out, 1)

                @block.vector
                def _(dve):
                    for h in range(1, 16, 2):
                        dve.wait_ge(mm, h + 1)
                        dve.tensor_copy(bias_t[:, h, :], ps[:, h % 4, :]).then_inc(dve_out, 1)

    def select_prompt(self):
        nc, ht, w_idx, mask = self.nc, self.ht, self.w_idx, self.mask_a
        ctx = ExitStack()
        with ctx:
            pos = self.sb("ix_relu", [P, 2, SEQ], F32, ctx)
            work = self.sb("ix_score", [P, TP - 1, SEQ], F32, ctx)
            best = self.sb("ix_best", [P, TP - 1, 8], F32, ctx)
            sp_ = self.ps("ix_ps", [P, 2, 512], ctx)
            mm, relu_done, add_done, causal_done, chain = (self.sem(f"ix_{n}") for n in ("mm", "relu", "add", "causal", "chain"))
            units = [(t, h) for t in range(1, TP) for h in range(IH)]
            with nc.Block() as block:
                @block.tensor
                def _(pe):
                    for u, (t, h) in enumerate(units):
                        half = slice(DH * (h % 2), DH * (h % 2) + DH)
                        nk = P * (t + 1)
                        if u >= 2:
                            pe.wait_ge(relu_done, u - 1)
                        pe.matmul(sp_[:, u % 2, :nk], ht[half, S_QI + h // 2, P * t:P * t + P], ht[half, S_KI, :nk],
                                  start=True, stop=True).then_inc(mm, 1)

                @block.scalar
                def _(act):
                    for u, (t, h) in enumerate(units):
                        nk = P * (t + 1)
                        act.wait_ge(mm, u + 1)
                        if u >= 2:
                            act.wait_ge(add_done, u - 1)
                        act.activation(pos[:, u % 2, :nk], sp_[:, u % 2, :nk], ACT.Relu).then_inc(relu_done, 1)

                @block.gpsimd
                def _(pool):
                    for t in range(1, TP):
                        pool.wait_ge(add_done, IH * t)
                        diag = work[:, t - 1, P * t:P * t + P]
                        pool.affine_select(out=diag, in_=diag, compare_op=ALU.is_ge, fill=NEG, base=0,
                                           pattern=[[-1, P]], channel_multiplier=1).then_inc(causal_done, 1)

                @block.vector
                def _(dve):
                    c = Chain(dve, chain)
                    for u, (t, h) in enumerate(units):
                        nk = P * (t + 1)
                        w = work[:, t - 1, :nk]
                        dve.wait_ge(relu_done, u + 1)
                        if h == 0:
                            dve.tensor_scalar(w, pos[:, u % 2, :nk], w_idx[:, t, h:h + 1], None, ALU.mult).then_inc(add_done, 1)
                        else:
                            dve.wait_ge(add_done, u)
                            dve.scalar_tensor_tensor(out=w, in0=pos[:, u % 2, :nk], scalar=w_idx[:, t, h:h + 1], in1=w,
                                                     op0=ALU.mult, op1=ALU.add).then_inc(add_done, 1)
                    dve.wait_ge(causal_done, TP - 1)
                    taken = [None] * TP
                    for _round in range(TOPA_P // 8):
                        found = [None] * TP
                        for t in range(1, TP):
                            if taken[t]:
                                c.need(taken[t])
                            found[t] = c.put(dve.max(best[:, t - 1, :], work[:, t - 1, :P * (t + 1)]))
                        for t in range(1, TP):
                            w = work[:, t - 1, :P * (t + 1)]
                            c.need(found[t])
                            taken[t] = c.put(dve.match_replace(w, best[:, t - 1, :], w, TAKEN))
                    for t in range(1, TP):
                        m, w = mask[:, t - 1, :P * (t + 1)], work[:, t - 1, :P * (t + 1)]
                        c.need(taken[t])
                        c.link(dve.tensor_scalar(m, w, TAKEN, None, ALU.is_equal))
                        c.link(dve.tensor_scalar(m, m, -1.0, -NEG, ALU.add, ALU.mult))

    def attend_prompt(self):
        nc, ht, ident = self.nc, self.ht, self.ident
        ctx = ExitStack()
        units = []
        for t in range(TP):
            units += [("a", h, t) for h in range(HQ)] + [("m", h, t) for h in range(HM)]
            units += [(kind, h, t) for h in range(HQ) for kind in "csw"]
        n = len(units)

        def keys(u):
            kind, h, t = units[u]
            return {"c": min(NCMP_P, (P // STRIDE) * t + 7), "m": MEM}.get(kind, P * (t + 1))

        def parts(u):
            return [(k, min(P, keys(u) - P * k)) for k in range(-(-keys(u) // P))]

        with ctx:
            lg = self.sb("at_logits", [P, 3, SEQ], F32, ctx)
            ex = self.sb("at_exp", [P, 3, SEQ], F32, ctx)
            et = self.sb("at_exp_t", [P, 2, 4, P], F32, ctx)
            mx = self.sb("at_max", [P, n], F32, ctx)
            sm = self.sb("at_sum", [P, n], F32, ctx)
            s_ps = self.ps("at_s_ps", [P, 3, 512], ctx)
            t_ps = self.ps("at_t_ps", [P, 2, 4, P], ctx)
            o_ps = self.ps("at_o_ps", [P, 2, 512], ctx)
            scored, logits_done, exp_done, turned, turn_out, mixed, fin_done, chain = (self.sem(f"at_{x}") for x in (
                "scored", "logits", "exp", "turned", "turn_out", "mixed", "fin", "chain"))

            with nc.Block() as block:
                @block.tensor
                def _(pe):
                    def score(u):
                        kind, h, t = units[u]
                        nk, g, cols = keys(u), h // GRP, slice(P * t, P * t + P)
                        half = slice(DH * (h % 2), DH * (h % 2) + DH)
                        q0 = S_QA if kind == "a" else S_QB
                        if u >= 3:
                            pe.wait_ge(logits_done, u - 2)
                            if units[u - 3][0] == "m":
                                pe.wait_ge(exp_done, u - 2)
                        if kind == "m":
                            lhs, rhs = ht[:, S_QM + h, cols], self.km_t[:, h, :]
                        else:
                            lhs = ht[half, q0 + h // 2, cols]
                            rhs = self.kcp_t[half, g, :nk] if kind == "c" else ht[half, {"a": S_KA, "s": S_KS, "w": S_KW}[kind] + g, :nk]
                        pe.matmul(s_ps[:, u % 3, :nk], lhs, rhs, start=True, stop=True).then_inc(scored, 1)

                    def turn(u):
                        pe.wait_ge(exp_done, u + 1)
                        if u >= 2:
                            pe.wait_ge(turn_out, u - 1)
                        for k, w in parts(u):
                            last = pe.transpose(t_ps[:w, u % 2, k, :], ex[:, u % 3, P * k:P * k + w], ident[:])
                        last.then_inc(turned, 1)

                    def mix(u):
                        kind, h, t = units[u]
                        g = h // GRP
                        pe.wait_ge(turn_out, u + 1)
                        if u >= 2:
                            pe.wait_ge(fin_done, u - 1)
                        dv = DHM if kind == "m" else DH
                        ps = parts(u)
                        for k, w in ps:
                            if kind == "m":
                                v = self.mkv[:, k, 2 * DHM * h + DHM:2 * DHM * (h + 1)]
                            elif kind == "c":
                                v = self.vcp[:w, g, :]
                            else:
                                v = self.vals[:w, k, {"a": 0, "s": 1, "w": 2}[kind], g, :]
                            last = pe.matmul(o_ps[:, u % 2, :dv], et[:w, u % 2, k, :], v, start=(k == 0), stop=(k == len(ps) - 1))
                        last.then_inc(mixed, 1)

                    for u in range(n + 3):
                        if u < n:
                            score(u)
                        if 2 <= u < n + 2:
                            turn(u - 2)
                        if u >= 3:
                            mix(u - 3)

                @block.scalar
                def _(act):
                    def exp(u):
                        kind, h, t = units[u]
                        act.wait_ge(logits_done, u + 1)
                        if u >= 3:
                            act.wait_ge(turned, u - 2)
                        src, scale = (s_ps, DHM ** -0.5) if kind == "m" else (lg, 1.0)
                        act.activation(ex[:, u % 3, :keys(u)], src[:, u % 3, :keys(u)], ACT.Exp, bias=mx[:, u:u + 1], scale=scale,
                                       accum_out=sm[:, u:u + 1]).then_inc(exp_done, 1)

                    def out(u):
                        act.wait_ge(turned, u + 1)
                        if u >= 2:
                            act.wait_ge(mixed, u - 1)
                        w = min(P, keys(u))
                        nk = len(parts(u))
                        act.copy(et[:w, u % 2, :nk, :], t_ps[:w, u % 2, :nk, :]).then_inc(turn_out, 1)

                    for u in range(n + 2):
                        if u < n:
                            exp(u)
                        if u >= 2:
                            out(u - 2)

                @block.vector
                def _(dve):
                    c = Chain(dve, chain)

                    def logits(u):
                        kind, h, t = units[u]
                        nk = keys(u)
                        l, m, sc = lg[:, u % 3, :nk], mx[:, u:u + 1], s_ps[:, u % 3, :nk]
                        dve.wait_ge(scored, u + 1)
                        if u >= 3:
                            dve.wait_ge(exp_done, u - 2)
                        x0 = SEQ - P - P * t
                        if kind == "m":
                            c.link(dve.tensor_reduce(m, sc, AX, ALU.max))
                            dve.tensor_scalar_mul(m, m, -DHM ** -0.5).then_inc(logits_done, 1)
                            return
                        if kind == "c":
                            bias = self.bias_t[:, HQ + h, x0 + 31:x0 + 31 + STRIDE * (nk - 1) + 1:STRIDE]
                        else:
                            bias = self.bias_t[:, h + (0 if kind == "a" else HQ), x0:x0 + nk]
                        if kind == "a" and t:
                            c.link(dve.tensor_tensor(l, sc, bias, ALU.add))
                            sc, bias = l, self.mask_a[:, t - 1, :nk]
                        c.link(dve.tensor_tensor_reduce(out=l, in0=sc, in1=bias, scale=1.0, scalar=NEG, op0=ALU.add, op1=ALU.max, accum_out=m))
                        dve.tensor_scalar(m, m, NEG / 10, -1.0, ALU.max, ALU.mult).then_inc(logits_done, 1)

                    def fin(u):
                        kind, h, t = units[u]
                        r = sm[:, u:u + 1]
                        dve.wait_ge(mixed, u + 1)
                        c.link(dve.tensor_scalar(r, r, 1e-30, None, ALU.max))
                        c.link(dve.reciprocal(r, r))
                        if kind == "a" or kind == "m":
                            w, b = (DH, 0) if kind == "a" else (DHM, 2)
                            dve.tensor_scalar(self.o_rows[:, t, b, w * h:w * h + w], o_ps[:, u % 2, :w], r, None, ALU.mult).then_inc(fin_done, 1)
                            return
                        o = self.o_rows[:, t, 1, DH * h:DH * h + DH]
                        gate = self.g_nsa[:, t, 3 * h + "csw".index(kind):3 * h + "csw".index(kind) + 1]
                        if kind == "c":
                            dve.tensor_scalar(o, o_ps[:, u % 2, :DH], r, gate, ALU.mult, ALU.mult).then_inc(fin_done, 1)
                        else:
                            c.link(dve.tensor_tensor(r, r, gate, ALU.mult))
                            dve.wait_ge(fin_done, u)
                            dve.scalar_tensor_tensor(out=o, in0=o_ps[:, u % 2, :DH], scalar=r, in1=o, op0=ALU.mult, op1=ALU.add).then_inc(fin_done, 1)

                    for u in range(n + 4):
                        if u < n:
                            logits(u)
                        if u >= 4:
                            fin(u - 4)

    def sample_attention(self):
        ctx = ExitStack()
        with ctx:
            self.sample_dsa()
            self.recycle()
            self.sample_cmp_slc()
            self.recycle()
            self.sample_window()
            self.sample_memory()
            self.recycle()

    def sample_constants(self, ctx):
        nc, i, s = self.nc, self.i, self.s
        self.own_mask = self.sb("own_mask", [DB * HQ, DB], F32, ctx)
        self.gate_bh = self.sb("gate_bh", [DB * HQ, 3], F32, ctx)
        self.pages_all = self.sb("pages_all", [P, DB, NPAGE], F32, ctx)
        self.group_of = self.sb("group_of", [DB * HQ, DB * KV], F32, ctx)
        self.heads_of = self.sb("heads_of", [DB * KV, DB * HQ], F32, ctx)
        self.iota32 = self.sb("iota32", [P, NPAGE], F32, ctx)
        self.part = self.sb("partition_no", [P, 1], I32, ctx)
        self.row_of = self.sb("chunk_rows", [P, 2 * DB], U32, ctx)
        own, group, heads = self.own_mask, self.group_of, self.heads_of
        tmp = ExitStack()
        self.copies("gates_out", [(s["gates"], self.g_nsa[:DB, TP, :]), (s["w8"], self.w_idx[:DB, TP, :])])
        with tmp:
            pages_i = self.sb("pages_i", [P, DB * NPAGE], I32, tmp)
            iota_i = self.sb("iota32_i", [P, NPAGE], I32, tmp)
            page_of = self.sb("chunk_pages", [P, 2 * DB], I32, tmp)
            page_f = self.sb("chunk_page_f", [P, 2 * DB], F32, tmp)
            sub_i = self.sb("chunk_sub_i", [P, 1], I32, tmp)
            sub_f = self.sb("chunk_sub_f", [P, 1], F32, tmp)
            loaded, made, chain = self.sem("sc_loaded"), self.sem("sc_made"), self.sem("sc_chain")
            with nc.Block() as block:
                @block.sync
                def _(sp):
                    sp.dma_start(self.gate_bh[:], s["gates"].rearrange("b (h c) -> (b h) c", c=3)).then_inc(loaded, 16)
                    sp.dma_start(pages_i[:], bass.AP(i["page_table"].tensor, 0, [[0, P], [1, DB * NPAGE]])).then_inc(loaded, 16)
                    with nc.allow_non_contiguous_dma(reason="the table of pages"):
                        for q in range(16):
                            src = bass.AP(i["page_table"].tensor, q, [[0, 8], [16, 2 * DB]])
                            sp.dma_start(page_of[8 * q:8 * q + 8, :], src).then_inc(loaded, 16)

                @block.gpsimd
                def _(pool):
                    n = 0

                    def link(ins):
                        nonlocal n
                        n += 1
                        ins.then_inc(made, 1)
                        pool.wait_ge(made, n)

                    link(pool.iota(iota_i[:], pattern=[[1, NPAGE]], base=0, channel_multiplier=0))
                    link(pool.iota(self.part[:], pattern=[[0, 1]], base=0, channel_multiplier=1))
                    link(pool.memset(own[:], 0.0))
                    link(pool.affine_select(out=own[:], in_=own[:], compare_op=ALU.is_ge, fill=NEG, base=0, pattern=[[-HQ, DB]], channel_multiplier=1))
                    link(pool.affine_select(out=own[:], in_=own[:], compare_op=ALU.is_ge, fill=NEG, base=HQ - 1, pattern=[[HQ, DB]], channel_multiplier=-1))
                    link(pool.memset(group[:], 1.0))
                    link(pool.affine_select(out=group[:], in_=group[:], compare_op=ALU.is_ge, fill=0.0, base=0, pattern=[[-GRP, DB * KV]], channel_multiplier=1))
                    link(pool.affine_select(out=group[:], in_=group[:], compare_op=ALU.is_ge, fill=0.0, base=GRP - 1, pattern=[[GRP, DB * KV]], channel_multiplier=-1))
                    link(pool.memset(heads[:], 1.0))
                    link(pool.affine_select(out=heads[:], in_=heads[:], compare_op=ALU.is_ge, fill=0.0, base=0, pattern=[[1, DB * HQ]], channel_multiplier=-GRP))
                    link(pool.affine_select(out=heads[:], in_=heads[:], compare_op=ALU.is_ge, fill=0.0, base=GRP - 1, pattern=[[-1, DB * HQ]], channel_multiplier=GRP))

                @block.vector
                def _(dve):
                    c = Chain(dve, chain)
                    dve.wait_ge(loaded, 16 * 18)
                    dve.wait_ge(made, 2)
                    c.link(dve.tensor_copy(page_f[:], page_of[:]))
                    c.link(dve.tensor_scalar(sub_i[:], self.part[:], 7, None, ALU.bitwise_and))
                    c.link(dve.tensor_copy(sub_f[:], sub_i[:]))
                    c.link(dve.tensor_scalar(page_f[:], page_f[:], float(PAGE // STRIDE), sub_f[:, 0:1], ALU.mult, ALU.add))
                    c.link(dve.tensor_copy(self.row_of[:], page_f[:]))
                    c.link(dve.tensor_copy(self.x8_t[:], self.xT[:, :, SEQ:]))
                    c.link(dve.tensor_copy(self.pages_all[:].rearrange("p b n -> p (b n)"), pages_i[:]))
                    c.link(dve.tensor_copy(self.iota32[:], iota_i[:]))

    def attend_samples(self, tag, nk, q0, keys, values, waits=(), keys_t=None, bias_t=None, bias=None, own=None, own_bias=0, gate=None,
                       prob=None, add=False, out0=0):
        nc, ident, qs = self.nc, self.ident, self.qs_t
        BH = DB * HQ
        tiles = [(j, min(P, nk - P * j)) for j in range(-(-nk // P))]
        nt = len(tiles)
        nown = DB if own is not None else 0
        units = [(b, j, m) for b in range(DB) for j, m in tiles]
        ctx = ExitStack()
        with ctx:
            kt = self.sb(f"{tag}_kt", [DH, 2, KV, P], F32, ctx)
            lt = self.sb(f"{tag}_lt", [P, nt, DB, KV, GRP], F32, ctx)
            lown = self.sb(f"{tag}_lown", [DB, DB, HQ], F32, ctx)
            pr = self.sb(f"{tag}_p", [BH, nk + DB], F32, ctx)
            plain = prob
            pt = self.sb(f"{tag}_pt", [P, nt, DB, HQ], F32, ctx)
            pown = self.sb(f"{tag}_pown", [DB, DB, HQ], F32, ctx)
            mx = self.sb(f"{tag}_mx", [BH, 1], F32, ctx)
            sm = self.sb(f"{tag}_sm", [BH, 1], F32, ctx)
            kt_ps = self.ps(f"{tag}_kt_ps", [P, 2, 512], ctx)
            lt_ps = self.ps(f"{tag}_lt_ps", [P, KV, 512], ctx)
            l_ps = kt_ps
            pt_ps = self.ps(f"{tag}_pt_ps", [P, 512], ctx)
            o_ps = self.ps(f"{tag}_o_ps", [P, 512], ctx)
            k_turned, k_out, scored, lt_out, l_turned, chain, soft_in, exp_done, prob_done, p_turned, p_out, mixed = (
                self.sem(f"{tag}_{n}") for n in ("k_turned", "k_out", "scored", "lt_out", "l_turned", "chain", "soft_in", "exp_done",
                                                 "prob_done", "p_turned", "p_out", "mixed"))
            ltv = lt_ps[:, :, :nt * DB * GRP].rearrange("p g (j b i) -> p g j b i", j=nt, b=DB)
            ptv = pt_ps[:, :nt * BH].rearrange("p (j c) -> p j c", j=nt)
            ov = o_ps[:, 0:4 * DB].rearrange("p (i b) -> p i b", b=DB)
            own_l, own_lt, own_p = o_ps[:DB, 64:64 + BH], o_ps[:BH, 128:128 + DB], o_ps[:DB, 192:192 + BH]

            with self.block(ATTEND) as block:
                @block.tensor
                def _(pe):
                    def turn(u):
                        b, j, m = units[u]
                        for sem, value in (waits(b) if waits else ()):
                            pe.wait_ge(sem, value)
                        if u >= 2:
                            pe.wait_ge(k_out, u - 1)
                        for g in range(KV):
                            last = pe.transpose(kt_ps[:DH, u % 2, P * g:P * g + m], keys(b, j, g), ident[:m, :m])
                        last.then_inc(k_turned, 1)

                    def score(u):
                        b, j, m = units[u]
                        if keys_t is None:
                            pe.wait_ge(k_out, u + 1)
                        for g in range(KV):
                            if keys_t is None:
                                lhs, q = kt[:, u % 2, g, :m], qs[:DH, q0 + GRP * g:q0 + GRP * g + GRP, b]
                            else:
                                lhs, q = keys_t(b, j, g), qs[DH * g:DH * g + DH, q0 + GRP * g:q0 + GRP * g + GRP, b]
                            last = pe.matmul(ltv[:m, g, j, b, :], lhs, q, start=True, stop=True)
                        last.then_inc(scored, 1)

                    if keys_t is None:
                        for u in range(len(units) + 1):
                            yield 0.5 * u / (len(units) + 1)
                            if u < len(units):
                                turn(u)
                            if u:
                                score(u - 1)
                    else:
                        for u in range(len(units)):
                            score(u)
                    if nown:
                        for g in range(KV):
                            q = qs[:DH, q0 + GRP * g:q0 + GRP * g + GRP, :].rearrange("p h b -> p b h")
                            dst = own_l.rearrange("p (b h) -> p b h", h=HQ)[:, :, GRP * g:GRP * g + GRP]
                            last = pe.matmul(dst, self.ks_t[:, KV * own + g, :], q, start=True, stop=True)
                        last.then_inc(scored, 1)
                    yield 0.5
                    pe.wait_ge(lt_out, 1)
                    for j, m in tiles:
                        last = pe.transpose(l_ps[:BH, j // 4, P * (j % 4):P * (j % 4) + m], lt[:m, j].rearrange("p b g i -> p (b g i)"), ident[:m, :m])
                    if nown:
                        last = pe.transpose(own_lt, lown[:].rearrange("p b h -> p (b h)"), ident[:DB, :DB])
                    last.then_inc(l_turned, 1)
                    pe.wait_ge(prob_done, 1)
                    for j, m in tiles:
                        last = pe.transpose(ptv[:m, j, :], pr[:, P * j:P * j + m], ident[:BH, :BH])
                    if nown:
                        last = pe.transpose(own_p, pr[:, nk:nk + DB], ident[:BH, :BH])
                    last.then_inc(p_turned, 1)
                    pe.wait_ge(p_out, 1)
                    started = [False, False]
                    for par in range(2):
                        half = slice(DH * par, DH * par + DH)
                        for g in range(KV):
                            if nown:
                                rhs = pown[:, :, GRP * g + par:GRP * g + GRP:2].rearrange("p b i -> p i b")
                                last = pe.matmul(ov[half, 2 * g:2 * g + 2, :], self.vals[:DB, TP, own, g, :], rhs,
                                                 start=not started[par], stop=False, skip_group_check=True)
                                started[par] = True
                    for u, (b, j, m) in enumerate(units):
                        yield 0.5 + 0.5 * u / len(units)
                        for g in range(KV):
                            for par in range(2):
                                half = slice(DH * par, DH * par + DH)
                                last = pe.matmul(ov[half, 2 * g:2 * g + 2, b], values(b, j, g), pt[:m, j, b, GRP * g + par:GRP * g + GRP:2],
                                                 start=not started[par], stop=True, skip_group_check=True)
                                started[par] = True
                    last.then_inc(mixed, 1)

                @block.scalar
                def _(act):
                    if keys_t is None:
                        for u, (b, j, m) in enumerate(units):
                            yield 0.5 * u / (len(units) + 1)
                            act.wait_ge(k_turned, u + 1)
                            if u >= 2:
                                act.wait_ge(scored, u - 1)
                            act.copy(kt[:, u % 2, :, :m], kt_ps[:DH, u % 2, :KV * P].rearrange("p (g m) -> p g m", g=KV)[:, :, :m]).then_inc(k_out, 1)
                    yield 0.5
                    act.wait_ge(soft_in, 1)
                    act.activation(pr[:, :nk + nown], pr[:, :nk + nown], ACT.Exp, bias=mx[:], accum_out=sm[:]).then_inc(exp_done, 1)

                @block.vector
                def _(dve):
                    c = Chain(dve, chain)
                    yield 0.5
                    dve.wait_ge(scored, len(units) + (1 if nown else 0))
                    for j, m in tiles:
                        for g in range(KV):
                            if bias_t is None:
                                c.put(dve.tensor_copy(lt[:m, j, :, g, :], ltv[:m, g, j]))
                            else:
                                c.put(dve.tensor_tensor(lt[:m, j, :, g, :], ltv[:m, g, j], bias_t(j)[:, :, GRP * g:GRP * g + GRP], ALU.add))
                    if nown:
                        c.put(dve.tensor_copy(lown[:].rearrange("p b h -> p (b h)"), own_l))
                    c.need(c.n)
                    dve.sem_inc(lt_out, 1)
                    dve.wait_ge(l_turned, 1)
                    for a in range(-(-nk // 512)):
                        w = min(512, nk - 512 * a)
                        dst = pr[:, 512 * a:512 * a + w]
                        if bias is None:
                            c.put(dve.tensor_copy(dst, l_ps[:BH, a, :w]))
                        else:
                            c.put(dve.tensor_tensor(dst, l_ps[:BH, a, :w], bias[:, 512 * a:512 * a + w], ALU.add))
                    if nown:
                        c.put(dve.scalar_tensor_tensor(out=pr[:, nk:nk + DB], in0=own_lt, scalar=self.bias_self[:, own_bias:own_bias + 1],
                                                       in1=self.own_mask[:], op0=ALU.add, op1=ALU.add))
                    c.need(c.n)
                    c.link(dve.tensor_reduce(mx[:], pr[:, :nk + nown], AX, ALU.max))
                    dve.tensor_scalar(mx[:], mx[:], -1.0, None, ALU.mult).then_inc(soft_in, 1)
                    dve.wait_ge(exp_done, 1)
                    c.link(dve.reciprocal(sm[:], sm[:]))
                    if prob is not None:
                        c.link(dve.tensor_scalar(plain[:, :nk], pr[:, :nk], sm[:, 0:1], None, ALU.mult))
                    if gate is not None:
                        c.link(dve.tensor_tensor(sm[:], sm[:], gate, ALU.mult))
                    dve.tensor_scalar(pr[:, :nk + nown], pr[:, :nk + nown], sm[:, 0:1], None, ALU.mult).then_inc(prob_done, 1)
                    dve.wait_ge(p_turned, 1)
                    for j, m in tiles:
                        c.put(dve.tensor_copy(pt[:m, j].rearrange("p b h -> p (b h)"), ptv[:m, j, :]))
                    if nown:
                        c.put(dve.tensor_copy(pown[:].rearrange("p b h -> p (b h)"), own_p))
                    c.need(c.n)
                    dve.sem_inc(p_out, 1)
                    yield 1.0
                    dve.wait_ge(mixed, 1)
                    o = self.o8_t[:, out0:out0 + 4, :]
                    if add:
                        c.link(dve.tensor_tensor(o, o, ov, ALU.add))
                    else:
                        c.link(dve.tensor_copy(o, ov))

    def sample_dsa(self):
        nc, i, s = self.nc, self.i, self.s
        ctx = ExitStack()
        with ctx:
            phys = self.sb("da_phys", [P, 2 * DB], U32, ctx)
            past_ix = self.sb("da_past_ix", [P, 2 * DB], U32, ctx)
            is_new = self.sb("da_is_new", [P, 2 * DB], F32, ctx)
            kv = self.sb("da_kv", [P, 2, DB, KV * 2 * DH], F32, ctx)
            bias = self.sb("da_bias", [P, 2, DB, 16], F32, ctx)
            own_bias = self.sb("da_own", [DB, 1], F32, ctx)
            self.pick_keys(phys, past_ix, is_new)
            self.gather("da_rows", [(kv[:, n // DB, n % DB, :], i["cache_a_kv"].rearrange("n p w -> (n p) w"), phys[:, n:n + 1]) for n in range(2 * DB)]
                        + [(bias[:, n // DB, n % DB, :], s["bias_pos"], past_ix[:, n:n + 1]) for n in range(2 * DB)])
            chain, was_new, old_self, new_self = (self.sem(f"da_{n}") for n in ("chain", "was_new", "old_self", "new_self"))
            ones = self.sb("da_ones", [P, DB * HQ], F32, ctx)
            hits = self.sb("da_hits", [DB * HQ, 2 * DB], F32, ctx)
            hit = self.sb("da_hit", [DB * HQ, DB], F32, ctx)
            own_saved = self.sb("da_own_saved", [DB * HQ, DB], F32, ctx)
            with nc.psum_tensor("da_h_ps", [P, 512], F32) as h_ps, self.block() as block:
                @block.vector
                def _(dve):
                    c = Chain(dve, chain)
                    c.link(dve.memset(ones[:], 1.0))
                    dve.sem_inc(was_new, 1)
                    c.link(dve.tensor_copy(own_saved[:], self.own_mask[:]))
                    flat = bias[:].rearrange("p j b h -> p (j b) h")
                    m = is_new[:].unsqueeze(2).to_broadcast([P, 2 * DB, 16])
                    c.link(dve.scalar_tensor_tensor(out=flat, in0=m, scalar=NEG, in1=flat, op0=ALU.mult, op1=ALU.add))
                    dve.wait_ge(new_self, 1)
                    c.link(dve.tensor_copy(hits[:], h_ps[:DB * HQ, :2 * DB]))
                    c.link(dve.tensor_tensor(hit[:], hits[:, 0:DB], hits[:, DB:2 * DB], ALU.add))
                    c.link(dve.tensor_scalar(hit[:], hit[:], -1.0, -NEG, ALU.add, ALU.mult))
                    c.link(dve.tensor_tensor(self.own_mask[:], self.own_mask[:], hit[:], ALU.add))

                @block.tensor
                def _(pe):
                    pe.wait_ge(was_new, 1)
                    pe.matmul(h_ps[:DB * HQ, :2 * DB], ones[:], is_new[:], start=True, stop=True).then_inc(new_self, 1)

            self.attend_samples("da_at", TOPA_S, 0, keys=lambda b, j, g: kv[:, j, b, 128 * g:128 * g + DH],
                                values=lambda b, j, g: kv[:, j, b, 128 * g + DH:128 * g + 128],
                                bias_t=lambda j: bias[:, j, :, 0:HQ], own=0, own_bias=0, out0=0)
            restored = self.sem("da_restored")
            with self.block() as block:
                @block.vector
                def _(dve):
                    dve.tensor_copy(self.own_mask[:], own_saved[:]).then_inc(restored, 1)

    def gather(self, tag, jobs, depth=4):
        sems = [self.sem(f"{tag}_in{n}") for n in range(min(depth, len(jobs)))]
        with self.block(len(jobs) // 2) as block:
            @block.gpsimd
            def _(pool):
                for n, (dst, table, rows) in enumerate(jobs):
                    yield n / len(jobs)
                    pool.indirect_dma_start(out=dst, out_offset=None, in_=table,
                                            in_offset=bass.IndirectOffsetOnAxis(ap=rows, axis=0)).then_inc(sems[n % depth], 16)
                for n, sem in enumerate(sems):
                    pool.wait_ge(sem, 16 * len(range(n, len(jobs), depth)))

    def index_scores(self):
        nc, i, s, ident = self.nc, self.i, self.s, self.ident
        ctx = ExitStack()
        NU, NBUF = 2 * DB, 4
        with ctx:
            ch = self.sb("is_ch", [P, NBUF, STRIDE * DH], F32, ctx)
            kt = self.sb("is_kt", [P, 2, 8, P], F32, ctx)
            qb = self.sb("is_q", [P, DB, 2, IH], F32, ctx)
            w = self.sb("is_w", [P, DB, IH], F32, ctx)
            rl = self.sb("is_relu", [P, STRIDE, IH], F32, ctx)
            sc = self.sb("is_score", [P, NU, STRIDE], F32, ctx)
            tr = self.ps("is_tr", [P, 4, 512], ctx)
            sp_ = self.ps("is_sp", [P, 2, 512], ctx)
            ch_in = [self.sem(f"is_ch_in{n}") for n in range(NBUF)]
            w_in, q_done, turned, act_out, dve_out, scored, sum_done, chain, stored = (self.sem(f"is_{n}") for n in (
                "w_in", "q", "turned", "act_out", "dve_out", "scored", "sum", "chain", "stored"))
            with nc.Block() as block:
                @block.sync
                def _(sp):
                    sp.dma_start(w[:].rearrange("p b h -> p (b h)"), bass.AP(s["w8"].tensor, 0, [[0, P], [1, DB * IH]])).then_inc(w_in, 16)
                    sp.wait_ge(sum_done, NU)
                    sp.dma_start(s["score"].rearrange("b (h c t) -> c (b h) t", h=2, t=STRIDE), sc[:]).then_inc(stored, 16)
                    sp.wait_ge(stored, 16)

                @block.gpsimd
                def _(pool):
                    view = i["cache_a_kidx"].rearrange("n (c r) w -> (n c) (r w)", r=STRIDE)
                    for u in range(NU):
                        if u >= NBUF:
                            pool.wait_ge(turned, 2 * (u - NBUF + 1))
                        pool.indirect_dma_start(out=ch[:, u % NBUF, :], out_offset=None, in_=view,
                                                in_offset=bass.IndirectOffsetOnAxis(ap=self.row_of[:, u:u + 1], axis=0)).then_inc(ch_in[u % NBUF], 16)

                @block.tensor
                def _(pe):
                    def turn(u):
                        pe.wait_ge(ch_in[u % NBUF], 16 * (u // NBUF + 1))
                        for a in range(2):
                            bank = 2 * (u % 2) + a
                            if u >= 2:
                                pe.wait_ge((act_out, dve_out)[a], u - 1)
                            for k in range(4):
                                c0 = (4 * a + k) * P
                                last = pe.transpose(tr[:, bank, P * k:P * k + P], ch[:, u % NBUF, c0:c0 + P], ident[:])
                            last.then_inc(turned, 1)

                    def score(u):
                        pe.wait_ge(act_out, u + 1)
                        pe.wait_ge(dve_out, u + 1)
                        if u >= 2:
                            pe.wait_ge(sum_done, u - 1)
                        for k in range(8):
                            last = pe.matmul(sp_[:, u % 2, 8 * k:8 * k + 8], kt[:, u % 2, k, :], qb[:, u // 2].rearrange("p t h -> p (t h)"),
                                             start=True, stop=True)
                        last.then_inc(scored, 1)

                    pe.wait_ge(q_done, 3)
                    for u in range(NU + 1):
                        if u < NU:
                            turn(u)
                        if u:
                            score(u - 1)

                @block.scalar
                def _(act):
                    for u in range(NU):
                        act.wait_ge(turned, 2 * u + 1)
                        if u >= 2:
                            act.wait_ge(scored, u - 1)
                        act.copy(kt[:, u % 2, 0:4, :], tr[:, 2 * (u % 2), :].rearrange("p (k n) -> p k n", k=4)).then_inc(act_out, 1)

                @block.vector
                def _(dve):
                    c = Chain(dve, chain)
                    dve.memset(qb[:], 0.0).then_inc(q_done, 1)
                    dve.wait_ge(q_done, 1)
                    for t in range(2):
                        half = slice(DH * t, DH * t + DH)
                        dve.tensor_copy(qb[half, :, t, :], self.qi_t[half].rearrange("p h b -> p b h")).then_inc(q_done, 1)
                    dve.wait_ge(w_in, 16)

                    def total(u):
                        dve.wait_ge(scored, u + 1)
                        c.link(dve.scalar_tensor_tensor(out=rl[:], in0=sp_[:, u % 2, :STRIDE * IH].rearrange("p (t h) -> p t h", h=IH), scalar=0.0,
                                                        in1=w[:, u // 2, :].unsqueeze(1).to_broadcast([P, STRIDE, IH]), op0=ALU.max, op1=ALU.mult))
                        c.link(dve.tensor_reduce(sc[:, u, :], rl[:], AX, ALU.add))
                        dve.sem_inc(sum_done, 1)

                    for u in range(NU):
                        dve.wait_ge(turned, 2 * u + 2)
                        if u >= 2:
                            dve.wait_ge(scored, u - 1)
                        dve.tensor_copy(kt[:, u % 2, 4:8, :], tr[:, 2 * (u % 2) + 1, :].rearrange("p (k n) -> p k n", k=4)).then_inc(dve_out, 1)
                        if u:
                            total(u - 1)
                    total(NU - 1)

    def pick_keys(self, phys, past_ix, is_new):
        nc, ident = self.nc, self.ident
        ctx = ExitStack()
        NC = 2 * DB
        with ctx:
            ixf = self.sb("pi_ixf", [DB, TOPA_S], F32, ctx)
            t_f = self.sb("pi_t", [P, NC], F32, ctx)
            t_i = self.sb("pi_ti", [P, 3, NC], U32, ctx)
            page = self.sb("pi_page", [P, 2, NC], F32, ctx)
            hot = self.sb("pi_hot", [P, DB, NPAGE], F32, ctx)
            tr = self.ps("pi_tr", [P, 512], ctx)
            chain, ready, turned = self.sem("pi_chain"), self.sem("pi_ready"), self.sem("pi_turned")
            with self.block() as block:
                @block.vector
                def _(dve):
                    c = Chain(dve, chain)
                    c.link(dve.tensor_copy(ixf[:], self.best_ix[:]))
                    dve.sem_inc(ready, 1)
                    dve.wait_ge(turned, 1)
                    c.link(dve.tensor_copy(t_f[:], tr[:, :NC]))
                    c.link(dve.tensor_scalar(is_new[:], t_f[:], float(PAST), None, ALU.is_equal))
                    c.link(dve.tensor_scalar(t_f[:], t_f[:], float(PAST - 1), None, ALU.min))
                    c.link(dve.tensor_copy(past_ix[:], t_f[:]))
                    c.link(dve.tensor_scalar(t_i[:, 0], past_ix[:], 7, None, ALU.logical_shift_right))
                    c.link(dve.tensor_scalar(t_i[:, 1], past_ix[:], PAGE - 1, None, ALU.bitwise_and))
                    c.link(dve.tensor_copy(page[:], t_i[:, 0:2]))
                    full = [P, DB, NPAGE]
                    for j in range(2):
                        cols = slice(DB * j, DB * j + DB)
                        c.link(dve.tensor_tensor(hot[:], page[:, 0, cols].unsqueeze(2).to_broadcast(full),
                                                 self.iota32[:].unsqueeze(1).to_broadcast(full), ALU.is_equal))
                        c.link(dve.tensor_tensor(hot[:], hot[:], self.pages_all[:], ALU.mult))
                        c.link(dve.tensor_reduce(t_f[:, cols], hot[:], AX, ALU.add))
                    c.link(dve.scalar_tensor_tensor(out=t_f[:], in0=t_f[:], scalar=float(PAGE), in1=page[:, 1], op0=ALU.mult, op1=ALU.add))
                    c.link(dve.tensor_copy(phys[:], t_f[:]))

                @block.tensor
                def _(pe):
                    pe.wait_ge(ready, 1)
                    for j in range(2):
                        last = pe.transpose(tr[:, DB * j:DB * j + DB], ixf[:, P * j:P * j + P], ident[:DB, :DB])
                    last.then_inc(turned, 1)

    def sample_cmp_slc(self):
        nc, i, s = self.nc, self.i, self.s
        ctx = ExitStack()
        NSLOT, NG = NSEL, DB * KV
        with ctx:
            rows = self.sb("sl_rows", [P, NG * 8], U32, ctx)
            bias = self.sb("sl_bias", [DB * HQ, NSLOT * BLK], F32, ctx)
            bias_rows = self.sb("sl_bias_rows", [DB * HQ, NSLOT], U32, ctx)
            tmp = ExitStack()
            with tmp:
                prob = self.sb("cm_prob", [DB * HQ, NCH_S + DB], F32, tmp)
                self.attend_samples("cm_at", NCMP_S, HQ, keys=None, keys_t=lambda b, j, g: self.kc_t[DH * g:DH * g + DH, b, P * j:P * j + min(P, NCMP_S - P * j)],
                                    values=lambda b, j, g: self.vc[:min(P, NCMP_S - P * j), b, j, g, :], bias=self.bias_cmp, prob=prob, out0=4,
                                    gate=self.gate_bh[:, 0:1])
                self.pick_blocks(prob, rows, bias_rows)
            kv_new = self.sb("sl_kv", [P, NG - 2 * KV, 8, 2 * DH], F32, ctx)
            old = [x.rearrange("p (g j w) -> p g j w", g=KV, j=8) for x in self.compressed_space()]
            kv = [kv_new[:, n] for n in range(NG - 2 * KV)] + [x[:, g] for x in old for g in range(KV)]
            self.gather("sl_gather", [(bias[:, BLK * n:BLK * n + BLK], s["bias_head"].rearrange("h (b t) -> (h b) t", t=BLK), bias_rows[:, n:n + 1])
                                      for n in range(NSLOT)]
                        + [(kv[n // 8][:, n % 8, :], i["cache_slc_kv"].rearrange("n p (g w) -> (n p g) w", g=KV), rows[:, n:n + 1]) for n in range(8 * NG)])
            dropped = self.sem("sl_dropped")
            with self.block() as block:
                @block.vector
                def _(dve):
                    dve.memset(bias[:, BLK * (NSLOT - 1):], NEG).then_inc(dropped, 1)
            self.attend_samples("sl_at", NSLOT * BLK, HQ, keys=lambda b, j, g: kv[KV * b + g][:, j, 0:DH], values=lambda b, j, g: kv[KV * b + g][:, j, DH:],
                                bias=bias, own=1, own_bias=1, gate=self.gate_bh[:, 1:2], add=True, out0=4)

    def compressed_space(self):
        return self.kc_t[:].rearrange("p b n -> p (b n)"), self.vc[:].rearrange("p b j g d -> p (b j g d)")

    def pick_blocks(self, prob, rows, bias_rows):
        nc, s = self.nc, self.s
        BH, NG = DB * HQ, DB * KV
        ctx = ExitStack()
        with ctx:
            pad = self.sb("pb_pad", [BH, NCH_S + 1], F32, ctx)
            imp = self.sb("pb_imp", [BH, 2, NBLK], F32, ctx)
            work = self.sb("pb_work", [NG, NBLK], F32, ctx)
            best = self.sb("pb_best", [NG, 2, 8], F32, ctx)
            blk = self.sb("pb_blk", [NG, NSEL], U32, ctx)
            parts = self.sb("pb_parts", [NG, 2, NSEL], U32, ctx)
            pf = self.sb("pb_pf", [NG, 2, NSEL], F32, ctx)
            blkf = self.sb("pb_blkf", [NG, NSEL], F32, ctx)
            hot = self.sb("pb_hot", [NG, NSEL, NPAGE], F32, ctx)
            base = self.sb("pb_base", [NG, NSEL], F32, ctx)
            pages_i = self.sb("pb_pages_i", [NG, NPAGE], I32, ctx)
            pages = self.sb("pb_pages", [NG, NPAGE], F32, ctx)
            odd_i = self.sb("pb_odd_i", [P, 4], I32, ctx)
            odd = self.sb("pb_odd", [P, 4], F32, ctx)
            two = self.sb("pb_two", [2, P], F32, ctx)
            base2 = self.sb("pb_base2", [2, NG, 8], F32, ctx)
            g_ps = self.ps("pb_g_ps", [P, 512], ctx)
            r_ps = self.ps("pb_r_ps", [P, 512], ctx)
            b_ps = self.ps("pb_b_ps", [P, 512], ctx)
            chain, pages_in, imp_done, g_done, blk_done, b_done, base_done, stored, base_in, r_done, two_done = (self.sem(f"pb_{n}") for n in (
                "chain", "pages_in", "imp", "g", "blk", "b", "base", "stored", "base_in", "r", "two"))
            with self.block() as block:
                @block.sync
                def _(sp):
                    sp.dma_start(pages_i[:], bass.AP(self.i["page_table"].tensor, 0, [[NPAGE, DB], [0, KV], [1, NPAGE]])).then_inc(pages_in, 16)
                    sp.wait_ge(base_done, 1)
                    sp.dma_start(s["sel_base"], base[:]).then_inc(stored, 16)
                    sp.wait_ge(stored, 16)
                    with nc.allow_non_contiguous_dma(reason="256 words"):
                        sp.dma_start(base2[:], bass.AP(s["sel_base"].tensor, 0, [[1, 2], [NSEL, NG], [2, 8]])).then_inc(base_in, 16)

                @block.gpsimd
                def _(pool):
                    pool.memset(two[:], 1.0).then_inc(two_done, 1)
                    pool.wait_ge(two_done, 1)
                    pool.affine_select(out=two[:], in_=two[:], compare_op=ALU.is_ge, fill=0.0, base=0, pattern=[[1, P]], channel_multiplier=-BLK).then_inc(two_done, 1)
                    pool.wait_ge(two_done, 2)
                    pool.affine_select(out=two[:], in_=two[:], compare_op=ALU.is_ge, fill=0.0, base=BLK - 1, pattern=[[-1, P]], channel_multiplier=BLK).then_inc(two_done, 1)

                @block.tensor
                def _(pe):
                    pe.wait_ge(imp_done, 1)
                    pe.matmul(g_ps[:NG, :NBLK], self.group_of[:], imp[:, 0, :], start=True, stop=True).then_inc(g_done, 1)
                    pe.wait_ge(blk_done, 1)
                    pe.matmul(b_ps[:BH, :NSEL], self.heads_of[:], blkf[:], start=True, stop=True).then_inc(b_done, 1)
                    pe.wait_ge(base_in, 16)
                    pe.wait_ge(two_done, 3)
                    pe.matmul(r_ps[:, :8 * NG], two[:], base2[:].rearrange("f q k -> f (q k)"), start=True, stop=True).then_inc(r_done, 1)

                @block.vector
                def _(dve):
                    c = Chain(dve, chain)
                    c.link(dve.tensor_scalar(odd_i[:, 0:1], self.part[:], 1, None, ALU.bitwise_and))
                    c.link(dve.tensor_scalar(odd_i[:, 1:2], self.part[:], BLK - 1, None, ALU.bitwise_and))
                    c.link(dve.tensor_scalar(odd_i[:, 2:3], self.part[:], HQ - 1, None, ALU.bitwise_and))
                    c.link(dve.tensor_copy(odd[:, 0:3], odd_i[:, 0:3]))
                    c.link(dve.tensor_scalar(odd[:, 1:2], odd[:, 1:2], float(KV), None, ALU.mult))
                    c.link(dve.tensor_scalar(odd[:, 2:3], odd[:, 2:3], float(HQ), float(NBLK), ALU.add, ALU.mult))
                    c.link(dve.memset(pad[:], 0.0))
                    c.link(dve.tensor_copy(pad[:, 1:1 + NCMP_S], prob[:, :NCMP_S]))
                    for n in range(2):
                        c.link(dve.tensor_reduce(imp[:, n], pad[:, 1 - n:1 - n + NCH_S].rearrange("p (j m) -> p j m", m=BLK // STRIDE), AX, ALU.add))
                    c.link(dve.tensor_tensor(imp[:, 0], imp[:, 0], imp[:, 1], ALU.add))
                    dve.sem_inc(imp_done, 1)
                    dve.wait_ge(g_done, 1)
                    c.link(dve.tensor_copy(work[:], g_ps[:NG, :NBLK]))
                    c.link(dve.memset(work[:, 0:1], -NEG))
                    c.link(dve.memset(work[:, NBLK - 1:NBLK], -NEG))
                    c.link(dve.max(best[:, 0], work[:]))
                    c.link(dve.max_index(blk[:, 0:8], best[:, 0], work[:]))
                    c.link(dve.match_replace(work[:], best[:, 0], work[:], TAKEN))
                    c.link(dve.max(best[:, 1], work[:]))
                    c.link(dve.max_index(blk[:, 8:16], best[:, 1], work[:]))
                    c.link(dve.tensor_copy(blkf[:], blk[:]))
                    dve.sem_inc(blk_done, 1)
                    dve.wait_ge(b_done, 1)
                    c.link(dve.tensor_scalar(bias_rows[:], b_ps[:BH, :NSEL], odd[:BH, 2:3], None, ALU.add))
                    c.link(dve.tensor_scalar(parts[:, 0], blk[:], 1, None, ALU.logical_shift_right))
                    c.link(dve.tensor_scalar(parts[:, 1], blk[:], 1, None, ALU.bitwise_and))
                    c.link(dve.tensor_copy(pf[:], parts[:]))
                    dve.wait_ge(pages_in, 16)
                    c.link(dve.tensor_copy(pages[:], pages_i[:]))
                    full = [NG, NSEL, NPAGE]
                    c.link(dve.tensor_tensor(hot[:], pf[:, 0].unsqueeze(2).to_broadcast(full), self.iota32[:NG].unsqueeze(1).to_broadcast(full), ALU.is_equal))
                    c.link(dve.tensor_tensor(hot[:], hot[:], pages[:].unsqueeze(1).to_broadcast(full), ALU.mult))
                    c.link(dve.tensor_reduce(base[:], hot[:], AX, ALU.add))
                    c.link(dve.tensor_scalar(base[:], base[:], float(PAGE * KV), odd[:NG, 0:1], ALU.mult, ALU.add))
                    c.link(dve.scalar_tensor_tensor(out=base[:], in0=pf[:, 1], scalar=float(BLK * KV), in1=base[:], op0=ALU.mult, op1=ALU.add))
                    dve.sem_inc(base_done, 1)
                    dve.wait_ge(r_done, 1)
                    c.link(dve.tensor_scalar(rows[:], r_ps[:, :8 * NG], odd[:, 1:2], None, ALU.add))

    def sample_window(self):
        i = self.i
        ctx = ExitStack()
        with ctx:
            kv = self.sb("wi_kv", [P, DB, WIN // P, KV * 2 * DH], F32, ctx)
            self.copies("wi_rows", [(kv[:], i["cache_win_kv"].rearrange("b (j p) w -> p b j w", p=P))])
            self.attend_samples("wi_at", WIN, HQ, keys=lambda b, j, g: kv[:, b, j, 128 * g:128 * g + DH],
                                values=lambda b, j, g: kv[:, b, j, 128 * g + DH:128 * g + 128], bias=self.bias_win, own=2, own_bias=1,
                                gate=self.gate_bh[:, 2:3], add=True, out0=4)

    def sample_memory(self):
        nc, i, ident = self.nc, self.i, self.ident
        ctx = ExitStack()
        mt, BH = MEM // P, DB * HM
        units = [(b, j, h) for b in range(DB) for j in range(mt) for h in range(HM)]
        with ctx:
            kv_new = self.sb("me_kv", [P, DB - 2, mt, HM * 2 * DHM], F32, ctx)
            kv = [kv_new[:, b] for b in range(DB - 2)] + [x.rearrange("p (j w) -> p j w", j=mt) for x in self.compressed_space()]
            kt = self.sb("me_kt", [P, 2, 4, P], F32, ctx)
            lt = self.sb("me_lt", [P, mt, DB, HM], F32, ctx)
            pr = self.sb("me_p", [BH, MEM], F32, ctx)
            pt = self.sb("me_pt", [P, mt, BH], F32, ctx)
            mx = self.sb("me_mx", [BH, 1], F32, ctx)
            sm = self.sb("me_sm", [BH, 1], F32, ctx)
            kt_ps = self.ps("me_kt_ps", [P, 2, 512], ctx)
            lt_ps = self.ps("me_lt_ps", [P, mt, DB, HM], ctx)
            l_ps = self.ps("me_l_ps", [P, 512], ctx)
            pt_ps = self.ps("me_pt_ps", [P, 512], ctx)
            o_ps = self.ps("me_o_ps", [P, 512], ctx)
            kv_in = [self.sem(f"me_kv_in{b}") for b in range(DB)]
            turned, out_done, scored, lt_out, l_turned, chain, soft_in, exp_done, prob_done, p_turned, p_out, mixed = (self.sem(f"me_{n}") for n in (
                "turned", "out", "scored", "lt_out", "l_turned", "chain", "soft_in", "exp", "prob", "p_turned", "p_out", "mixed"))
            ov = o_ps[:, :HM * DB].rearrange("p (h b) -> p h b", b=DB)
            with self.block(MEMORY) as block:
                @block.sync
                def _(sp):
                    for b in range(DB):
                        sp.dma_start(kv[b], i["cache_mem_kv"][b].rearrange("(j p) w -> p j w", p=P)).then_inc(kv_in[b], 16)

                @block.tensor
                def _(pe):
                    def turn(u):
                        b, j = u // mt, u % mt
                        pe.wait_ge(kv_in[b], 16)
                        if u >= 2:
                            pe.wait_ge(out_done, u - 1)
                        for h in range(HM):
                            last = pe.transpose(kt_ps[:, u % 2, P * h:P * h + P], kv[b][:, j, 2 * DHM * h:2 * DHM * h + DHM], ident[:])
                        last.then_inc(turned, 1)

                    def score(u):
                        b, j = u // mt, u % mt
                        pe.wait_ge(out_done, u + 1)
                        for h in range(HM):
                            last = pe.matmul(lt_ps[:, j, b, h:h + 1], kt[:, u % 2, h, :], self.qm_t[:, h, b:b + 1], start=True, stop=True)
                        last.then_inc(scored, 1)

                    for u in range(DB * mt + 1):
                        yield 0.6 * u / (DB * mt + 1)
                        if u < DB * mt:
                            turn(u)
                        if u:
                            score(u - 1)
                    yield 0.6
                    pe.wait_ge(lt_out, 1)
                    for j in range(mt):
                        last = pe.transpose(l_ps[:BH, P * j:P * j + P], lt[:, j].rearrange("p b h -> p (b h)"), ident[:])
                    last.then_inc(l_turned, 1)
                    pe.wait_ge(prob_done, 1)
                    for j in range(mt):
                        last = pe.transpose(pt_ps[:, BH * j:BH * j + BH], pr[:, P * j:P * j + P], ident[:BH, :BH])
                    last.then_inc(p_turned, 1)
                    pe.wait_ge(p_out, 1)
                    for b in range(DB):
                        yield 0.6 + 0.4 * b / DB
                        for h in range(HM):
                            for j in range(mt):
                                last = pe.matmul(ov[:, h, b:b + 1], kv[b][:, j, 2 * DHM * h + DHM:2 * DHM * (h + 1)], pt[:, j, HM * b + h:HM * b + h + 1],
                                                 start=(j == 0), stop=(j == mt - 1))
                    last.then_inc(mixed, 1)

                @block.scalar
                def _(act):
                    for u in range(DB * mt):
                        yield 0.6 * u / (DB * mt + 1)
                        act.wait_ge(turned, u + 1)
                        if u >= 2:
                            act.wait_ge(scored, u - 1)
                        act.copy(kt[:, u % 2], kt_ps[:, u % 2, :].rearrange("p (h m) -> p h m", h=HM)).then_inc(out_done, 1)
                    yield 0.6
                    act.wait_ge(soft_in, 1)
                    act.activation(pr[:], pr[:], ACT.Exp, bias=mx[:], scale=DHM ** -0.5, accum_out=sm[:]).then_inc(exp_done, 1)

                @block.vector
                def _(dve):
                    c = Chain(dve, chain)
                    yield 0.6
                    dve.wait_ge(scored, DB * mt)
                    c.link(dve.tensor_copy(lt[:], lt_ps[:]))
                    dve.sem_inc(lt_out, 1)
                    dve.wait_ge(l_turned, 1)
                    c.link(dve.tensor_copy(pr[:], l_ps[:BH, :MEM]))
                    c.link(dve.tensor_reduce(mx[:], pr[:], AX, ALU.max))
                    dve.tensor_scalar(mx[:], mx[:], -DHM ** -0.5, None, ALU.mult).then_inc(soft_in, 1)
                    dve.wait_ge(exp_done, 1)
                    c.link(dve.reciprocal(sm[:], sm[:]))
                    dve.tensor_scalar(pr[:], pr[:], sm[:, 0:1], None, ALU.mult).then_inc(prob_done, 1)
                    dve.wait_ge(p_turned, 1)
                    c.link(dve.tensor_copy(pt[:].rearrange("p j c -> p (j c)"), pt_ps[:, :mt * BH]))
                    dve.sem_inc(p_out, 1)
                    yield 1.0
                    dve.wait_ge(mixed, 1)
                    c.link(dve.tensor_copy(self.o8_t[:, 8:12, :], ov))

    def finish_rows(self, tag, x_t, o_t, rows, load_x, h, xf, save=(), rounds=(0, 0, 0)):
        nt, i = len(rows), self.i
        t_view = o_t[:, :KD]
        tmp = ExitStack()
        with tmp:
            mixed = self.sb(f"{tag}_mixed", [P, nt, D], F32, tmp)

            def turn(name, dst):
                self.transposes(f"{tag}_{name}", [(dst[:, 4 * q:4 * q + 4, P * t:P * t + r], [mixed[:r, t, P * k:P * k + P] for k in range(4 * q, 4 * q + 4)])
                                                  for t, r in enumerate(rows) for q in range(2)])

            self.merge(tag, x_t, o_t, rows, mixed, [(h[:r, t, :], load_x[t]) for t, r in enumerate(rows)], rounds[0])
            turn("mixed", t_view)
            self.linear(f"{tag}_out", t_view, rows, i["w_out"], D, h, add=h, rounds=rounds[1])
            self.recycle()
            self.norm_rows(f"{tag}_ffn", h, i["ln_ffn"], rows, t_view, keep=xf)
            self.linear(f"{tag}_pq", t_view, rows, i["w_pq"], D, mixed, also=save, rounds=rounds[2])
            turn("pq", x_t)

    def finish_prompt(self):
        s = self.s
        h, self.xf_prompt = (self.heads_space(TP * D * n, [TP, D]) for n in (1, 0))
        self.finish_rows("fp", self.xT[:, :, :SEQ], self.oT, ROWS[:TP], self.xs[:TP], h, self.xf_prompt,
                         save=[(s["h"].rearrange("(t p) d -> p t d", p=P), h)], rounds=(2.5, 2, 3))

    def heads_space(self, first, shape):
        words = self.ht[:].rearrange("p a b -> p (a b)")
        return words[:, first:first + shape[0] * shape[1]].rearrange("p (a b) -> p a b", b=shape[1])

    def prompt_experts(self):
        ctx = ExitStack()
        NBUF = 6
        with ctx:
            idx = self.e_idx = self.sb("e_idx", [P, TP, HP * PTOP], U32, ctx)
            gate = self.e_gate = self.sb("e_gate", [P, TP, HP * PTOP], F32, ctx)
            dots = self.sb("ex_dots", [P, TP, HP * PTOP], F32, ctx)
            coef = self.sb("ex_coef", [P, TP, HP * PTOP], F32, ctx)
            y = self.heads_space(TP * D, [2, D])
            diag = self.heads_space(TP * D + 2 * D, [8, P])
            u_new = self.sb("ex_u", [P, NBUF // 2, D], F32, ctx)
            u_old = self.heads_space(TP * D + 3 * D, [NBUF // 2, D])
            v = self.oT[:].rearrange("p a b -> p (a b)").rearrange("p (a b) -> p a b", b=D)
            y_ps = self.ps("ex_y_ps", [P, 2, 512], ctx)
            work = ExitStack()
            with work:
                retrieval = self.retrieval("pk", self.xT, [P] * TP, work)
                self.retrieve_first(retrieval)
                beside = self.beside = Beside(self.sem("beside_ended"))
                self.retrieve_rest(retrieval, 1, 2, RETRIEVE_NEXT)
                self.retrieve_rest(retrieval, 2, TP, RETRIEVE_LAST)
            w1 = self.xT[:].rearrange("p a b -> p (a b)")[:, :2 * STRIDE * P].rearrange("p (k n) -> p k n", n=P)
            self.compress([("sample", b) for b in range(DB)], COMPRESS, w1)
            self.sample_attention()
            self.beside = None
            self.mix_experts("ex", ROWS[:TP], [HP * PTOP] * TP, NBUF,
                             u=lambda n: u_new[:, n % NBUF] if n % NBUF < NBUF // 2 else u_old[:, n % NBUF - NBUF // 2],
                             v=lambda n: v[:, n % NBUF], x=lambda t: self.xf_prompt[:, t], index=lambda t, m: idx[:, t, m:m + 1],
                             gate=lambda t: gate[:, t], dots=dots, coef=coef, diag=diag, y=lambda t: y[:, t % 2], y_ps=y_ps,
                             h=[self.s["h"][P * t:P * t + P, :] for t in range(TP)],
                             dst=[self.o["y_prompt"][0, P * t:P * t + P, :] for t in range(TP)],
                             chosen=retrieval["idx_done"], beside=beside)

    def finish(self):
        self.h = self.sb("h", [P, 1, D])
        self.xf = self.sb("xf", [P, 1, D])
        self.finish_rows("fs", self.x8_t, self.o8_t, [DB], self.xs[TP:], self.h, self.xf)
        self.recycle()
        idx = self.e_idx = self.sb("es_idx", [P, 1, HP * PTOP], U32)
        self.e_gate = self.sb("es_gate", [P, 1, HP * PTOP])
        xf8 = self.e_xf8 = self.sb("e_xf8", [P, D])
        ctx = ExitStack()
        with ctx:
            self.retrieve_first(self.retrieval("pks", self.x8_t, [DB], ctx))
        self.spread_samples()
        ctx = ExitStack()
        with ctx:
            u, v = self.sb("exs_u", [P, HP, D], F32, ctx), self.sb("exs_v", [P, HP, D], F32, ctx)
            dots, coef = self.sb("exs_dots", [P, 1, HP], F32, ctx), self.sb("exs_coef", [P, 1, HP], F32, ctx)
            diag = self.sb("exs_diag", [P, 8, P], F32, ctx)
            y_ps = self.ps("exs_y_ps", [P, 2, 512], ctx)
            self.mix_experts("exs", [DB], [HP], HP, u=lambda n: u[:, n % HP], v=lambda n: v[:, n % HP], x=lambda t: xf8[:],
                             index=lambda t, m: self.e_idx8[:, m:m + 1], gate=lambda t: self.e_gate8[:], dots=dots, coef=coef, diag=diag,
                             y=lambda t: self.h[:, 0], y_ps=y_ps, h=None, dst=[self.o["y_sample"][:, 0, :]], chosen=None, beside=None)

    def merge(self, tag, xT, oT, rows, mixed, also, rounds):
        nc, i = self.nc, self.i
        nt = len(rows)
        ctx = ExitStack()
        jobs = [(q, c) for q in range(2) for c in range(3)]
        units = [(j, t) for j in range(len(jobs)) for t in range(nt)]
        with ctx:
            wg = self.sb(f"{tag}_mg_wg", [P, 2, KD, 512], F32, ctx)
            wb = self.sb(f"{tag}_mg_wb", [P, 2, 4, 512], F32, ctx)
            sig = self.sb(f"{tag}_mg_sig", [P, 2, 512], F32, ctx)
            prod = self.sb(f"{tag}_mg_prod", [P, 512], F32, ctx)
            g_ps = self.ps(f"{tag}_mg_g_ps", [P, 2, 512], ctx)
            u_ps = self.ps(f"{tag}_mg_u_ps", [P, 2, 512], ctx)
            w_in = [self.sem(f"{tag}_mg_w_in{n}") for n in range(2)]
            gate_mm, branch_mm, sig_done, sum_done, chain, also_done, round_done = (self.sem(f"{tag}_mg_{n}") for n in (
                "gate_mm", "branch_mm", "sig", "sum", "chain", "also", "rounds"))
            with nc.Block() as block:
                @block.sync
                def _(sp):
                    for j, (q, c) in enumerate(jobs):
                        if j >= 2:
                            sp.wait_ge(branch_mm, (j - 1) * nt)
                        sp.dma_start(wg[:, j % 2], i["w_gate"][:, D * c + 512 * q:D * c + 512 * q + 512].rearrange("(k p) n -> p k n", p=P)).then_inc(w_in[j % 2], 16)
                        sp.dma_start(wb[:, j % 2], i["w_branch"][c, :, 512 * q:512 * q + 512].rearrange("(k p) n -> p k n", p=P)).then_inc(w_in[j % 2], 16)
                        if j == 1:
                            for dst, src in also:
                                sp.dma_start(dst, src).then_inc(also_done, 16)
                    sp.wait_ge(also_done, 16 * len(also))

                @block.tensor
                def _(pe):
                    for u, (j, t) in enumerate(units):
                        q, c = jobs[j]
                        r, cols = rows[t], slice(P * t, P * t + rows[t])
                        if t == 0:
                            pe.wait_ge(w_in[j % 2], 32 * (j // 2 + 1))
                        if u >= 2:
                            pe.wait_ge(sig_done, u - 1)
                        for k in range(KD):
                            last = pe.matmul(g_ps[:r, u % 2, :], xT[:, k, cols], wg[:, j % 2, k, :], start=(k == 0), stop=(k == KD - 1))
                        last.then_inc(gate_mm, 1)
                        if u >= 2:
                            pe.wait_ge(sum_done, u - 1)
                        for k in range(4):
                            last = pe.matmul(u_ps[:r, u % 2, :], oT[:, 4 * c + k, cols], wb[:, j % 2, k, :], start=(k == 0), stop=(k == 3))
                        last.then_inc(branch_mm, 1)

                @block.scalar
                def _(act):
                    for u, (j, t) in enumerate(units):
                        act.wait_ge(gate_mm, u + 1)
                        if u >= 2:
                            act.wait_ge(sum_done, u - 1)
                        act.activation(sig[:rows[t], u % 2, :], g_ps[:rows[t], u % 2, :], ACT.Sigmoid).then_inc(sig_done, 1)

                @block.vector
                def _(dve):
                    ch = Chain(dve, chain)
                    steps = Chain(dve, round_done)
                    for u, (j, t) in enumerate(units):
                        q, c = jobs[j]
                        r = rows[t]
                        m = mixed[:r, t, 512 * q:512 * q + 512]
                        dve.wait_ge(sig_done, u + 1)
                        dve.wait_ge(branch_mm, u + 1)
                        if c == 0:
                            dve.tensor_tensor(m, sig[:r, u % 2, :], u_ps[:r, u % 2, :], ALU.mult).then_inc(sum_done, 1)
                        else:
                            if u:
                                dve.wait_ge(sum_done, u)
                            ch.link(dve.tensor_tensor(prod[:r, :], sig[:r, u % 2, :], u_ps[:r, u % 2, :], ALU.mult))
                            dve.tensor_tensor(m, m, prod[:r, :], ALU.add).then_inc(sum_done, 1)
                        for _ in range(int((u + 1) * rounds) - int(u * rounds)):
                            self.pick_round_step(steps)
                    if steps.n:
                        steps.need(steps.n)

    def retrieval(self, tag, q_t, rows, ctx):
        nc, i, ident = self.nc, self.i, self.ident
        HK = 2 * HP
        e_idx, e_gate = self.e_idx, self.e_gate
        keys_t = self.sb(f"{tag}_sk_t", [P, NKEY], F32, ctx)
        iota_f = self.sb(f"{tag}_pk_iota_f", [P, PTOP], F32, ctx)
        sc = self.sb(f"{tag}_pk_score", [P, HK, NKEY], F32, ctx)
        v = self.sb(f"{tag}_pk_v", [P, HK, PTOP], F32, ctx)
        ix = self.sb(f"{tag}_pk_i", [P, HK, PTOP], U32, ctx)
        ixf = self.sb(f"{tag}_pk_if", [P, HK, PTOP], F32, ctx)
        cand = self.sb(f"{tag}_pk_cand", [P, HP, PTOP, PTOP], F32, ctx)
        fv = self.sb(f"{tag}_pk_fv", [P, HP, PTOP], F32, ctx)
        fp = self.sb(f"{tag}_pk_fp", [P, HP, PTOP], U32, ctx)
        fa = self.sb(f"{tag}_pk_fa", [P, 2, HP, PTOP], U32, ctx)
        faf = self.sb(f"{tag}_pk_faf", [P, 2, HP, PTOP], F32, ctx)
        hot = self.sb(f"{tag}_pk_hot", [P, HP, PTOP, PTOP], F32, ctx)
        sel = self.sb(f"{tag}_pk_sel", [P, 2, HP, PTOP], F32, ctx)
        ss = self.sb(f"{tag}_pk_sum", [P, HP], F32, ctx)
        s_ps = self.ps(f"{tag}_pk_s_ps", [P, 4, 4, NKEY], ctx)
        mm, out_done, taken, idx_done, tile_done, chain, diff_done, exp_done = (self.sem(f"{tag}_{n}") for n in (
            "mm", "out", "taken", "idx", "tile", "chain", "diff", "exp"))
        c = Chain(None, chain)

        def scores(pe, n):
            t, r = n, rows[n]
            for a in range(2):
                if n:
                    pe.wait_ge(out_done, 4 * (n - 1) + 2 * a + 2)
                for b in range(4):
                    for p in range(2):
                        half = slice(DH * p, DH * p + DH)
                        last = pe.matmul(s_ps[:r, 2 * a + p, b, :], q_t[half, 4 * a + b, P * t:P * t + r], keys_t[half, :],
                                         start=True, stop=True)
                        if b == 3:
                            last.then_inc(mm, 1)

        def keep(act, n):
            r = rows[n]
            if n:
                act.wait_ge(taken, n)
            for a in range(4):
                act.wait_ge(mm, 4 * n + a + 1)
                h0, p = 4 * (a // 2), a % 2
                act.copy(sc[:r, 2 * h0 + p:2 * h0 + 8:2, :], s_ps[:r, a]).then_inc(out_done, 1)

        def soft(act, n):
            r = rows[n]
            act.wait_ge(diff_done, n + 1)
            act.activation(fv[:r], fv[:r], ACT.Exp).then_inc(exp_done, 1)

        def pick(dve, n):
            t, r = n, rows[n]
            c.eng = dve

            def top16(m, src, vals, idx):
                at = []
                for k in range(m):
                    at.append(c.put(dve.max(vals[:r, k, 0:8], src(k))))
                    yield
                for k in range(m):
                    c.need(at[k])
                    at[k] = c.put(dve.max_index(idx[:r, k, 0:8], vals[:r, k, 0:8], src(k)))
                    yield
                for k in range(m):
                    c.need(at[k])
                    at[k] = c.put(dve.match_replace(src(k), vals[:r, k, 0:8], src(k), NEG))
                    yield
                for k in range(m):
                    c.need(at[k])
                    at[k] = c.put(dve.max(vals[:r, k, 8:16], src(k)))
                    yield
                for k in range(m):
                    c.need(at[k])
                    at[k] = c.put(dve.max_index(idx[:r, k, 8:16], vals[:r, k, 8:16], src(k)))
                    yield
                c.need(at[m - 1])

            dve.wait_ge(out_done, 4 * n + 4)
            yield from top16(HK, lambda k: sc[:r, k, :], v, ix)
            dve.sem_inc(taken, 1)
            c.link(dve.tensor_copy(ixf[:r], ix[:r]))
            yield
            v2 = v[:r].rearrange("p (h s) k -> p h s k", s=2)
            i2 = ixf[:r].rearrange("p (h s) k -> p h s k", s=2)
            full = [r, HP, PTOP, PTOP]
            c.link(dve.tensor_tensor(cand[:r], v2[:, :, 0, :].unsqueeze(3).to_broadcast(full),
                                     v2[:, :, 1, :].unsqueeze(2).to_broadcast(full), ALU.add))
            yield
            yield from top16(HP, lambda k: cand[:r, k].rearrange("p a b -> p (a b)"), fv, fp)
            c.link(dve.tensor_scalar(fa[:r, 0], fp[:r], 4, None, ALU.logical_shift_right))
            c.link(dve.tensor_scalar(fa[:r, 1], fp[:r], 15, None, ALU.bitwise_and))
            c.link(dve.tensor_copy(faf[:r], fa[:r]))
            yield
            for a in range(2):
                c.link(dve.tensor_tensor(hot[:r], faf[:r, a].unsqueeze(3).to_broadcast(full),
                                         iota_f[:r].unsqueeze(1).unsqueeze(1).to_broadcast(full), ALU.is_equal))
                yield
                c.link(dve.tensor_tensor(hot[:r], hot[:r], i2[:, :, a, :].unsqueeze(2).to_broadcast(full), ALU.mult))
                yield
                c.link(dve.tensor_reduce(sel[:r, a], hot[:r], AX, ALU.add))
                yield
            flat = lambda x: x.rearrange("p h k -> p (h k)")
            c.link(dve.scalar_tensor_tensor(out=flat(sel[:r, 0]), in0=flat(sel[:r, 0]), scalar=float(NKEY), in1=flat(sel[:r, 1]),
                                            op0=ALU.mult, op1=ALU.add))
            dve.tensor_copy(e_idx[:r, t, :], flat(sel[:r, 0])).then_inc(idx_done, 1)
            c.link(dve.tensor_copy(ss[:r], fv[:r, :, 0]))
            dve.tensor_tensor(fv[:r], fv[:r], ss[:r].unsqueeze(2).to_broadcast([r, HP, PTOP]), ALU.subtract).then_inc(diff_done, 1)
            yield

        def gate(dve, n):
            t, r = n, rows[n]
            c.eng = dve
            dve.wait_ge(exp_done, n + 1)
            c.link(dve.tensor_reduce(ss[:r], fv[:r], AX, ALU.add))
            c.link(dve.reciprocal(ss[:r], ss[:r]))
            dve.tensor_tensor(e_gate[:r, t, :].rearrange("p (h k) -> p h k", h=HP), fv[:r],
                              ss[:r].unsqueeze(2).to_broadcast([r, HP, PTOP]), ALU.mult).then_inc(tile_done, 1)
            dve.wait_ge(tile_done, n + 1)

        return {"tag": tag, "rows": rows, "scores": scores, "keep": keep, "soft": soft, "pick": pick, "gate": gate, "idx_done": idx_done,
                "chain": c, "keys_t": keys_t, "iota_f": iota_f}

    def retrieve_first(self, part):
        nc, i, ident, tag, keys_t, c = self.nc, self.i, self.ident, part["tag"], part["keys_t"], part["chain"]
        tmp = ExitStack()
        with tmp:
            rows = self.sb(f"{tag}_sk_rows", [NKEY, 2, DH], F32, tmp)
            iota_i = self.sb(f"{tag}_iota_i", [P, PTOP], I32, tmp)
            k_ps = self.ps(f"{tag}_k_ps", [P, P], tmp)
            keys_in, keys_mm, keys_done, iota_done = (self.sem(f"{tag}_{n}") for n in ("keys_in", "keys_mm", "keys_done", "iota"))
            with nc.Block() as block:
                @block.sync
                def _(sp):
                    sp.dma_start(rows[:], i["sub_keys"].rearrange("p k d -> k p d")).then_inc(keys_in, 16)

                @block.gpsimd
                def _(pool):
                    pool.iota(iota_i[:], pattern=[[1, PTOP]], base=0, channel_multiplier=0).then_inc(iota_done, 1)

                @block.tensor
                def _(pe):
                    pe.wait_ge(keys_in, 16)
                    pe.transpose(k_ps[:], rows[:].rearrange("k p d -> k (p d)"), ident[:]).then_inc(keys_mm, 1)
                    pe.wait_ge(keys_done, 1)
                    part["scores"](pe, 0)

                @block.scalar
                def _(act):
                    act.wait_ge(keys_mm, 1)
                    act.copy(keys_t[:], k_ps[:]).then_inc(keys_done, 1)
                    part["keep"](act, 0)
                    part["soft"](act, 0)

                @block.vector
                def _(dve):
                    c.eng = dve
                    dve.wait_ge(iota_done, 1)
                    c.link(dve.tensor_copy(part["iota_f"][:], iota_i[:]))
                    for _ in part["pick"](dve, 0):
                        pass
                    part["gate"](dve, 0)

    def retrieve_rest(self, part, tile, end, steps):
        n_rest, STEPS = end - tile, 140
        with self.block(steps) as block:
            @block.tensor
            def _(pe):
                for n in range(n_rest):
                    yield n / n_rest
                    part["scores"](pe, tile + n)

            @block.scalar
            def _(act):
                for n in range(n_rest):
                    yield n / n_rest
                    part["keep"](act, tile + n)
                    yield (n + 1) / n_rest
                    part["soft"](act, tile + n)

            @block.vector
            def _(dve):
                for n in range(n_rest):
                    for m, _ in enumerate(part["pick"](dve, tile + n)):
                        yield min(n + m / STEPS, n + 1) / n_rest
                    yield (n + 1) / n_rest
                    part["gate"](dve, tile + n)

    def spread_samples(self):
        s = self.s
        self.copies("spread_out", [(s["x8"], self.xf[:DB, 0, :]), (s["gate8"], self.e_gate[:DB, 0, :]), (s["idx8"], self.e_idx[:DB, 0, :])])
        pairs = []
        for k in range(PTOP):
            at = slice(DB * k, DB * k + DB)
            pairs.append((self.e_xf8[at, :], s["x8"]))
            pairs.append((self.e_gate8[at, :], bass.AP(s["gate8"].tensor, k, [[P, DB], [PTOP, HP]])))
            pairs.append((self.e_idx8[at, :], bass.AP(s["idx8"].tensor, k, [[P, DB], [PTOP, HP]])))
        self.copies("spread_in", pairs)

    def mix_experts(self, tag, rows, slots, nbuf, u, v, x, index, gate, dots, coef, diag, y, y_ps, h, dst, chosen, beside):
        nc, i, ident = self.nc, self.i, self.ident
        nt, spread = len(rows), rows[0] < P
        first = [sum(slots[:t]) for t in range(nt)]
        ctx = ExitStack()
        with ctx:
            same = self.sb(f"{tag}_same", [P, DB], F32, ctx)
            u_in = [self.sem(f"{tag}_u_in{n}") for n in range(nbuf)]
            v_in = [self.sem(f"{tag}_v_in{n}") for n in range(nbuf)]
            h_in = [self.sem(f"{tag}_h_in{n}") for n in range(2)]
            stored = [self.stores("y_sample")] * 2 if spread else [self.stores("y_even"), self.stores("y_odd")]
            dot_done, gelu_done, coef_done, diag_done, mix_done, y_done, same_done = (self.sem(f"{tag}_{n}") for n in (
                "dot", "gelu", "coef", "diag", "mix", "y", "same"))

            def steps(k):
                nu = slots[k] if k < nt else 0
                nv = slots[k - 1] if k else 0
                return [(slots[0] * k + m, m if m < nu else None, m if m < nv else None) for m in range(max(nu, nv))]

            def others(name, eng, step=10 ** 9):
                if beside:
                    beside.advance(name, eng, step)

            with nc.Block() as block:
                @block.gpsimd
                def _(pool):
                    if spread:
                        pool.memset(same[:], 0.0).then_inc(same_done, 1)
                        for n in range(P // DB):
                            pool.wait_ge(same_done, n + 1)
                            pool.affine_select(out=same[:], in_=same[:], compare_op=ALU.not_equal, fill=1.0, base=-DB * n,
                                               pattern=[[-1, DB]], channel_multiplier=1).then_inc(same_done, 1)
                    for k in range(nt + 1):
                        if chosen is not None and k < nt:
                            pool.wait_ge(chosen, k + 1)
                        for step, su, sv in steps(k):
                            others("gpsimd", pool, step)
                            if su is not None:
                                n = first[k] + su
                                if n >= nbuf:
                                    pool.wait_ge(dot_done, n - nbuf + 1)
                                pool.indirect_dma_start(out=u(n), out_offset=None, in_=i["u_tab"],
                                                        in_offset=bass.IndirectOffsetOnAxis(ap=index(k, su), axis=0)).then_inc(u_in[n % nbuf], 16)
                            if sv is not None:
                                n = first[k - 1] + sv
                                if n >= nbuf:
                                    pool.wait_ge(mix_done, n - nbuf + 1)
                                pool.indirect_dma_start(out=v(n), out_offset=None, in_=i["v_tab"],
                                                        in_offset=bass.IndirectOffsetOnAxis(ap=index(k - 1, sv), axis=0)).then_inc(v_in[n % nbuf], 16)
                    others("gpsimd", pool)

                @block.vector
                def _(dve):
                    for k in range(nt + 1):
                        for step, su, sv in steps(k):
                            others("vector", dve, step)
                            if su is not None:
                                n = first[k] + su
                                dve.wait_ge(u_in[n % nbuf], 16 * (n // nbuf + 1))
                                dve.tensor_tensor_reduce(out=u(n), in0=u(n), in1=x(k), scale=1.0, scalar=0.0, op0=ALU.mult, op1=ALU.add,
                                                         accum_out=dots[:, k, su:su + 1]).then_inc(dot_done, 1)
                        if k < nt:
                            dve.wait_ge(gelu_done, k + 1)
                            dve.tensor_tensor(coef[:, k, :slots[k]], coef[:, k, :slots[k]], gate(k), ALU.mult).then_inc(coef_done, 1)
                        if k:
                            t, r = k - 1, rows[k - 1]
                            dve.wait_ge(mix_done, first[t] + slots[t])
                            if h:
                                dve.wait_ge(h_in[t % 2], 16 * (t // 2 + 1))
                            for q in range(2):
                                half = slice(512 * q, 512 * q + 512)
                                dve.tensor_tensor(y(t)[:r, half], y_ps[:r, q, :], y(t)[:r, half], ALU.add).then_inc(y_done, 1)
                    others("vector", dve)

                @block.scalar
                def _(act):
                    def store(t):
                        act.wait_ge(y_done, 2 * (t + 1))
                        act.dma_start(dst[t], y(t)[:rows[t], :]).then_inc(stored[t % 2], 16)

                    for k in range(nt + 1):
                        if k >= 2:
                            store(k - 2)
                        if k and h:
                            if k >= 3:
                                act.wait_ge(stored[(k - 1) % 2], 16 * ((k - 1) // 2))
                            act.dma_start(y(k - 1), h[k - 1]).then_inc(h_in[(k - 1) % 2], 16)
                        if k:
                            act.wait_ge(coef_done, k)
                        for step, su, sv in steps(k):
                            others("scalar", act, step)
                            if sv is not None:
                                n = first[k - 1] + sv
                                if n >= 8:
                                    act.wait_ge(mix_done, n - 7)
                                if spread:
                                    act.wait_ge(same_done, P // DB + 1)
                                src, w = (same, DB) if spread else (ident, P)
                                act.activation(diag[:, n % 8, :w], src[:], ACT.Copy, scale=coef[:, k - 1, sv:sv + 1]).then_inc(diag_done, 1)
                        if k < nt:
                            act.wait_ge(dot_done, first[k] + slots[k])
                            act.activation(coef[:, k, :slots[k]], dots[:, k, :slots[k]], ACT.Gelu_apprx_tanh).then_inc(gelu_done, 1)
                    store(nt - 1)
                    act.wait_ge(stored[0], 16 * ((nt + 1) // 2))
                    if nt > 1:
                        act.wait_ge(stored[1], 16 * (nt // 2))
                    others("scalar", act)

                @block.tensor
                def _(pe):
                    for k in range(nt + 1):
                        if k >= 2:
                            pe.wait_ge(y_done, 2 * (k - 1))
                        for step, su, sv in steps(k):
                            others("tensor", pe, step)
                            if sv is not None:
                                n, r = first[k - 1] + sv, rows[k - 1]
                                pe.wait_ge(diag_done, n + 1)
                                pe.wait_ge(v_in[n % nbuf], 16 * (n // nbuf + 1))
                                for q in range(2):
                                    last = pe.matmul(y_ps[:r, q, :], diag[:, n % 8, :r], v(n)[:, 512 * q:512 * q + 512],
                                                     start=(sv == 0), stop=(sv == slots[k - 1] - 1))
                                last.then_inc(mix_done, 1)
                    others("tensor", pe)

                @block.sync
                def _(sp):
                    others("sync", sp)


_INS = ["x_prompt", "x_sample", "mem_prompt", "cache_a_kv", "cache_a_kidx", "cache_cmp_kv", "cache_slc_kv", "cache_win_kv",
        "cache_mem_kv", "page_table", "ln_mix", "w_in", "g_qa", "g_ka", "g_qb", "g_kcmp", "g_kslc", "g_kwin", "g_qm", "g_km",
        "rel_table", "w_cmp1", "w_cmp2", "cmp_pe", "ln_mem", "w_mem_kv", "w_gate", "w_branch", "w_out", "ln_ffn", "w_pq",
        "sub_keys", "u_tab", "v_tab"]
_OUTS = [("y_prompt", (1, SEQ, D)), ("y_sample", (DB, 1, D)),
         ("a_kv_p", (1, SEQ, KV * 2 * DH)), ("a_kidx_p", (1, SEQ, DH)), ("cmp_kv_p", (1, SEQ, KV * 2 * DH)),
         ("slc_kv_p", (1, SEQ, KV * 2 * DH)), ("win_kv_p", (1, WIN, KV * 2 * DH)), ("mem_kv_p", (1, MEM, HM * 2 * DHM)),
         ("a_kv_s", (DB, 1, KV * 2 * DH)), ("a_kidx_s", (DB, 1, DH)), ("cmp_kv_s", (DB, 1, KV * 2 * DH)),
         ("slc_kv_s", (DB, 1, KV * 2 * DH)), ("win_kv_s", (DB, WIN, KV * 2 * DH))]
_FULL = {"a_kv": (KV, 2, DH), "a_kidx": (DH,), "cmp_kv": (KV, 2, DH), "slc_kv": (KV, 2, DH), "win_kv": (KV, 2, DH), "mem_kv": (HM, 2, DHM)}
_FLAT = {"cache_a_kv": 3, "cache_cmp_kv": 3, "cache_slc_kv": 3, "cache_win_kv": 3, "cache_mem_kv": 3}
_SCRATCH = [("bias_rev", (16, 640)), ("bias_pos", (PAST + P, 16)), ("gates", (DB, 24)), ("score", (DB, PAST)),
            ("sel_base", (16, 16)), ("self_logit", (3, DB, HQ)), ("bias_head", (16, PAST)), ("w8", (DB, IH)), ("x8", (DB, D)), ("gate8", (DB, P)), ("idx8", (DB, P)),
            ("h", (SEQ, D))]


def kernel(**inputs):
    import numpy as _np
    import concourse.bacc as _bacc
    from concourse import mybir as _mybir
    from concourse.bass_utils import run_bass_kernel_spmd as _run

    nc = _bacc.Bacc("TRN2", target_bir_lowering=False, num_devices=1)
    arrays, ins, outs, scratch = {}, {}, {}, {}
    for name in _INS:
        a = _np.ascontiguousarray(inputs[name])
        if name in _FLAT:
            a = a.reshape(a.shape[:2] + (-1,))
        arrays[f"in_{name}"] = a
        ins[name] = nc.dram_tensor(f"in_{name}", a.shape, _mybir.dt.from_np(a.dtype), kind="ExternalInput").ap()
    ins["bounds"] = nc.inline_tensor(bucket_bounds(), "bucket_bounds").ap()
    for name, shape in _OUTS:
        outs[name] = nc.dram_tensor(f"out_{name}", shape, _mybir.dt.float32, kind="ExternalOutput").ap()
    for name, shape in _SCRATCH:
        scratch[name] = nc.dram_tensor(f"tmp_{name}", shape, _mybir.dt.uint32 if name.startswith("idx") else _mybir.dt.float32).ap()
    Kernel(nc, ins, outs, scratch).build()
    r = _run(nc, [arrays], core_ids=[0])
    got = []
    for name, shape in _OUTS:
        a = r.results[0][f"out_{name}"]
        tail = _FULL.get(name[:-2])
        got.append(a.reshape(shape[:2] + tail) if tail else a)
    return tuple(got)
```
